# Optimizing a Trainium2 kernel written in Bass

```python
import math
import jax
import jax.numpy as jnp
from jax import lax
import numpy as np

D_MODEL = 1024
BATCH = 1
SEQ = 512
DEPTH = 2

N_META = 16
BLOCK = 128
META_PAD = BLOCK - N_META
ROPE_THETA = 10000.0
LN_EPS = 1e-5
NEG = -1e30

DA_HEADS = 4
DA_DIM = 64
WB_HEADS = 8
WB_KV = 2
WB_DIM = 64
WINDOW = 128
MC_HEADS = 4
MC_QK = 128
MC_V = 128
CONV_W = 3
N_BRANCH = 3
BRANCH_W = 512
N_GROUPS = 4
EXP_PER_GROUP = 8
N_EXPERTS = N_GROUPS * EXP_PER_GROUP
TOP_K = 2
D_EXPERT = 512

A_Q = DA_HEADS * 2 * DA_DIM
A_K = DA_HEADS * 2 * DA_DIM
A_V = DA_HEADS * 2 * DA_DIM
B_Q = WB_HEADS * WB_DIM
B_K = WB_KV * WB_DIM
B_V = WB_KV * WB_DIM
C_Q = MC_HEADS * MC_QK
C_K = MC_HEADS * MC_QK
C_V = MC_HEADS * MC_V
C_O = MC_HEADS * MC_V
C_G = 4 * MC_HEADS
GATE_W = N_BRANCH * D_MODEL
SPLITS = (A_Q, A_K, A_V, B_Q, B_K, B_V, C_Q, C_K, C_V, C_O, C_G, GATE_W)
D_IN = sum(SPLITS)

kernel_name = "hybrid_diffattn_swa_mlstm_hmoe_encoder"

F32 = jnp.float32

def layer_norm(x, g, b):
    x32 = x.astype(F32)
    mu = x32.mean(-1, keepdims=True)
    var = jnp.square(x32 - mu).mean(-1, keepdims=True)
    return ((x32 - mu) * lax.rsqrt(var + LN_EPS) * g.astype(F32) + b.astype(F32)).astype(x.dtype)

def rope_tables(length, dim):
    pos = jnp.arange(length, dtype=F32)
    inv = 1.0 / (ROPE_THETA ** (jnp.arange(0, dim, 2, dtype=F32) / dim))
    ang = pos[:, None] * inv[None, :]
    return jnp.cos(ang), jnp.sin(ang)

def apply_rope(x, cos, sin):
    shape = (cos.shape[0],) + (1,) * (x.ndim - 3) + (cos.shape[1],)
    c = cos.reshape(shape).astype(x.dtype)
    s = sin.reshape(shape).astype(x.dtype)
    x1, x2 = jnp.split(x, 2, axis=-1)
    return jnp.concatenate([x1 * c - x2 * s, x2 * c + x1 * s], axis=-1)

def pad_front(x, n, value=0.0):
    return jnp.pad(x, [(0, 0), (n, 0)] + [(0, 0)] * (x.ndim - 2), constant_values=value)

def diff_attention(q, k, v, lam, lam_init, norm_g):
    bsz, length = q.shape[:2]
    qp = pad_front(q, META_PAD)
    nb = qp.shape[1] // BLOCK
    qb = qp.reshape(bsz, nb, BLOCK, DA_HEADS, 2, DA_DIM).transpose(1, 0, 2, 3, 4, 5)
    scale = DA_DIM ** -0.5

    def one_block(qblk):
        s = jnp.einsum('bqhcd,bkhcd->bhcqk', qblk, k).astype(F32) * scale
        p = jax.nn.softmax(s, axis=-1)
        a = p[:, :, 0] - lam * p[:, :, 1]
        return jnp.einsum('bhqk,bkhe->bqhe', a.astype(v.dtype), v)

    o = lax.map(one_block, qb)
    o = o.transpose(1, 0, 2, 3, 4).reshape(bsz, nb * BLOCK, DA_HEADS, 2 * DA_DIM)[:, META_PAD:]
    o32 = o.astype(F32)
    o32 = o32 * lax.rsqrt(jnp.mean(jnp.square(o32), -1, keepdims=True) + LN_EPS) * norm_g.astype(F32) * (1.0 - lam_init)
    return o32.astype(v.dtype).reshape(bsz, length, A_V)

def windowed_gqa(q, k, v, sink):
    bsz, length = q.shape[:2]
    lp = length + META_PAD
    nb = lp // BLOCK
    grp = WB_HEADS // WB_KV
    qb = pad_front(q, META_PAD).reshape(bsz, nb, BLOCK, WB_KV, grp, WB_DIM)
    k_meta, v_meta = k[:, :N_META], v[:, :N_META]

    def band(t):
        tp = jnp.pad(t, [(0, 0), (META_PAD + BLOCK, BLOCK), (0, 0), (0, 0)])
        tp = tp.reshape(bsz, nb + 2, BLOCK, WB_KV, WB_DIM)
        return jnp.concatenate([tp[:, :-2], tp[:, 1:-1], tp[:, 2:]], axis=2)

    kb, vb = band(k), band(v)
    scale = WB_DIM ** -0.5
    s_band = jnp.einsum('bnqkgd,bnskd->bnkgqs', qb, kb).astype(F32) * scale
    s_meta = jnp.einsum('bnqkgd,bmkd->bnkgqm', qb, k_meta).astype(F32) * scale
    qidx = jnp.arange(nb)[:, None] * BLOCK + jnp.arange(BLOCK)[None, :]
    kidx = (jnp.arange(nb)[:, None] - 1) * BLOCK + jnp.arange(3 * BLOCK)[None, :]
    valid = ((kidx[:, None, :] >= BLOCK) & (kidx[:, None, :] < lp)
             & (jnp.abs(qidx[:, :, None] - kidx[:, None, :]) <= WINDOW))
    s_band = jnp.where(valid[None, :, None, None], s_band, NEG)
    s_sink = jnp.broadcast_to(sink.astype(F32).reshape(1, 1, WB_KV, grp, 1, 1), s_meta.shape[:-1] + (1,))
    p = jax.nn.softmax(jnp.concatenate([s_band, s_meta, s_sink], axis=-1), axis=-1)
    p_band = p[..., :3 * BLOCK].astype(v.dtype)
    p_meta = p[..., 3 * BLOCK:3 * BLOCK + N_META].astype(v.dtype)
    o = (jnp.einsum('bnkgqs,bnskd->bnqkgd', p_band, vb)
         + jnp.einsum('bnkgqm,bmkd->bnqkgd', p_meta, v_meta))
    return o.reshape(bsz, lp, B_Q)[:, META_PAD:]

def mlstm_direction(q, k, v, li, lf):
    bsz, lp, heads, dk = q.shape
    dv = v.shape[-1]
    nch = lp // BLOCK

    def chunks(t):
        return jnp.moveaxis(t.reshape((bsz, nch, BLOCK, heads) + t.shape[3:]), 3, 1)

    qc, kc, vc, lic, lfc = chunks(q), chunks(k), chunks(v), chunks(li), chunks(lf)
    b = jnp.cumsum(lfc, axis=-1)
    g = b[..., -1]
    a = g[..., None] - b + lic
    tril = jnp.tril(jnp.ones((BLOCK, BLOCK), dtype=bool))
    dmat = jnp.where(tril, b[..., :, None] - b[..., None, :] + lic[..., None, :], NEG)

    def step(carry, inp):
        c_st, n_st, m_st = carry
        k_i, v_i, a_i, g_i = inp
        m_new = jnp.maximum(g_i + m_st, a_i.max(-1))
        decay = jnp.exp(g_i + m_st - m_new)
        w = jnp.exp(a_i - m_new[..., None])
        c_new = decay[..., None, None] * c_st + jnp.einsum('bhc,bhcd,bhce->bhde', w, k_i, v_i)
        n_new = decay[..., None] * n_st + jnp.einsum('bhc,bhcd->bhd', w, k_i)
        return (c_new, n_new, m_new), (c_st, n_st, m_st)

    init = (jnp.zeros((bsz, heads, dk, dv), F32), jnp.zeros((bsz, heads, dk), F32), jnp.zeros((bsz, heads), F32))
    xs = (jnp.moveaxis(kc, 2, 0), jnp.moveaxis(vc, 2, 0), jnp.moveaxis(a, 2, 0), jnp.moveaxis(g, 2, 0))
    _, (c_prev, n_prev, m_prev) = lax.scan(step, init, xs)
    c_prev = jnp.moveaxis(c_prev, 0, 2)
    n_prev = jnp.moveaxis(n_prev, 0, 2)
    m_prev = jnp.moveaxis(m_prev, 0, 2)
    inter_log = b + m_prev[..., None]
    m_t = jnp.maximum(inter_log, dmat.max(-1))
    inter = jnp.exp(inter_log - m_t)
    s = jnp.einsum('bhncd,bhnsd->bhncs', qc, kc) * jnp.exp(dmat - m_t[..., None])
    num = inter[..., None] * jnp.einsum('bhncd,bhnde->bhnce', qc, c_prev) + jnp.einsum('bhncs,bhnse->bhnce', s, vc)
    den = inter * jnp.einsum('bhncd,bhnd->bhnc', qc, n_prev) + s.sum(-1)
    h = num / jnp.maximum(jnp.abs(den), jnp.exp(-m_t))[..., None]
    return jnp.moveaxis(h, 1, 3).reshape(bsz, lp, heads, dv)

def mlstm_mixer(cq, ck, cv, co, cg, conv_w, conv_b, gate_b, norm_g):
    bsz, length, _ = cq.shape
    qk = jnp.concatenate([cq, ck], axis=-1)
    qk = lax.conv_general_dilated(qk, conv_w[:, None, :].astype(qk.dtype), (1,), [(CONV_W // 2, CONV_W // 2)],
                                  dimension_numbers=('NWC', 'WIO', 'NWC'), feature_group_count=C_Q + C_K)
    qk = jax.nn.silu(qk + conv_b.astype(qk.dtype)).astype(F32)
    q = qk[..., :C_Q].reshape(bsz, length, MC_HEADS, MC_QK)
    k = qk[..., C_Q:].reshape(bsz, length, MC_HEADS, MC_QK) * (MC_QK ** -0.5)
    v = cv.astype(F32).reshape(bsz, length, MC_HEADS, MC_V)
    gates = (cg.astype(F32) + gate_b.astype(F32)).reshape(bsz, length, 4, MC_HEADS)
    li_f = gates[:, :, 0]
    lf_f = jax.nn.log_sigmoid(gates[:, :, 1])
    li_b = gates[:, :, 2]
    lf_b = jax.nn.log_sigmoid(gates[:, :, 3])
    qp, kp, vp = pad_front(q, META_PAD), pad_front(k, META_PAD), pad_front(v, META_PAD)
    h_f = mlstm_direction(qp, kp, vp, pad_front(li_f, META_PAD, NEG), pad_front(lf_f, META_PAD))

    def flip(t):
        return jnp.flip(t, axis=1)

    h_b = flip(mlstm_direction(flip(qp), flip(kp), flip(vp),
                               flip(pad_front(li_b, META_PAD, NEG)), flip(pad_front(lf_b, META_PAD))))
    h = h_f[:, META_PAD:] + h_b[:, META_PAD:]
    mu = h.mean(-1, keepdims=True)
    var = jnp.square(h - mu).mean(-1, keepdims=True)
    hn = (h - mu) * lax.rsqrt(var + LN_EPS) * norm_g.astype(F32).reshape(MC_HEADS, MC_V)
    return (hn.reshape(bsz, length, C_V) * jax.nn.sigmoid(co.astype(F32))).astype(cq.dtype)

def token_mixer(h, cos, sin, lam_init, w_in, conv_w, conv_b, gate_b, lam_q1, lam_k1, lam_q2, lam_k2,
                diff_g, sink, mlstm_g, w_branch, w_out):
    bsz, length, _ = h.shape
    z = h @ w_in
    cuts = np.cumsum(SPLITS)[:-1].tolist()
    aq, ak, av, bq, bk, bv, cq, ck, cv, co, cg, gz = jnp.split(z, cuts, axis=-1)
    qa = apply_rope(aq.reshape(bsz, length, DA_HEADS, 2, DA_DIM), cos, sin)
    ka = apply_rope(ak.reshape(bsz, length, DA_HEADS, 2, DA_DIM), cos, sin)
    va = av.reshape(bsz, length, DA_HEADS, 2 * DA_DIM)
    lam = (jnp.exp(jnp.sum(lam_q1.astype(F32) * lam_k1.astype(F32)))
           - jnp.exp(jnp.sum(lam_q2.astype(F32) * lam_k2.astype(F32))) + lam_init)
    out_a = diff_attention(qa, ka, va, lam, lam_init, diff_g)
    qb = apply_rope(bq.reshape(bsz, length, WB_HEADS, WB_DIM), cos, sin)
    kb = apply_rope(bk.reshape(bsz, length, WB_KV, WB_DIM), cos, sin)
    vb = bv.reshape(bsz, length, WB_KV, WB_DIM)
    out_b = windowed_gqa(qb, kb, vb, sink)
    out_c = mlstm_mixer(cq, ck, cv, co, cg, conv_w, conv_b, gate_b, mlstm_g)
    gates = jax.nn.sigmoid(gz.reshape(bsz, length, N_BRANCH, D_MODEL))
    merged = (gates[:, :, 0] * (out_a @ w_branch[0])
              + gates[:, :, 1] * (out_b @ w_branch[1])
              + gates[:, :, 2] * (out_c @ w_branch[2]))
    return merged @ w_out

def hier_moe(h, w_rg, b_rg, w_re, b_re, w_gate, w_up, w_down):
    bsz, length, dm = h.shape
    n_tok = bsz * length
    xf = h.reshape(n_tok, dm)
    g_logits = (xf @ w_rg).astype(F32) + b_rg.astype(F32)
    g_prob = jax.nn.softmax(g_logits, axis=-1)
    g_sel = jnp.argmax(g_logits, axis=-1)
    p_grp = jnp.max(g_prob, axis=-1)
    e_logits = ((xf @ w_re).astype(F32) + b_re.astype(F32)).reshape(n_tok, N_GROUPS, EXP_PER_GROUP)
    e_logits = e_logits[jnp.arange(n_tok), g_sel]
    top_v, top_i = lax.top_k(e_logits, TOP_K)
    w_tok = jax.nn.softmax(top_v, axis=-1) * p_grp[:, None]
    expert = g_sel[:, None].astype(jnp.int32) * EXP_PER_GROUP + top_i.astype(jnp.int32)
    n_assign = n_tok * TOP_K
    n_blocks = -(-(n_assign + N_EXPERTS * (BLOCK - 1)) // BLOCK)
    e_flat = expert.reshape(-1)
    t_flat = jnp.repeat(jnp.arange(n_tok, dtype=jnp.int32), TOP_K)
    w_flat = w_tok.reshape(-1)
    order = jnp.argsort(e_flat)
    e_s, t_s, w_s = e_flat[order], t_flat[order], w_flat[order]
    counts = jnp.bincount(e_flat, length=N_EXPERTS)
    start = jnp.cumsum(counts) - counts
    pcounts = (counts + BLOCK - 1) // BLOCK * BLOCK
    pend = jnp.cumsum(pcounts)
    pstart = pend - pcounts
    dest = pstart[e_s] + jnp.arange(n_assign, dtype=jnp.int32) - start[e_s]
    slot_tok = jnp.zeros((n_blocks * BLOCK,), jnp.int32).at[dest].set(t_s)
    slot_w = jnp.zeros((n_blocks * BLOCK,), F32).at[dest].set(w_s)
    block_e = jnp.minimum(jnp.searchsorted(pend, jnp.arange(n_blocks) * BLOCK, side='right'), N_EXPERTS - 1)
    xs = xf[slot_tok].reshape(n_blocks, BLOCK, dm)

    def run_expert(args):
        xb, e = args
        return (jax.nn.silu(xb @ w_gate[e]) * (xb @ w_up[e])) @ w_down[e]

    ys = lax.map(run_expert, (xs, block_e)).reshape(n_blocks * BLOCK, dm)
    y = jnp.zeros_like(xf).at[slot_tok].add(ys * slot_w[:, None].astype(ys.dtype))
    return y.reshape(bsz, length, dm)

def setup_inputs(seed: int = 0) -> dict:
    key = jax.random.key(seed)
    ks = jax.random.split(key, 32)
    beta = (8.0 * DEPTH) ** -0.25

    def nrm(k, shape, scale):
        return jax.random.normal(k, shape, F32) * scale

    offs = np.cumsum((0,) + SPLITS)
    col_scale = np.ones((D_IN,), np.float32)
    for i in (2, 5, 8):
        col_scale[offs[i]:offs[i + 1]] = beta
    f_bias = jnp.linspace(3.0, 6.0, MC_HEADS, dtype=F32)
    zeros_h = jnp.zeros((MC_HEADS,), F32)
    gate_base = jnp.stack([zeros_h, f_bias, zeros_h, f_bias])
    return {
        "x": nrm(ks[0], (BATCH, SEQ, D_MODEL), 1.0),
        "meta": nrm(ks[1], (N_META, D_MODEL), 1.0),
        "ln_in_g": 1.0 + nrm(ks[2], (D_MODEL,), 0.02),
        "ln_in_b": nrm(ks[3], (D_MODEL,), 0.02),
        "w_in": nrm(ks[4], (DEPTH, D_MODEL, D_IN), D_MODEL ** -0.5) * jnp.asarray(col_scale),
        "conv_w": nrm(ks[5], (DEPTH, CONV_W, C_Q + C_K), CONV_W ** -0.5),
        "conv_b": nrm(ks[6], (DEPTH, C_Q + C_K), 0.02),
        "gate_b": (gate_base[None] + nrm(ks[7], (DEPTH, 4, MC_HEADS), 0.1)).reshape(DEPTH, C_G),
        "lam_q1": nrm(ks[8], (DEPTH, DA_DIM), 0.1),
        "lam_k1": nrm(ks[9], (DEPTH, DA_DIM), 0.1),
        "lam_q2": nrm(ks[10], (DEPTH, DA_DIM), 0.1),
        "lam_k2": nrm(ks[11], (DEPTH, DA_DIM), 0.1),
        "diff_g": 1.0 + nrm(ks[12], (DEPTH, 2 * DA_DIM), 0.02),
        "sink": nrm(ks[13], (DEPTH, WB_HEADS), 0.5),
        "mlstm_g": 1.0 + nrm(ks[14], (DEPTH, C_V), 0.02),
        "w_branch": nrm(ks[15], (DEPTH, N_BRANCH, BRANCH_W, D_MODEL), BRANCH_W ** -0.5),
        "w_out": nrm(ks[16], (DEPTH, D_MODEL, D_MODEL), D_MODEL ** -0.5 * beta),
        "ln1_g": 1.0 + nrm(ks[17], (DEPTH, D_MODEL), 0.02),
        "ln1_b": nrm(ks[18], (DEPTH, D_MODEL), 0.02),
        "ln2_g": 1.0 + nrm(ks[19], (DEPTH, D_MODEL), 0.02),
        "ln2_b": nrm(ks[20], (DEPTH, D_MODEL), 0.02),
        "w_rg": nrm(ks[21], (DEPTH, D_MODEL, N_GROUPS), D_MODEL ** -0.5),
        "b_rg": nrm(ks[22], (DEPTH, N_GROUPS), 0.01),
        "w_re": nrm(ks[23], (DEPTH, D_MODEL, N_EXPERTS), D_MODEL ** -0.5),
        "b_re": nrm(ks[24], (DEPTH, N_EXPERTS), 0.01),
        "w_gate": nrm(ks[25], (DEPTH, N_EXPERTS, D_MODEL, D_EXPERT), D_MODEL ** -0.5 * beta),
        "w_up": nrm(ks[26], (DEPTH, N_EXPERTS, D_MODEL, D_EXPERT), D_MODEL ** -0.5 * beta),
        "w_down": nrm(ks[27], (DEPTH, N_EXPERTS, D_EXPERT, D_MODEL), D_EXPERT ** -0.5 * beta),
    }

def reference(x, meta, ln_in_g, ln_in_b, w_in, conv_w, conv_b, gate_b, lam_q1, lam_k1, lam_q2, lam_k2,
              diff_g, sink, mlstm_g, w_branch, w_out, ln1_g, ln1_b, ln2_g, ln2_b,
              w_rg, b_rg, w_re, b_re, w_gate, w_up, w_down):
    bsz = x.shape[0]
    alpha = (2.0 * DEPTH) ** 0.25
    h = jnp.concatenate([jnp.broadcast_to(meta.astype(x.dtype)[None], (bsz, N_META, D_MODEL)), x], axis=1)
    h = layer_norm(h, ln_in_g, ln_in_b)
    cos, sin = rope_tables(h.shape[1], DA_DIM)
    for l in range(DEPTH):
        lam_init = 0.8 - 0.6 * math.exp(-0.3 * l)
        y = token_mixer(h, cos, sin, lam_init, w_in[l], conv_w[l], conv_b[l], gate_b[l],
                        lam_q1[l], lam_k1[l], lam_q2[l], lam_k2[l], diff_g[l], sink[l], mlstm_g[l],
                        w_branch[l], w_out[l])
        h = layer_norm(alpha * h + y, ln1_g[l], ln1_b[l])
        y = hier_moe(h, w_rg[l], b_rg[l], w_re[l], b_re[l], w_gate[l], w_up[l], w_down[l])
        h = layer_norm(alpha * h + y, ln2_g[l], ln2_b[l])
    return h[:, N_META:]


_drawn_inputs = setup_inputs


def setup_inputs(seed=0):
    import zlib

    import numpy as np

    out = dict(_drawn_inputs(seed))
    spreads = {}
    factors = {'conv_b': 8.0,
     'lam_q1': 7.903,
     'lam_k1': 4.315,
     'lam_q2': 5.489,
     'lam_k2': 7.218,
     'diff_g': 36.271,
     'sink': 200.0,
     'mlstm_g': 29.003,
     'b_rg': 187.921,
     'b_re': 190.572}
    for name, (base, spread) in spreads.items():
        noise = np.random.default_rng([zlib.crc32(name.encode()), seed]).standard_normal(out[name].shape)
        drawn = base * np.exp(spread * noise) if base else spread * noise
        out[name] = jnp.asarray(drawn.astype(out[name].dtype))
    for name, factor in factors.items():
        out[name] = (out[name] * factor).astype(out[name].dtype)
    return out
```

```python
from contextlib import ExitStack

import numpy as np

import concourse.bass as bass
from concourse import mybir

F32 = mybir.dt.float32
I32 = mybir.dt.int32
U32 = mybir.dt.uint32
ALU = mybir.AluOpType
ACT = mybir.ActivationFunctionType
AX = mybir.AxisListType

P = 128
DM = 1024
KD = DM // P
META = 16
SEQ = 512
L = META + SEQ
HALF = L // 2
NT = 5
TOK = [(0, META)] + [(META + P * i, P) for i in range(4)]
DEPTH = 2
ALPHA = (2.0 * DEPTH) ** 0.25
EPS = 1e-5
NEG = -1e30
LOW = -3e38

DIN = 7440
COL = {"aq": 0, "ak": 512, "av": 1024, "bq": 1536, "bkv": 2048, "cq": 2304, "ck": 2816, "cv": 3328,
       "co": 3840, "cg": 4352, "gz": 4368}
QSCALE = 64 ** -0.5
MSCALE = 128 ** -0.5
NE = 32
MAXB = 40
DE = 512

CONST = {}
_at = 0
for _n, _w in (("cos", L), ("sin", L), ("ident", P), ("rot", P), ("mask0", 144), ("mask1", 272),
               ("mask2", 400), ("ltri", P), ("ones", P), ("valid", NT), ("wg4", 4), ("we32", NE),
               ("thr", NT), ("jj", MAXB), ("zero", NE)):
    CONST[_n] = (_at, _w)
    _at += _w
NCONST = _at

ROW = {"gate_b": (0, 16), "b_r": (16, 36), "sink": (52, 8), "lam": (60, 256), "neg_lam_init": (316, 1),
       "one_minus": (317, 1)}
NROW = 318
NCOLP = 24 + 8 + 4 + 1

RING = 0
SLOT = 4096
X = 3 * SLOT
Y = X + 6912
Z = Y + 3 * 4 * L
W = Z + 5392
ARENA = W + 5952


def program(nc, a):
    ctx = ExitStack()
    with ctx:
        def sb(name, shape, dt=F32):
            return ctx.enter_context(nc.sbuf_tensor(name, shape, dt))

        def sem(name):
            return ctx.enter_context(nc.semaphore(name))

        layer_sems = []

        def lsem(name):
            s = sem(name)
            layer_sems.append(s)
            return s

        xs = nc.dram_tensor("moe_rows", [(MAXB + 1) * P, DM], F32, kind="Internal").ap()
        mrow = nc.dram_tensor("mlstm_max_rows", [2, 8, L], F32, kind="Internal").ap()

        arena = sb("arena", [P, ARENA])
        h_tok = sb("h_tok", [P, NT, DM])
        hT = sb("hT", [P, KD, L])
        cst = sb("cst", [P, NCONST])
        lngb = sb("lngb", [P, 2, DM])
        rowp = sb("rowp", [P, NROW])
        colp = sb("colp", [P, NCOLP])
        w_r = sb("w_r", [P, KD, 36])
        bn = sb("bn", [P, NT, 12])
        mv = sb("mv", [P, NT, 2])
        rstd = sb("rstd", [P, NT])
        st = sb("st", [P, 64])
        rs = sb("rs", [P, 2, NT, 8])
        ss = sb("ss", [P, NT, 4, 2])
        ssr = sb("ssr", [P, NT, 4])
        cg = sb("cg", [P, 2, NT, 16])
        gcol = sb("gcol", [P, NT, 32])
        lg = sb("lg", [P, NT, 36])
        r5 = sb("r5", [P, 12, NT])
        r4 = sb("r4", [P, 3, NT, 4])
        e32 = sb("e32", [P, 4, NT, NE])
        zeros = e32[:, :, :, :].rearrange("p a b c -> p (a b c)")[:, 0:512]
        n32 = sb("n32", [P, 4, NE])
        dst = sb("dst", [P, NT, 2], U32)
        tab = sb("tab", [1, MAXB + 8], I32)

        ps = ctx.enter_context(nc.psum_tensor("ps", [P, 8, 512], F32))

        def C(name, rows=P, w=None):
            at, width = CONST[name]
            return cst[0:rows, at:at + (width if w is None else w)]

        def R(name):
            at, width = ROW[name]
            return rowp[:, at:at + width]

        def v(at, *dims):
            n = int(np.prod(dims))
            f = arena[:, at:at + n]
            if len(dims) == 2:
                return f.rearrange("p (a b) -> p a b", b=dims[1])
            if len(dims) == 3:
                return f.rearrange("p (a b c) -> p a b c", b=dims[1], c=dims[2])
            return f

        ident = C("ident")
        slot = [v(RING + SLOT * i, KD, 512) for i in range(3)]
        qA, kA, vA = v(X, 4, L), v(X + 4 * L, 4, L), v(X + 8 * L, NT, 512)
        qC, kC, vC = qA, kA, v(X + 8 * L, NT, 4, 129)
        merged = v(X, KD, L)
        outT = v(Y, 3, 4, L)
        mb = v(Y + 8 * L, 2, 2, L)
        qB, kB, vB = v(Z, 4, L), v(Z + 4 * L, L), v(Z + 5 * L, NT, 128)
        sco = v(Z + 3280, 4, L)
        raw = v(W, 4, HALF)
        t_sin = v(W + 4 * HALF, 2, HALF)
        pA = v(W, 2, 2, L)
        ptA = v(W + 4 * L, 2, 4, P)
        ptm = v(W + 4 * L + 1024, 2, P)
        oA = v(W + 4 * L + 1024 + 256, NT, 512)
        sB = v(W, 3, 400)
        oB = v(X, NT, 512)
        sq = v(W, 2, 512)
        craw = v(W, 2, L + 2)
        ctmp = v(W + 2 * (L + 2), 2, L)
        SAT = [[0], [0]]
        for j in range(NT):
            SAT[0].append(SAT[0][-1] + L - TOK[j][0])
        SAT[1][0] = SAT[0][-1]
        for j in range(NT):
            SAT[1].append(SAT[1][-1] + sum(TOK[j]))
        NS = SAT[1][-1]
        sC = [v(W, NS), v(Z, NS)]
        hsum = v(W + NS, NT, 512)
        ROWS = [v(Z + L * i, L) for i in range(6)] + [v(W + 3172 + L * i, L) for i in range(5)]
        LF, LI, ZR, BF, BB, UF, UB, MF, MB, EF, EB = [r[0:8, :] for r in ROWS]
        gzw = [v(RING + 6144 * p, KD, 512) for p in range(2)]
        wbw = [v(RING + 6144 * p + 4096, 4, 512) for p in range(2)]
        sg = v(W, 2, L)
        tg = v(W + 2 * L, 2, L)
        wout = [v(RING + SLOT * i, KD, 512) for i in range(2)]
        WSET = 3 * SLOT
        mo = 2 * WSET
        assert mo + 6656 <= ARENA and NS <= 3280
        xe = v(mo, DM)
        xeT = v(mo + 1024, KD, P)
        sil = v(mo + 2048, DE)
        hid = v(mo + 2560, DE)
        hidT = v(mo + 3072, 4, P)
        ye = v(mo + 3584, DM)
        gath = v(0, NT, 2, DM)
        tabf = arena[:, mo + MAXB * NE:mo + MAXB * NE + 64]

        const_in = sem("const_in")
        x_in = sem("x_in")
        xs_zeroed = sem("xs_zeroed")
        ln0_in = sem("ln0_in")
        out_done = sem("out_done")
        scattered = sem("scattered")
        gathered = [sem(f"gathered{i}") for i in range(NT)]
        arrived = sem("arrived")
        go = {e: sem(f"go_{e}") for e in ("pe", "act", "dve", "pool")}

        zero_ready = lsem("zero_ready")
        phase_done = lsem("phase_done")
        dve_step = lsem("dve_step")
        act_step = lsem("act_step")
        slot_in = [lsem(f"slot_in{i}") for i in range(3)]
        slot_used = lsem("slot_used")
        par_in = lsem("par_in")
        ln2_in = lsem("ln2_in")
        unit_mm = lsem("unit_mm")
        unit_ev = lsem("unit_ev")
        rot_mm = lsem("rot_mm")
        rot_ev = lsem("rot_ev")
        conv_done = lsem("conv_done")
        silu_done = lsem("silu_done")
        a_s, a_m, a_exp, a_comb, a_t, a_tev, a_tmev, a_o, a_oev = [lsem(f"a_{n}") for n in
            ("s", "m", "exp", "comb", "t", "tev", "tmev", "o", "oev")]
        b_s, b_m, b_exp, b_t, b_tev, b_tmev, b_o, b_snk, b_oev = [lsem(f"b_{n}") for n in
            ("s", "m", "exp", "t", "tev", "tmev", "o", "snk", "oev")]
        g_lf, g_exp, g_ln, g_t, g_rows, g_e, g_t2, g_col = [lsem(f"g_{n}") for n in
            ("lf", "exp", "ln", "t", "rows", "e", "t2", "col")]
        m_out = lsem("m_out")
        m_in = [lsem(f"m_in{i}") for i in range(2)]
        c_qk, c_w, c_mul, c_sel, c_pv, c_post, c_mbused = [lsem(f"c_{n}") for n in
            ("qk", "w", "mul", "sel", "pv", "post", "mbused")]
        n_ready, n_sqrt, n_norm, n_t, n_ev = [lsem(f"n_{n}") for n in ("ready", "sqrt", "norm", "t", "ev")]
        pair_in = [lsem(f"pair_in{i}") for i in range(2)]
        pair_used, gate_mm, gate_sig, gate_tmp, gate_free = [lsem(f"gate_{n}") for n in
            ("pair_used", "mm", "sig", "tmp", "free")]
        wout_in = [lsem(f"wout_in{i}") for i in range(2)]
        y_mm, y_ev = lsem("y_mm"), lsem("y_ev")
        r_mm, r_lg, r_exp, r_exp2, r_cnt, r_rank, r_tab, r_a, r_b = [lsem(f"r_{n}") for n in
            ("mm", "lg", "exp", "exp2", "cnt", "rank", "tab", "a", "b")]
        rows_back = lsem("rows_back")
        wg_in, wu_in, wd_in, xe_in, ys_out = [lsem(f"moe_{n}") for n in ("wg_in", "wu_in", "wd_in", "xe_in", "ys_out")]
        e_xt, e_xtev, e_g, e_u, e_sil, e_hid, e_ht, e_htev, e_dn, e_ye = [lsem(f"e_{n}") for n in
            ("xt", "xtev", "g", "u", "sil", "hid", "ht", "htev", "dn", "ye")]
        FREE = {"pe": [(e_g, 1), (e_u, 1), (e_dn, 1)], "act": [(e_sil, 1)], "dve": [(e_hid, 1), (e_ye, 2)],
                "sp": [(ys_out, 16)]}

        def start_free(eng, who):
            for s, n in FREE[who]:
                eng.sem_inc(s, n)

        l_var, l_sqrt, l_mul, l_add, l_t, l_ev = [lsem(f"l_{n}") for n in ("var", "sqrt", "mul", "add", "t", "ev")]

        UNITS = []
        for kind, n in (("aq", 4), ("ak", 4)):
            UNITS += [(kind, c, h) for c in range(n) for h in range(2)]
        UNITS += [("av", i, 0) for i in range(NT)]
        UNITS += [("bq", c, h) for c in range(4) for h in range(2)]
        UNITS += [("bk", 0, h) for h in range(2)]
        UNITS += [("bv", i, 0) for i in range(NT)]
        NAB = len(UNITS)
        UNITS += [("cg", i, 0) for i in range(NT)]
        for kind in ("cq", "ck"):
            UNITS += [(kind, c, h) for c in range(4) for h in range(2)]
        UNITS += [("cv", i, 0) for i in range(NT)]
        UNITS += [("co", c, h) for c in range(4) for h in range(2)]
        WBLOCK = {"aq": 0, "ak": 1, "av": 2, "bq": 3, "bk": 4, "bv": 4, "cg": 4, "cq": 5, "ck": 6, "cv": 7, "co": 8}
        NROT = sum(k in ("aq", "ak", "bq", "bk") for k, _, _ in UNITS)
        ROPE = {"aq": lambda c: qA[:, c, :], "ak": lambda c: kA[:, c, :],
                "bq": lambda c: qB[:, c, :], "bk": lambda c: kB[:, :]}

        def halves(bank, rows=P):
            return ps[0:rows, bank:bank + 2, 0:HALF]

        def two(apx):
            return apx.rearrange("p (a b) -> p a b", b=HALF)

        class Phase:

            def __init__(self, eng):
                self.eng, self.n = eng, 0

            def __call__(self):
                self.n += 1
                self.eng.drain().then_inc(phase_done, 1)
                self.eng.wait_ge(phase_done, 3 * self.n)

        def end_layer(eng, who):
            eng.drain().then_inc(arrived, 1)
            eng.wait_ge(go[who], 1)
            eng.sem_clear(go[who])

        def next_layer(sp):
            sp.wait_ge(arrived, 4)
            for s in layer_sems:
                sp.sem_clear(s)
            sp.sem_clear(arrived)
            for g in go.values():
                sp.sem_inc(g, 1)

        BKEYS = [[(0, 16), (16, 128)], [(0, 272)], [(0, 400)], [(0, 16), (144, 384)], [(0, 16), (272, 256)]]
        BTILES = [[1], [1, 2], [1, 2, 3], [2, 3, 4], [3, 4]]
        BHEAD = [0, 4, 1, 5, 2, 6, 3, 7]
        BMASK = ["mask0", "mask1", "mask2", "mask2", "mask2"]
        bwidth = [sum(n for _, n in k) for k in BKEYS]

        block = ctx.enter_context(nc.Block())

        @block.sync
        def _(sp):
            sp.dma_start(cst[:, :], a["consts"]).then_inc(const_in, 16)
            sp.dma_start(h_tok[0:META, 0, :], a["meta"]).then_inc(x_in, 16)
            sp.dma_start(h_tok[:, 1:NT, :], a["x"][0].rearrange("(i p) n -> p i n", p=P)).then_inc(x_in, 16)
            sp.dma_start(lngb[:, 0, :], a["ln_in_g"].partition_broadcast(P)).then_inc(ln0_in, 16)
            sp.dma_start(lngb[:, 1, :], a["ln_in_b"].partition_broadcast(P)).then_inc(ln0_in, 16)
            next_layer(sp)
            with sp.Fori(0, DEPTH) as l:
                def lay(t, pat, **kw):
                    return t[bass.ds(l, 1)].rearrange("o " + pat, **kw)

                sp.dma_start(rowp[:, :], a["rowp"][bass.ds(l, 1), :].broadcast_to([P, NROW])).then_inc(par_in, 16)
                sp.dma_start(colp[:, :], lay(a["colp"], "p n -> (o p) n")).then_inc(par_in, 16)
                sp.dma_start(w_r[:, :, :], lay(a["w_r"], "(k p) n -> (o p) k n", p=P)).then_inc(par_in, 16)
                for i, n in enumerate(("ln1_g", "ln1_b")):
                    sp.dma_start(lngb[:, i, :], a[n][bass.ds(l, 1), :].broadcast_to([P, DM])).then_inc(par_in, 16)

                def w_cols(at, n):
                    return lay(a["w_in"], "(k p) n -> (o p) k n", p=P)[:, :, at:at + n]

                for n, kind in enumerate(("aq", "ak", "av", "bq", "bkv", "cq", "ck", "cv", "co")):
                    if n >= 3:
                        sp.wait_ge(slot_used, n - 2)
                    if kind == "bq":
                        for g in range(2):
                            for k in range(KD):
                                sp.dma_start(
                                    slot[n % 3][:, k, :].rearrange("p (c g d) -> p c g d", g=2, d=64)[:, :, g, :],
                                    w_cols(COL["bq"] + 256 * g, 256)[:, k, :].rearrange("p (c d) -> p c d", d=64),
                                ).then_inc(slot_in[n % 3], 16)
                    elif kind == "bkv":
                        sp.dma_start(slot[n % 3][:, :, 0:256], w_cols(COL["bkv"], 256)).then_inc(slot_in[n % 3], 16)
                        sp.dma_start(slot[n % 3][:, :, 256:272], w_cols(COL["cg"], 16)).then_inc(slot_in[n % 3], 16)
                    else:
                        sp.dma_start(slot[n % 3][:, :, :], w_cols(COL[kind], 512)).then_inc(slot_in[n % 3], 16)

                with sp.If(l < 1):
                    sp.wait_ge(zero_ready, 1)
                    for hf in range(2):
                        sp.dma_start(xs.rearrange("(b p) n -> p b n", p=P)[:, :, 512 * hf:512 * hf + 512],
                                     zeros.unsqueeze(1).broadcast_to([P, MAXB + 1, 512])).then_inc(xs_zeroed, 16)

                sp.wait_ge(g_rows, 1)
                sp.dma_start(mrow[0], MF).then_inc(m_out, 16)
                sp.dma_start(mrow[1], MB).then_inc(m_out, 16)
                sp.wait_ge(m_out, 32)
                for h in range(4):
                    if h >= 2:
                        sp.wait_ge(c_mbused, h - 1)
                    for d in range(2):
                        sp.dma_start(mb[:, h % 2, d, :],
                                     mrow[d, 4 * d + h:4 * d + h + 1, :].broadcast_to([P, L])).then_inc(m_in[h % 2], 16)

                def load_pair(t, hf):
                    sp.dma_start(gzw[hf][:, :, :],
                                 lay(a["w_in"], "(k p) n -> (o p) k n", p=P)[:, :, bass.ds(t * 1024 + (COL["gz"] + 512 * hf), 512)]
                                 ).then_inc(pair_in[hf], 16)
                    wb = a["w_branch"].rearrange("l b (k p) n -> (l b) p k n", p=P)
                    sp.dma_start(wbw[hf][:, :, :],
                                 wb[bass.ds(l * 3 + t, 1), :, :, 512 * hf:512 * hf + 512].rearrange("o p k n -> (o p) k n")
                                 ).then_inc(pair_in[hf], 16)
                sp.wait_ge(slot_used, 8)
                load_pair(0, 0)
                sp.wait_ge(slot_used, 9)
                load_pair(0, 1)
                with sp.Fori(1, 3) as t:
                    for hf in range(2):
                        sp.wait_ge(pair_used, t * 2 + (hf - 1))
                        load_pair(t, hf)
                sp.wait_ge(pair_used, 5)
                wo = lay(a["w_out"], "(k p) n -> (o p) k n", p=P)
                sp.dma_start(wout[0][:, :, :], wo[:, :, 0:512]).then_inc(wout_in[0], 16)
                sp.wait_ge(pair_used, 6)
                sp.dma_start(wout[1][:, :, :], wo[:, :, 512:1024]).then_inc(wout_in[1], 16)

                sp.wait_ge(l_add, NT)
                sp.wait_ge(l_mul, NT)
                for i, n in enumerate(("ln2_g", "ln2_b")):
                    sp.dma_start(lngb[:, i, :], a[n][bass.ds(l, 1), :].broadcast_to([P, DM])).then_inc(ln2_in, 16)

                start_free(sp, "sp")
                sp.wait_ge(r_tab, 1)
                nb = sp.value_load(tab[0:1, MAXB:MAXB + 1], min_val=9, max_val=MAXB)
                wg3 = a["w_gate"].rearrange("l e (k p) n -> (l e) p k n", p=P)
                wu3 = a["w_up"].rearrange("l e (k p) n -> (l e) p k n", p=P)
                wd3 = a["w_down"].rearrange("l e (k p) n -> (l e) p k n", p=P)

                def w_set(j, part):
                    return arena[:, bass.ds((j % 2) * WSET + part * SLOT, SLOT)]

                def load_rows(j):
                    sp.dma_start(xe, xs[bass.ds(j * P, P), :]).then_inc(xe_in, 16)

                def load_w(j, part, e, source, done):
                    sp.dma_start(w_set(j, part).rearrange("p (k n) -> p k n", n=(DE, DE, DM)[part]),
                                 source[bass.ds(e, 1)].rearrange("o p k n -> (o p) k n")).then_inc(done, 16)

                def store_rows(j):
                    sp.dma_start(xs[bass.ds(j * P, P), :], ye).then_inc(ys_out, 16)

                e0 = l * NE + sp.value_load(tab[0:1, 0:1], min_val=0, max_val=NE - 1)
                for part, (source, done) in enumerate(((wg3, wg_in), (wu3, wu_in), (wd3, wd_in))):
                    sp.dma_start(arena[:, part * SLOT:(part + 1) * SLOT].rearrange("p (k n) -> p k n", n=(DE, DE, DM)[part]),
                                 source[bass.ds(e0, 1)].rearrange("o p k n -> (o p) k n")).then_inc(done, 16)
                sp.wait_ge(scattered, l * 160 + 160)
                sp.dma_start(xe, xs[0:P, :]).then_inc(xe_in, 16)
                with sp.Fori(0, nb - 1) as i:
                    e = l * NE + sp.value_load(tab[0:1, bass.ds(i + 1, 1)], min_val=0, max_val=NE - 1)
                    sp.wait_ge(e_xt, i + 1)
                    load_rows(i + 1)
                    sp.wait_ge(e_g, i + 1)
                    sp.wait_ge(wg_in, i * 16 + 16)
                    load_w(i + 1, 0, e, wg3, wg_in)
                    sp.wait_ge(e_u, i + 1)
                    sp.wait_ge(wu_in, i * 16 + 16)
                    load_w(i + 1, 1, e, wu3, wu_in)
                    sp.wait_ge(e_dn, i + 1)
                    sp.wait_ge(wd_in, i * 16 + 16)
                    load_w(i + 1, 2, e, wd3, wd_in)
                    sp.wait_ge(e_ye, i * 2 + 4)
                    store_rows(i)
                sp.wait_ge(e_xt, nb)
                load_rows(nb)
                sp.wait_ge(e_ye, nb * 2 + 2)
                store_rows(nb - 1)
                sp.wait_ge(ys_out, nb * 16 + 16)
                sp.sem_inc(rows_back, 1)

                next_layer(sp)
            sp.dma_start(a["out"][0].rearrange("(i p) n -> p i n", p=P), h_tok[:, 1:NT, :]).then_inc(out_done, 16)
            sp.wait_ge(out_done, 16)

        @block.gpsimd
        def _(pool):
            def norm_bias():
                for i, (_, n) in enumerate(TOK):
                    pool.wait_ge(l_mul, i + 1)
                    pool.tensor_tensor(h_tok[0:n, i, :], h_tok[0:n, i, :], lngb[0:n, 1, :], ALU.add).then_inc(l_add, 1)

            pool.wait_ge(ln0_in, 32)
            norm_bias()
            end_layer(pool, "pool")
            with pool.Fori(0, DEPTH) as l:
                pool.wait_ge(par_in, 80)
                for h in range(4):
                    for j, (t0, n) in enumerate(TOK):
                        for d in range(2):
                            pool.wait_ge(c_mul, 2 * (NT * h + j) + d + 1)
                            at = SAT[d][j] + (0 if d == 0 else t0)
                            blk = sC[h % 2][0:n, at:at + n]
                            sgn = 1 if d == 0 else -1
                            pool.affine_select(out=blk, in_=blk, compare_op=ALU.is_ge, fill=0.0, base=0,
                                               pattern=[[sgn, n]], channel_multiplier=-sgn).then_inc(c_sel, 1)
                pool.wait_ge(par_in, 80)
                for i, (_, n) in enumerate(TOK):
                    pool.wait_ge(l_mul, i + 1)
                    pool.tensor_tensor(h_tok[0:n, i, :], h_tok[0:n, i, :], lngb[0:n, 1, :], ALU.add).then_inc(l_add, 1)
                pool.wait_ge(xs_zeroed, 32)
                pool.wait_ge(l_add, NT)
                pool.wait_ge(r_tab, 1)
                for i, (_, n) in enumerate(TOK):
                    for k in range(2):
                        pool.indirect_dma_start(
                            out=xs, out_offset=bass.IndirectOffsetOnAxis(ap=dst[0:n, i, k:k + 1], axis=0),
                            in_=h_tok[0:n, i, :], in_offset=None).then_inc(scattered, 16)
                pool.wait_ge(rows_back, 1)
                pool.wait_ge(phase_done, 3 * 10)
                for i, (_, n) in enumerate(TOK):
                    for k in range(2):
                        pool.indirect_dma_start(
                            out=gath[0:n, i, k, :], out_offset=None, in_=xs,
                            in_offset=bass.IndirectOffsetOnAxis(ap=dst[0:n, i, k:k + 1], axis=0)).then_inc(gathered[i], 16)
                pool.wait_ge(ln2_in, 32)
                for i, (_, n) in enumerate(TOK):
                    pool.wait_ge(l_mul, NT + i + 1)
                    pool.tensor_tensor(h_tok[0:n, i, :], h_tok[0:n, i, :], lngb[0:n, 1, :], ALU.add).then_inc(l_add, 1)
                end_layer(pool, "pool")

        @block.tensor
        def _(pe):
            def norm_transposes(first):
                for i, (t0, n) in enumerate(TOK):
                    pe.wait_ge(l_add, first + i + 1)
                    if i >= 2:
                        pe.wait_ge(l_ev, first + i - 1)
                    for k in range(KD):
                        mm = pe.transpose(ps[:, 4 + 2 * (i % 2) + k // 4, P * (k % 4):P * (k % 4) + n],
                                          h_tok[0:n, i, P * k:P * k + P], ident[0:n, 0:n])
                    mm.then_inc(l_t, 1)

            def unit(u):
                kind, c, hf = UNITS[u]
                bank = u % 4
                w = slot[WBLOCK[kind] % 3]
                if u >= 4:
                    pe.wait_ge(unit_ev, u - 3)
                if kind in ("av", "bv", "cv", "cg"):
                    t0, n = TOK[c]
                    lo, width = {"av": (0, 512), "bv": (128, 128), "cv": (0, 512), "cg": (256, 16)}[kind]
                    for k in range(KD):
                        mm = pe.matmul(ps[0:n, bank, 0:width], hT[:, k, t0:t0 + n], w[:, k, lo:lo + width],
                                       start=(k == 0), stop=(k == KD - 1))
                else:
                    for k in range(KD):
                        mm = pe.matmul(ps[:, bank, 0:HALF], w[:, k, P * c:P * c + P],
                                       hT[:, k, HALF * hf:HALF * hf + HALF], start=(k == 0), stop=(k == KD - 1))
                mm.then_inc(unit_mm, 1)

            def rotate(u, r):
                pe.wait_ge(unit_ev, u + 1)
                if r >= 4:
                    pe.wait_ge(rot_ev, r - 3)
                pe.matmul(ps[:, 4 + r % 4, 0:HALF], C("rot"), raw[:, r % 4, :], start=True, stop=True).then_inc(rot_mm, 1)

            nd = {3: 16, 4: 2}
            need = []
            tot = [0, 0, 0]
            for n in range(9):
                tot[n % 3] += 16 * nd.get(n, 1)
                need.append(tot[n % 3])

            def units(lo, hi, extra=None):
                r = sum(UNITS[u][0] in ROPE for u in range(lo))
                pending = None
                for u in range(lo, hi):
                    b = WBLOCK[UNITS[u][0]]
                    if u == 0 or WBLOCK[UNITS[u - 1][0]] != b:
                        pe.wait_ge(slot_in[b % 3], need[b])
                    unit(u)
                    if pending is not None:
                        rotate(pending, r)
                        r += 1
                        pending = None
                    if UNITS[u][0] in ROPE:
                        pending = u
                    if extra and u in extra:
                        extra[u]()
                if pending is not None:
                    rotate(pending, r)

            LASTU = {}
            for u, (kind, _, _) in enumerate(UNITS):
                LASTU[WBLOCK[kind]] = u

            def attention_a():
                def scores(n):
                    i, h = n // 4, n % 4
                    t0, m = TOK[i]
                    if n >= 1:
                        pe.wait_ge(a_exp, 2 * n)
                    for hf in range(2):
                        for c in range(2):
                            mm = pe.matmul(ps[0:m, 3 + 2 * c + hf, 0:HALF], qA[64 * c:64 * c + 64, h, t0:t0 + m],
                                           kA[64 * c:64 * c + 64, h, HALF * hf:HALF * hf + HALF], start=True, stop=True)
                            if hf == 1:
                                mm.then_inc(a_s, 1)

                def turn(n):
                    m = TOK[n // 4][1]
                    pe.wait_ge(a_comb, n + 1)
                    if n >= 2:
                        pe.wait_ge(a_tev, n - 1)
                    if n >= 1:
                        pe.wait_ge(a_tmev, n)
                    prob = pA[0:m, n % 2, 0, :]
                    for j in range(1, NT):
                        pe.transpose(ps[:, (7, 1)[n % 2], P * (j - 1):P * (j - 1) + m],
                                     prob[:, TOK[j][0]:TOK[j][0] + P], ident[0:m, 0:m])
                    pe.transpose(ps[0:META, 0, 0:m], prob[:, 0:META], ident[0:m, 0:m]).then_inc(a_t, 1)

                def values(n):
                    i, h = n // 4, n % 4
                    m = TOK[i][1]
                    pe.wait_ge(a_tev, n + 1)
                    pe.wait_ge(a_tmev, n + 1)
                    if h == 0 and i >= 1:
                        pe.wait_ge(a_oev, i)
                    o = ps[0:m, 2, P * h:P * h + P]
                    for j in range(1, NT):
                        pe.matmul(o, ptA[:, n % 2, j - 1, 0:m], vA[:, j, P * h:P * h + P], start=(j == 1), stop=False)
                    pe.matmul(o, ptm[0:META, n % 2, 0:m], vA[0:META, 0, P * h:P * h + P],
                              start=False, stop=True).then_inc(a_o, 1)

                scores(0)
                for n in range(4 * NT):
                    if n + 1 < 4 * NT:
                        scores(n + 1)
                    turn(n)
                    if n >= 1:
                        values(n - 1)
                values(4 * NT - 1)

            def attention_b():
                def scores(n):
                    i = n // 8
                    t0, m = TOK[i]
                    c = BHEAD[n % 8]
                    if n >= 4:
                        pe.wait_ge(b_m, n - 2)
                    at = 0
                    for k0, w in BKEYS[i]:
                        for g in range(2):
                            mm = pe.matmul(ps[0:m, 3 + (n + g) % 4, at:at + w], qB[64 * g:64 * g + 64, c, t0:t0 + m],
                                           kB[64 * g:64 * g + 64, k0:k0 + w], start=True, stop=True)
                            if (k0, w) == BKEYS[i][-1]:
                                mm.then_inc(b_s, 1)
                        at += w

                def turn(n):
                    i = n // 8
                    m = TOK[i][1]
                    pe.wait_ge(b_exp, n + 1)
                    if n >= 2:
                        pe.wait_ge(b_tev, n - 1)
                    if n >= 1:
                        pe.wait_ge(b_tmev, n)
                    for x, j in enumerate(BTILES[i]):
                        pe.transpose(ps[:, (7, 1)[n % 2], P * x:P * x + m],
                                     sB[0:m, n % 3, META + P * x:META + P * x + P], ident[0:m, 0:m])
                    pe.transpose(ps[0:META, 0, 0:m], sB[0:m, n % 3, 0:META], ident[0:m, 0:m]).then_inc(b_t, 1)

                def values(n):
                    i, h = n // 8, BHEAD[n % 8]
                    m, g = TOK[i][1], h // 4
                    pe.wait_ge(b_tev, n + 1)
                    pe.wait_ge(b_tmev, n + 1)
                    if n % 8 == 0 and i >= 1:
                        pe.wait_ge(b_oev, i)
                    o = ps[0:m, 2, 64 * h:64 * h + 64]
                    for x, j in enumerate(BTILES[i]):
                        pe.matmul(o, ptA[:, n % 2, x, 0:m], vB[:, j, 64 * g:64 * g + 64], start=(x == 0), stop=False)
                    pe.matmul(o, ptm[0:META, n % 2, 0:m], vB[0:META, 0, 64 * g:64 * g + 64],
                              start=False, stop=True).then_inc(b_o, 1)

                N = 8 * NT
                scores(0)
                for n in range(N):
                    if n % 2 == 0 and n + 2 < N:
                        scores(n + 2)
                    turn(n)
                    if n >= 1:
                        values(n - 1)
                values(N - 1)

            def branch_transposes(src, first, want):
                for i, (_, n) in enumerate(TOK):
                    want(i)
                    q = first + i
                    if q >= 4:
                        pe.wait_ge(n_ev, q - 3)
                    for c in range(4):
                        mm = pe.transpose(ps[:, 4 + q % 4, P * c:P * c + n], src[0:n, i, P * c:P * c + P], ident[0:n, 0:n])
                    mm.then_inc(n_t, 1)

            def gate_rows():
                pe.wait_ge(g_lf, 1)
                for i, (t0, n) in enumerate(TOK):
                    for kind in range(2):
                        bank, at = (4 + 2 * kind, t0) if i < 4 else (5 + 2 * kind, 0)
                        mm = pe.transpose(ps[0:8, bank, at:at + n], cg[0:n, 1, i, 8 * kind:8 * kind + 8], ident[0:n, 0:n])
                mm.then_inc(g_t, 1)

            def gate_columns():
                pe.wait_ge(g_e, 1)
                pe.wait_ge(g_rows, 1)
                for i, (t0, n) in enumerate(TOK):
                    for x, row in enumerate((UF, UB, EF, EB)):
                        mm = pe.transpose(ps[0:n, 4, 32 * i + 8 * x:32 * i + 8 * x + 8], row[:, t0:t0 + n], ident[0:8, 0:8])
                mm.then_inc(g_t2, 1)

            QKB = (0, 3)

            def mlstm():
                def qk(h, j):
                    q = NT * h + j
                    t0, n = TOK[j]
                    if q >= 2:
                        pe.wait_ge(c_mul, 2 * (q - 1))
                    b = QKB[q % 2]
                    pe.matmul(ps[0:n, b, 0:272], kC[:, h, t0:t0 + n], qC[:, h, 0:272], start=True, stop=True)
                    pe.matmul(ps[0:n, b + 1, 0:256], kC[:, h, t0:t0 + n], qC[:, h, 272:L],
                              start=True, stop=True).then_inc(c_qk, 1)

                def values(h, i):
                    q = NT * h + i
                    t0, m = TOK[i]
                    if i == 0:
                        pe.wait_ge(c_sel, 2 * NT * (h + 1))
                    if q >= 2:
                        pe.wait_ge(c_post, q - 1)
                    bank = 5 + q % 2
                    for d, js in enumerate((range(i + 1), range(i, NT))):
                        for x, j in enumerate(js):
                            n = TOK[j][1]
                            at = SAT[d][j] + t0 - (TOK[j][0] if d == 0 else 0)
                            mm = pe.matmul(ps[0:m, bank, 256 * d:256 * d + 129], sC[h % 2][0:n, at:at + m],
                                           vC[0:n, j, h, :], start=(x == 0), stop=(x == len(js) - 1))
                    mm.then_inc(c_pv, 1)

                for h in range(5):
                    for j in range(NT):
                        if h < 4:
                            qk(h, j)
                        if h >= 1:
                            values(h - 1, j)

            def gates():
                with pe.Fori(0, 3) as t:
                    for hf in range(2):
                        pe.wait_ge(pair_in[hf], t * 32 + 32)
                        for c in range(4):
                            u = 4 * hf + c
                            s = 4 * (u % 2)
                            pe.wait_ge(gate_free, t * 8 + (u + 1))
                            for b in range(2):
                                for k in range(KD):
                                    pe.matmul(ps[:, s + b, 0:HALF], gzw[hf][:, k, P * c:P * c + P],
                                              hT[:, k, HALF * b:HALF * b + HALF], start=(k == 0), stop=(k == KD - 1))
                            for b in range(2):
                                for k in range(4):
                                    mm = pe.matmul(ps[:, s + 2 + b, 0:HALF], wbw[hf][:, k, P * c:P * c + P],
                                                   arena[:, bass.ds(t * (4 * L) + (Y + k * L + HALF * b), HALF)],
                                                   start=(k == 0), stop=(k == 3))
                            mm.then_inc(gate_mm, 1)
                        pe.drain().then_inc(pair_used, 1)

            def project_out():
                for i, (t0, n) in enumerate(TOK):
                    for hf in range(2):
                        q = 2 * i + hf
                        if i == 0:
                            pe.wait_ge(wout_in[hf], 16)
                        if q >= 4:
                            pe.wait_ge(y_ev, q - 3)
                        for k in range(KD):
                            mm = pe.matmul(ps[0:n, q % 4, :], merged[:, k, t0:t0 + n], wout[hf][:, k, :],
                                           start=(k == 0), stop=(k == KD - 1))
                        mm.then_inc(y_mm, 1)

            def router():
                pe.wait_ge(l_ev, NT)
                for i, (t0, n) in enumerate(TOK):
                    for k in range(KD):
                        mm = pe.matmul(ps[0:n, 0, 36 * i:36 * i + 36], hT[:, k, t0:t0 + n], w_r[:, k, :],
                                       start=(k == 0), stop=(k == KD - 1))
                mm.then_inc(r_mm, 1)
                pe.wait_ge(r_cnt, 1)
                for i in range(NT + 1):
                    for j in range(min(i + 1, NT)):
                        whole = j < i
                        mm = pe.matmul(ps[:, 1, NE * i:NE * i + NE], C("ones") if whole else C("ltri"), e32[:, 2, j, :],
                                       start=(j == 0), stop=(j == min(i, NT - 1)))
                mm.then_inc(r_rank, 1)

            def experts():
                start_free(pe, "pe")
                pe.wait_ge(r_tab, 1)
                nb = pe.value_load(tab[0:1, MAXB:MAXB + 1], min_val=9, max_val=MAXB)

                def rows_turn():
                    for k in range(KD):
                        mm = pe.transpose(ps[:, 2 + k // 4, P * (k % 4):P * (k % 4) + P], xe[:, P * k:P * k + P], ident)
                    mm.then_inc(e_xt, 1)

                pe.wait_ge(xe_in, 16)
                rows_turn()
                with pe.Fori(0, nb) as j:
                    def weights(part, at, n):
                        return arena[:, bass.ds((j % 2) * WSET + (part * SLOT + at), n)]

                    pe.wait_ge(e_xtev, j + 1)
                    pe.wait_ge(e_sil, j + 1)
                    pe.wait_ge(wg_in, j * 16 + 16)
                    for k in range(KD):
                        mm = pe.matmul(ps[:, 0, :], xeT[:, k, :], weights(0, DE * k, DE), start=(k == 0), stop=(k == KD - 1))
                    mm.then_inc(e_g, 1)
                    pe.wait_ge(e_hid, j + 1)
                    pe.wait_ge(wu_in, j * 16 + 16)
                    for k in range(KD):
                        mm = pe.matmul(ps[:, 1, :], xeT[:, k, :], weights(1, DE * k, DE), start=(k == 0), stop=(k == KD - 1))
                    mm.then_inc(e_u, 1)
                    pe.wait_ge(xe_in, j * 16 + 32)
                    rows_turn()
                    pe.wait_ge(e_hid, j + 2)
                    for c in range(4):
                        mm = pe.transpose(ps[:, 4, P * c:P * c + P], hid[:, P * c:P * c + P], ident)
                    mm.then_inc(e_ht, 1)
                    pe.wait_ge(e_htev, j + 1)
                    pe.wait_ge(wd_in, j * 16 + 16)
                    pe.wait_ge(e_ye, j * 2 + 2)
                    for hf in range(2):
                        for k in range(4):
                            mm = pe.matmul(ps[:, 5 + hf, :], hidT[:, k, :], weights(2, DM * k + 512 * hf, 512),
                                           start=(k == 0), stop=(k == 3))
                    mm.then_inc(e_dn, 1)

            pe.wait_ge(const_in, 16)
            norm_transposes(0)
            end_layer(pe, "pe")
            with pe.Fori(0, DEPTH) as l:
                phase = Phase(pe)
                block_done = lambda: pe.drain().then_inc(slot_used, 1)
                units(0, NAB, {LASTU[b]: block_done for b in range(4)})
                phase()
                attention_a()
                phase()
                attention_b()
                phase()
                branch_transposes(oA, 0, lambda i: pe.wait_ge(n_norm, i + 1))
                branch_transposes(oB, NT, lambda i: pe.wait_ge(b_oev, NT))
                phase()

                def cq_done():
                    block_done()
                    gate_rows()

                def cv_done():
                    block_done()
                    gate_columns()

                units(NAB, len(UNITS), {LASTU[4]: block_done, LASTU[5]: cq_done, LASTU[6]: block_done,
                                        LASTU[7]: cv_done, LASTU[8]: block_done})
                phase()
                mlstm()
                phase()
                branch_transposes(hsum, 2 * NT, lambda i: pe.wait_ge(n_norm, NT + i + 1))
                phase()
                gates()
                phase()
                project_out()
                norm_transposes(0)
                router()
                phase()
                experts()
                phase()
                norm_transposes(NT)
                end_layer(pe, "pe")

        @block.scalar
        def _(act):
            steps = [0]

            def link(ins):
                steps[0] += 1
                ins.then_inc(act_step, 1)
                act.wait_ge(act_step, steps[0])

            def norm_root(n):
                act.wait_ge(l_var, n)
                act.activation(rstd[:, :], rstd[:, :], ACT.Sqrt).then_inc(l_sqrt, 1)

            def norm_evacuate(first):
                for i, (t0, n) in enumerate(TOK):
                    act.wait_ge(l_t, first + i + 1)
                    b = 4 + 2 * (i % 2)
                    act.activation(hT[:, 0:4, t0:t0 + n], ps[:, b, :].rearrange("p (k n) -> p k n", n=P)[:, :, 0:n], ACT.Copy)
                    act.activation(hT[:, 4:8, t0:t0 + n], ps[:, b + 1, :].rearrange("p (k n) -> p k n", n=P)[:, :, 0:n],
                                   ACT.Copy).then_inc(l_ev, 1)

            def evacuate(u, r, chunk):
                kind, c, hf = UNITS[u]
                bank = ps[:, u % 4, :]
                act.wait_ge(unit_mm, u + 1)
                cols = slice(HALF * hf, HALF * hf + HALF)
                if kind in ROPE:
                    if r >= 4:
                        act.wait_ge(rot_ev, r - 3)
                    scale = QSCALE if kind in ("aq", "bq") else 1.0
                    act.activation(raw[:, r % 4, :], bank[:, 0:HALF], ACT.Copy, scale=scale).then_inc(unit_ev, 1)
                elif kind in ("av", "bv", "cv", "cg"):
                    n = TOK[c][1]
                    if kind == "av":
                        o, i_ = vA[0:n, c, :], bank[0:n, :]
                    elif kind == "bv":
                        o, i_ = vB[0:n, c, :], bank[0:n, 0:128]
                    elif kind == "cv":
                        o, i_ = vC[0:n, c, :, 0:128], bank[0:n, :].rearrange("p (h d) -> p h d", d=128)
                    else:
                        o, i_ = cg[0:n, 0, c, :], bank[0:n, 0:16]
                    act.activation(o, i_, ACT.Copy).then_inc(unit_ev, 1)
                elif kind in ("cq", "ck"):
                    if chunk >= 2:
                        act.wait_ge(conv_done, chunk - 1)
                    act.activation(craw[:, chunk % 2, 1 + HALF * hf:1 + HALF * hf + HALF], bank[:, 0:HALF],
                                   ACT.Copy).then_inc(unit_ev, 1)
                else:
                    act.activation(sco[:, c, cols], bank[:, 0:HALF], ACT.Sigmoid).then_inc(unit_ev, 1)

            def attention_a():
                def exp(n, c):
                    m = TOK[n // 4][1]
                    act.wait_ge(a_m, 2 * n + c + 1)
                    if n >= 2 and c == 0:
                        act.wait_ge(a_t, n - 1)
                    act.activation(two(pA[0:m, n % 2, c, :]), halves(3 + 2 * c, m), ACT.Exp,
                                   bias=st[0:m, 2 * (n % 2) + c:2 * (n % 2) + c + 1],
                                   accum_out=st[0:m, 4 + 2 * (n % 2) + c:5 + 2 * (n % 2) + c]).then_inc(a_exp, 1)

                def evac(n):
                    m = TOK[n // 4][1]
                    act.wait_ge(a_t, n + 1)
                    if n >= 2:
                        act.wait_ge(a_o, n - 1)
                    act.activation(ptA[:, n % 2, :, 0:m],
                                   ps[:, (7, 1)[n % 2], :].rearrange("p (j q) -> p j q", q=P)[:, :, 0:m],
                                   ACT.Copy).then_inc(a_tev, 1)

                for n in range(4 * NT):
                    exp(n, 0)
                    if n >= 1:
                        evac(n - 1)
                    exp(n, 1)
                evac(4 * NT - 1)

            def attention_b():
                def exp(n):
                    i, h = n // 8, BHEAD[n % 8]
                    m = TOK[i][1]
                    act.wait_ge(b_m, n + 1)
                    act.activation(sB[0:m, n % 3, 0:bwidth[i]], sB[0:m, n % 3, 0:bwidth[i]], ACT.Exp,
                                   bias=st[0:m, 16 + h:17 + h],
                                   accum_out=st[0:m, 24 + h:25 + h]).then_inc(b_exp, 1)

                def evac(n):
                    i = n // 8
                    m, nbk = TOK[i][1], len(BTILES[i])
                    act.wait_ge(b_t, n + 1)
                    if n >= 2:
                        act.wait_ge(b_o, n - 1)
                    act.activation(ptA[:, n % 2, 0:nbk, 0:m],
                                   ps[:, (7, 1)[n % 2], 0:P * nbk].rearrange("p (j q) -> p j q", q=P)[:, :, 0:m],
                                   ACT.Copy).then_inc(b_tev, 1)

                for n in range(8 * NT):
                    exp(n)
                    if n >= 1:
                        evac(n - 1)
                    if n % 8 == 7:
                        m = TOK[n // 8][1]
                        act.wait_ge(b_snk, 2 * (n // 8) + 1)
                        act.activation(st[0:m, 40:48], st[0:m, 32:40], ACT.Exp).then_inc(b_snk, 1)
                evac(8 * NT - 1)

            def mlstm():
                for h in range(4):
                    act.wait_ge(m_in[h % 2], 32 * (h // 2 + 1))
                    for j, (t0, n) in enumerate(TOK):
                        for d in range(2):
                            lo, hi = (t0, L) if d == 0 else (0, t0 + n)
                            if h >= 2 and j == 0 and d == 0:
                                act.wait_ge(c_pv, NT * (h - 1))
                            col = 8 * d + 4 * d + h
                            act.activation(sC[h % 2][0:n, SAT[d][j]:SAT[d][j] + hi - lo], mb[0:n, h % 2, d, lo:hi], ACT.Exp,
                                           scale=-1.0, bias=gcol[0:n, j, col:col + 1]).then_inc(c_w, 1)
                    act.drain().then_inc(c_mbused, 1)

            norm_root(1)
            norm_evacuate(0)
            end_layer(act, "act")
            with act.Fori(0, DEPTH) as l:
                phase = Phase(act)
                steps[0] = 0
                r = 0
                for u in range(NAB):
                    evacuate(u, r, 0)
                    r += UNITS[u][0] in ROPE
                act.wait_ge(n_ready, 1)
                act.activation(st[:, 10:12], st[:, 8:10], ACT.Exp).then_inc(n_sqrt, 1)
                phase()
                attention_a()
                phase()
                act.wait_ge(n_ready, 2)
                act.activation(ssr[:, :, :], ssr[:, :, :], ACT.Sqrt).then_inc(n_sqrt, 1)
                attention_b()
                phase()
                for q in range(2 * NT):
                    t0, n = TOK[q % NT]
                    act.wait_ge(n_t, q + 1)
                    src = ps[:, 4 + q % 4, :].rearrange("p (c t) -> p c t", t=P)[:, :, 0:n]
                    act.activation(outT[:, q // NT, :, t0:t0 + n], src, ACT.Copy,
                                   scale=(colp[:, 36:37] if q < NT else 1.0)).then_inc(n_ev, 1)
                phase()
                chunk = 0

                def silu(ch):
                    c = ch % 4
                    act.wait_ge(conv_done, ch + 1)
                    d_ = (qC if ch < 4 else kC)[:, c, :]
                    act.activation(d_, ctmp[:, ch % 2, :], ACT.Silu, bias=colp[:, 24 + ch:25 + ch]).then_inc(silu_done, 1)

                for u in range(NAB, len(UNITS)):
                    kind, c, hf = UNITS[u]
                    if kind in ("cq", "ck") and hf == 0:
                        chunk = c + 4 * (kind == "ck")
                        if chunk >= 2:
                            silu(chunk - 2)
                    if kind == "cq" and c == 0 and hf == 0:
                        act.wait_ge(g_exp, 1)
                        act.activation(cg[:, 1, :, :], cg[:, 1, :, :], ACT.Exp, scale=-1.0).then_inc(g_exp, 1)
                        act.wait_ge(g_exp, 2)
                        act.activation(cg[:, 1, :, :], cg[:, 1, :, :], ACT.Ln, bias=1.0).then_inc(g_ln, 1)
                    if kind == "cv" and c == 0:
                        silu(6)
                        silu(7)
                        act.wait_ge(g_rows, 1)
                        act.activation(EF, EF, ACT.Exp, scale=-1.0)
                        act.activation(EB, EB, ACT.Exp, scale=-1.0).then_inc(g_e, 1)
                    evacuate(u, 0, chunk)
                phase()
                mlstm()
                phase()
                act.wait_ge(n_ready, 3)
                act.activation(ssr[:, :, :], ssr[:, :, :], ACT.Sqrt).then_inc(n_sqrt, 1)
                phase()
                with act.Fori(0, 3) as t:
                    for u in range(8):
                        act.wait_ge(gate_mm, t * 8 + (u + 1))
                        act.activation(two(sg[:, u % 2, :]), halves(4 * (u % 2)), ACT.Sigmoid).then_inc(gate_sig, 1)
                phase()
                norm_root(1)
                norm_evacuate(0)
                act.wait_ge(r_a, 1)
                act.activation(r4[:, 0, :, :], r4[:, 0, :, :], ACT.Exp).then_inc(r_exp, 1)
                act.wait_ge(r_b, 1)
                act.activation(r5[:, 4, :], r5[:, 3, :], ACT.Exp).then_inc(r_exp2, 1)
                phase()
                start_free(act, "act")
                nb = act.value_load(tab[0:1, MAXB:MAXB + 1], min_val=9, max_val=MAXB)

                def rows_evacuate(done):
                    act.wait_ge(e_xt, done)
                    act.activation(xeT[:, :, :].rearrange("p (b k) n -> p b (k n)", b=2), ps[:, 2:4, :], ACT.Copy).then_inc(e_xtev, 1)

                rows_evacuate(1)
                with act.Fori(0, nb) as j:
                    act.wait_ge(e_g, j + 2)
                    act.activation(sil, ps[:, 0, :], ACT.Silu).then_inc(e_sil, 1)
                    act.wait_ge(e_u, j + 2)
                    rows_evacuate(j + 2)
                    act.wait_ge(ys_out, j * 16 + 16)
                    act.wait_ge(e_dn, j + 2)
                    act.activation(ye[:, 512:1024], ps[:, 6, :], ACT.Copy).then_inc(e_ye, 1)
                phase()
                norm_root(2)
                norm_evacuate(NT)
                end_layer(act, "act")

        @block.vector
        def _(dve):
            steps = [0]

            def link(ins):
                steps[0] += 1
                ins.then_inc(dve_step, 1)
                dve.wait_ge(dve_step, steps[0])

            def norm_stats(i, n):
                dve.bn_stats(bn[0:n, i, 0:6], h_tok[0:n, i, 0:512])
                link(dve.bn_stats(bn[0:n, i, 6:12], h_tok[0:n, i, 512:1024]))
                link(dve.bn_aggr(mv[0:n, i, :], bn[0:n, i, :]))

            def norm_apply(n_sq):
                dve.tensor_scalar(rstd[:, :], mv[:, :, 1], EPS, None, ALU.add).then_inc(l_var, 1)
                dve.wait_ge(l_sqrt, n_sq)
                link(dve.reciprocal(rstd[:, :], rstd[:, :]))
                for i, (_, n) in enumerate(TOK):
                    link(dve.tensor_scalar(h_tok[0:n, i, :], h_tok[0:n, i, :], mv[0:n, i, 0:1], rstd[0:n, i:i + 1],
                                           ALU.subtract, ALU.mult))
                    dve.tensor_tensor(h_tok[0:n, i, :], h_tok[0:n, i, :], lngb[0:n, 0, :], ALU.mult).then_inc(l_mul, 1)

            def rope(u, r):
                kind, c, hf = UNITS[u]
                cols = slice(HALF * hf, HALF * hf + HALF)
                dve.wait_ge(rot_mm, r + 1)
                dve.tensor_tensor(t_sin[:, r % 2, :], ps[:, 4 + r % 4, 0:HALF], C("sin")[:, cols], ALU.mult)
                link(dve.tensor_tensor(raw[:, r % 4, :], raw[:, r % 4, :], C("cos")[:, cols], ALU.mult))
                dve.tensor_tensor(ROPE[kind](c)[:, cols], raw[:, r % 4, :], t_sin[:, r % 2, :], ALU.add).then_inc(rot_ev, 1)

            def attention_a():
                nlam = st[:, 12:13]

                def rowmax(n, c):
                    m = TOK[n // 4][1]
                    dve.wait_ge(a_s, 2 * n + c + 1)
                    dve.tensor_reduce(st[0:m, 2 * (n % 2) + c:2 * (n % 2) + c + 1], halves(3 + 2 * c, m), AX.XY, ALU.max,
                                      negate=True).then_inc(a_m, 1)

                def combine(n):
                    i, h = n // 4, n % 4
                    m = TOK[i][1]
                    s = 4 + 2 * (n % 2)
                    dve.wait_ge(a_exp, 2 * n + 2)
                    dve.reciprocal(rs[0:m, 0, i, h:h + 1], st[0:m, s:s + 1])
                    link(dve.reciprocal(st[0:m, 14:15], st[0:m, s + 1:s + 2]))
                    link(dve.scalar_tensor_tensor(st[0:m, 13:14], st[0:m, s:s + 1], nlam[0:m, :], st[0:m, 14:15], ALU.mult, ALU.mult))
                    dve.scalar_tensor_tensor(pA[0:m, n % 2, 0, :], pA[0:m, n % 2, 1, :], st[0:m, 13:14], pA[0:m, n % 2, 0, :],
                                             ALU.mult, ALU.add).then_inc(a_comb, 1)

                def meta_evac(n):
                    m = TOK[n // 4][1]
                    dve.wait_ge(a_t, n + 1)
                    if n >= 2:
                        dve.wait_ge(a_o, n - 1)
                    dve.tensor_copy(ptm[0:META, n % 2, 0:m], ps[0:META, 0, 0:m]).then_inc(a_tmev, 1)

                def out(i):
                    m = TOK[i][1]
                    dve.wait_ge(a_o, 4 * (i + 1))
                    dve.tensor_tensor(oA[0:m, i, :].rearrange("p (h d) -> p h d", d=P),
                                      ps[0:m, 2, :].rearrange("p (h d) -> p h d", d=P),
                                      rs[0:m, 0, i, 0:4].unsqueeze(2).broadcast_to([m, 4, P]), ALU.mult).then_inc(a_oev, 1)

                rowmax(0, 0)
                rowmax(0, 1)
                for n in range(4 * NT):
                    if n >= 1:
                        meta_evac(n - 1)
                    combine(n)
                    if n + 1 < 4 * NT:
                        rowmax(n + 1, 0)
                    if n >= 4 and n % 4 == 0:
                        out(n // 4 - 1)
                    if n + 1 < 4 * NT:
                        rowmax(n + 1, 1)
                meta_evac(4 * NT - 1)
                out(NT - 1)

            def attention_b():
                def rowmax(n):
                    i, h = n // 8, BHEAD[n % 8]
                    m, w = TOK[i][1], bwidth[i]
                    dve.wait_ge(b_s, n + 1)
                    if n >= 2:
                        dve.wait_ge(b_m, n - 1)
                    if n >= 3:
                        dve.wait_ge(b_t, n - 2)
                    link(dve.tensor_tensor_reduce(sB[0:m, n % 3, 0:w], ps[0:m, 3 + n % 4, 0:w], C(BMASK[i], m, w), 1.0, LOW,
                                                  ALU.add, ALU.max, st[0:m, 60 + n % 2:61 + n % 2]))
                    dve.tensor_scalar(st[0:m, 16 + h:17 + h], st[0:m, 60 + n % 2:61 + n % 2], R("sink")[0:m, h:h + 1], -1.0, ALU.max, ALU.mult
                                      ).then_inc(b_m, 1)

                def meta_evac(n):
                    m = TOK[n // 8][1]
                    dve.wait_ge(b_t, n + 1)
                    if n >= 2:
                        dve.wait_ge(b_o, n - 1)
                    dve.tensor_copy(ptm[0:META, n % 2, 0:m], ps[0:META, 0, 0:m]).then_inc(b_tmev, 1)

                def sink(i):
                    m = TOK[i][1]
                    dve.wait_ge(b_m, 8 * (i + 1))
                    dve.tensor_tensor(st[0:m, 32:40], R("sink")[0:m, :], st[0:m, 16:24], ALU.add).then_inc(b_snk, 1)
                    dve.wait_ge(b_exp, 8 * (i + 1))
                    dve.wait_ge(b_snk, 2 * (i + 1))
                    link(dve.tensor_tensor(st[0:m, 48:56], st[0:m, 24:32], st[0:m, 40:48], ALU.add))
                    link(dve.reciprocal(rs[0:m, 1, i, :], st[0:m, 48:56]))

                def out(i):
                    m = TOK[i][1]
                    dve.wait_ge(b_o, 8 * (i + 1))
                    dve.tensor_tensor(oB[0:m, i, :].rearrange("p (h d) -> p h d", d=64),
                                      ps[0:m, 2, :].rearrange("p (h d) -> p h d", d=64),
                                      rs[0:m, 1, i, :].unsqueeze(2).broadcast_to([m, 8, 64]), ALU.mult).then_inc(b_oev, 1)

                N = 8 * NT
                rowmax(0)
                for n in range(N):
                    if n >= 1:
                        meta_evac(n - 1)
                    if n >= 8 and n % 8 == 0:
                        out(n // 8 - 1)
                    if n % 8 == 7:
                        sink(n // 8)
                    if n + 1 < N:
                        rowmax(n + 1)
                meta_evac(N - 1)
                out(NT - 1)

            def lambdas():
                dve.wait_ge(par_in, 80)
                lam = R("lam").rearrange("p (a b) -> p a b", b=64)
                for x in range(2):
                    ins = dve.tensor_tensor_reduce(t_sin[:, 0, 64 * x:64 * x + 64], lam[:, 2 * x, :], lam[:, 2 * x + 1, :], 1.0, 0.0,
                                                   ALU.mult, ALU.add, st[:, 8 + x:9 + x])
                ins.then_inc(n_ready, 1)
                dve.wait_ge(n_ready, 1)

            def lambda_end():
                dve.wait_ge(n_sqrt, 1)
                link(dve.tensor_tensor(st[:, 13:14], st[:, 11:12], st[:, 10:11], ALU.subtract))
                link(dve.tensor_tensor(st[:, 12:13], st[:, 13:14], R("neg_lam_init"), ALU.add))
                link(dve.tensor_tensor(colp[:, 36:37], colp[:, 36:37], R("one_minus"), ALU.mult))

            def rms_stats():
                for i, (_, n) in enumerate(TOK):
                    o = oA[0:n, i, :]
                    link(dve.tensor_tensor(sq[0:n, i % 2, :], o, o, ALU.mult))
                    link(dve.tensor_reduce(ssr[0:n, i, :], sq[0:n, i % 2, :].rearrange("p (h d) -> p h d", d=P), AX.X, ALU.add))
                dve.tensor_scalar(ssr[:, :, :], ssr[:, :, :], 1.0 / P, EPS, ALU.mult, ALU.add).then_inc(n_ready, 1)

            def rms_apply():
                dve.wait_ge(n_sqrt, 2)
                link(dve.reciprocal(ssr[:, :, :], ssr[:, :, :]))
                for i, (_, n) in enumerate(TOK):
                    o = oA[0:n, i, :].rearrange("p (h d) -> p h d", d=P)
                    dve.tensor_tensor(o, o, ssr[0:n, i, :].unsqueeze(2).broadcast_to([n, 4, P]), ALU.mult).then_inc(n_norm, 1)

            def gate_logs():
                dve.wait_ge(unit_ev, NAB + NT)
                link(dve.tensor_tensor(cg[:, 0, :, :], cg[:, 0, :, :], R("gate_b").unsqueeze(1).broadcast_to([P, NT, 16]), ALU.add))
                dve.scalar_tensor_tensor(cg[:, 1, :, :], cg[:, 0, :, :], -1.0, cg[:, 0, :, :], ALU.mult, ALU.max).then_inc(g_exp, 1)

            def gate_logs2():
                dve.wait_ge(g_ln, 1)
                z = cg[:, 0, :, :].rearrange("p t (d k h) -> p t d k h", d=2, k=2)
                for d in range(2):
                    zl = z[:, :, d, 1, :]
                    ll = cg[:, 1, :, 8 * d + 4:8 * d + 8]
                    link(dve.scalar_tensor_tensor(zl, zl, 0.0, ll, ALU.min, ALU.subtract))
                for d in range(2):
                    dve.tensor_copy(cg[:, 1, :, 4 * d:4 * d + 4], z[:, :, d, 1, :])
                    ins = dve.tensor_copy(cg[:, 1, :, 8 + 4 * d:12 + 4 * d], z[:, :, d, 0, :])
                ins.then_inc(g_lf, 1)

            def gate_scans():
                dve.wait_ge(g_t, 1)
                dve.memset(ZR, 0.0)
                for bank, row in ((4, LF), (6, LI)):
                    dve.tensor_copy(row[:, 0:400], ps[0:8, bank, 0:400])
                    link(dve.tensor_copy(row[:, 400:L], ps[0:8, bank + 1, 0:P]))
                dve.tensor_tensor_scan(BF, ZR, LF, 0.0, ALU.add, ALU.add)
                link(dve.tensor_tensor_scan(BB[:, ::-1], ZR, LF[:, ::-1], 0.0, ALU.add, ALU.add))
                dve.tensor_tensor(UF, LI, BF, ALU.subtract)
                link(dve.tensor_tensor(UB, LI, BB, ALU.subtract))
                dve.tensor_tensor_scan(MF, ZR, UF, 0.0, ALU.add, ALU.max)
                link(dve.tensor_tensor_scan(MB[:, ::-1], ZR, UB[:, ::-1], 0.0, ALU.add, ALU.max))
                dve.tensor_tensor(EF, MF, BF, ALU.add)
                dve.tensor_tensor(EB, MB, BB, ALU.add).then_inc(g_rows, 1)

            def gate_cols():
                dve.wait_ge(g_t2, 1)
                dve.tensor_copy(gcol[0:META, 0, :], ps[0:META, 4, 0:32])
                dve.tensor_copy(gcol[:, 1:NT, :], ps[:, 4, 32:32 * NT].rearrange("p (t x) -> p t x", x=32)).then_inc(g_col, 1)

            def conv(ch):
                u = NAB + NT + 2 * ch + 1
                dve.wait_ge(unit_ev, u + 1)
                if ch >= 2:
                    dve.wait_ge(silu_done, ch - 1)
                src, o = craw[:, ch % 2, :], ctmp[:, ch % 2, :]
                tap = [colp[:, 3 * ch + k:3 * ch + k + 1] for k in range(3)]
                link(dve.tensor_scalar(o, src[:, 0:L], tap[0], None, ALU.mult))
                link(dve.scalar_tensor_tensor(o, src[:, 1:L + 1], tap[1], o, ALU.mult, ALU.add))
                dve.scalar_tensor_tensor(o, src[:, 2:L + 2], tap[2], o, ALU.mult, ALU.add).then_inc(conv_done, 1)

            def mlstm():
                def weigh(h, j):
                    q = NT * h + j
                    t0, n = TOK[j]
                    b = (0, 3)[q % 2]
                    dve.wait_ge(c_qk, q + 1)
                    for d in range(2):
                        lo, hi = (t0, L) if d == 0 else (0, t0 + n)
                        dve.wait_ge(c_w, 2 * q + d + 1)
                        for bank, x0, x1 in ((b, lo, min(hi, 272)), (b + 1, max(lo, 272), hi)):
                            if x1 > x0:
                                s = sC[h % 2][0:n, SAT[d][j] + x0 - lo:SAT[d][j] + x1 - lo]
                                base = 0 if bank == b else 272
                                ins = dve.scalar_tensor_tensor(s, ps[0:n, bank, x0 - base:x1 - base], MSCALE, s, ALU.mult, ALU.mult)
                        ins.then_inc(c_mul, 1)

                def post(h, i):
                    q = NT * h + i
                    m = TOK[i][1]
                    dve.wait_ge(c_pv, q + 1)
                    bank = ps[0:m, 5 + q % 2, :]
                    den = bank.rearrange("p (d x) -> p d x", x=256)[:, :, 128]
                    em = gcol[0:m, i, 16:32].rearrange("p (d x) -> p d x", x=8)
                    for d in range(2):
                        ins = dve.tensor_scalar(st[0:m, 56 + d:57 + d], den[:, d:d + 1], -1.0, em[:, d, 4 * d + h:4 * d + h + 1],
                                                ALU.mult, ALU.max)
                    link(ins)
                    link(dve.tensor_tensor(st[0:m, 56:58], st[0:m, 56:58], den, ALU.max))
                    link(dve.reciprocal(st[0:m, 58:60], st[0:m, 56:58]))
                    o = hsum[0:m, i, P * h:P * h + P]
                    link(dve.tensor_scalar(o, bank[:, 0:P], st[0:m, 58:59], None, ALU.mult))
                    link(dve.scalar_tensor_tensor(o, bank[:, 256:256 + P], st[0:m, 59:60], o, ALU.mult, ALU.add))
                    dve.bn_stats(bn[0:m, i, 0:6], o).then_inc(c_post, 1)
                    dve.wait_ge(c_post, q + 1)
                    dve.bn_aggr(ss[0:m, i, h, :], bn[0:m, i, 0:6])

                for h in range(5):
                    for j in range(NT):
                        if h < 4:
                            weigh(h, j)
                        if h >= 1:
                            post(h - 1, j)

            def c_norm():
                link(dve.tensor_scalar(ssr[:, :, :], ss[:, :, :, 1], EPS, None, ALU.add))
                dve.drain().then_inc(n_ready, 1)
                dve.wait_ge(n_sqrt, 3)
                link(dve.reciprocal(ssr[:, :, :], ssr[:, :, :]))
                for i, (_, n) in enumerate(TOK):
                    for h in range(4):
                        o = hsum[0:n, i, P * h:P * h + P]
                        ins = dve.tensor_scalar(o, o, ss[0:n, i, h, 0:1], ssr[0:n, i, h:h + 1], ALU.subtract, ALU.mult)
                    ins.then_inc(n_norm, 1)

            def c_out():
                for i, (t0, n) in enumerate(TOK):
                    q = 2 * NT + i
                    dve.wait_ge(n_t, q + 1)
                    for c in range(4):
                        ins = dve.scalar_tensor_tensor(outT[:, 2, c, t0:t0 + n], ps[:, 4 + q % 4, P * c:P * c + n],
                                                       colp[:, 32 + c:33 + c], sco[:, c, t0:t0 + n], ALU.mult, ALU.mult)
                    ins.then_inc(n_ev, 1)

            def router():
                dve.wait_ge(r_mm, 1)
                for i, (_, n) in enumerate(TOK):
                    ins = dve.tensor_tensor(lg[0:n, i, :], ps[0:n, 0, 36 * i:36 * i + 36], R("b_r")[0:n, :], ALU.add)
                link(ins)
                g4, x32 = lg[:, :, 0:4], lg[:, :, 4:36]
                b5 = lambda k, w: r5[:, k, :].unsqueeze(2).broadcast_to([P, NT, w])
                link(dve.tensor_reduce(r5[:, 0, :], g4, AX.X, ALU.max))
                dve.tensor_tensor(r4[:, 0, :, :], g4, b5(0, 4), ALU.subtract).then_inc(r_a, 1)
                link(dve.tensor_tensor(r4[:, 1, :, :], g4, b5(0, 4), ALU.is_equal))
                link(dve.tensor_tensor(r4[:, 1, :, :], r4[:, 1, :, :], C("wg4").unsqueeze(1).broadcast_to([P, NT, 4]), ALU.mult))
                link(dve.tensor_reduce(r5[:, 1, :], r4[:, 1, :, :], AX.X, ALU.max))
                link(dve.tensor_tensor(r4[:, 2, :, :], r4[:, 1, :, :], b5(1, 4), ALU.is_equal))
                link(dve.tensor_scalar(r4[:, 2, :, :], r4[:, 2, :, :], -1.0, -NEG, ALU.add, ALU.mult))
                dve.wait_ge(xs_zeroed, 32)
                em = e32[:, 3, :, :]
                link(dve.tensor_tensor(em.rearrange("p t (g e) -> p t g e", e=8), x32.rearrange("p t (g e) -> p t g e", e=8),
                                       r4[:, 2, :, :].unsqueeze(3).broadcast_to([P, NT, 4, 8]), ALU.add))
                we = C("we32").unsqueeze(1).broadcast_to([P, NT, NE])
                for k in range(2):
                    oh = e32[:, k, :, :]
                    link(dve.tensor_reduce(r5[:, 5 + k, :], em, AX.X, ALU.max))
                    link(dve.tensor_tensor(oh, em, b5(5 + k, NE), ALU.is_equal))
                    link(dve.tensor_tensor(oh, oh, we, ALU.mult))
                    link(dve.tensor_reduce(r5[:, 1, :], oh, AX.X, ALU.max))
                    link(dve.tensor_tensor(oh, oh, b5(1, NE), ALU.is_equal))
                    if k == 0:
                        link(dve.scalar_tensor_tensor(em, oh, 2 * NEG, em, ALU.mult, ALU.add))
                dve.tensor_tensor(r5[:, 3, :], r5[:, 6, :], r5[:, 5, :], ALU.subtract).then_inc(r_b, 1)
                link(dve.tensor_tensor(e32[:, 2, :, :], e32[:, 0, :, :], e32[:, 1, :, :], ALU.add))
                dve.tensor_tensor(e32[:, 2, :, :], e32[:, 2, :, :], C("valid").unsqueeze(2).broadcast_to([P, NT, NE]),
                                  ALU.mult).then_inc(r_cnt, 1)
                dve.wait_ge(r_exp, 1)
                link(dve.tensor_reduce(r5[:, 2, :], r4[:, 0, :, :], AX.X, ALU.add))
                dve.wait_ge(r_exp2, 1)
                link(dve.scalar_tensor_tensor(r5[:, 9, :], r5[:, 4, :], 1.0, r5[:, 2, :], ALU.add, ALU.mult))
                link(dve.reciprocal(r5[:, 7, :], r5[:, 9, :]))
                link(dve.tensor_tensor(r5[:, 8, :], r5[:, 7, :], r5[:, 4, :], ALU.mult))
                dve.wait_ge(r_rank, 1)
                link(dve.tensor_copy(n32[:, 0, :], ps[:, 1, NE * NT:NE * NT + NE]))
                cmp = e32[:, 3, :, :].rearrange("p t e -> p (t e)").rearrange("p (e t) -> p e t", t=NT)
                link(dve.tensor_tensor(cmp, n32[:, 0, :].unsqueeze(2).broadcast_to([P, NE, NT]),
                                       C("thr").unsqueeze(1).broadcast_to([P, NE, NT]), ALU.is_gt))
                link(dve.tensor_reduce(n32[:, 1, :], cmp, AX.X, ALU.add))
                link(dve.tensor_tensor_scan(n32[:, 2, :], C("zero"), n32[:, 1, :], 0.0, ALU.add, ALU.add))
                link(dve.tensor_tensor(n32[:, 3, :], n32[:, 2, :], n32[:, 1, :], ALU.subtract))
                link(dve.tensor_scalar(n32[:, 3, :], n32[:, 3, :], float(P), None, ALU.mult))
                link(dve.tensor_tensor(e32[:, 3, :, :], ps[:, 1, 0:NE * NT].rearrange("p (t e) -> p t e", e=NE),
                                       n32[:, 3, :].unsqueeze(1).broadcast_to([P, NT, NE]), ALU.add))
                for k in range(2):
                    link(dve.tensor_tensor(e32[:, k, :, :], e32[:, k, :, :], e32[:, 3, :, :], ALU.mult))
                    link(dve.tensor_reduce(r5[:, 10 + k, :], e32[:, k, :, :], AX.X, ALU.add))
                    dve.tensor_copy(dst[:, :, k], r5[:, 10 + k, :])
                big = arena[0:1, mo:mo + MAXB * NE].rearrange("p (j e) -> p j e", e=NE)
                link(dve.tensor_tensor(big, n32[0:1, 2, :].unsqueeze(1).broadcast_to([1, MAXB, NE]),
                                       C("jj", 1).unsqueeze(2).broadcast_to([1, MAXB, NE]), ALU.is_le))
                link(dve.tensor_reduce(tabf[0:1, 0:MAXB], big, AX.X, ALU.add))
                link(dve.tensor_scalar(tabf[0:1, 0:MAXB], tabf[0:1, 0:MAXB], float(NE - 1), None, ALU.min))
                link(dve.tensor_copy(tabf[0:1, MAXB:MAXB + 1], n32[0:1, 2, NE - 1:NE]))
                dve.tensor_copy(tab[0:1, 0:MAXB + 1], tabf[0:1, 0:MAXB + 1]).then_inc(r_tab, 1)

            for t in (mv, ssr, ss, cg, lg, rs, gcol):
                dve.memset(t[:], 1.0)
            dve.wait_ge(const_in, 16)
            dve.wait_ge(x_in, 32)
            dve.wait_ge(ln0_in, 32)
            for i, (_, n) in enumerate(TOK):
                norm_stats(i, n)
            norm_apply(1)
            end_layer(dve, "dve")
            with dve.Fori(0, DEPTH) as l:
                phase = Phase(dve)
                steps[0] = 0
                dve.memset(zeros, 0.0).then_inc(zero_ready, 1)
                lambdas()
                r = 0
                for u in range(NAB):
                    if UNITS[u][0] in ROPE:
                        rope(u, r)
                        r += 1
                lambda_end()
                phase()
                attention_a()
                phase()
                rms_stats()
                rms_apply()
                attention_b()
                phase()
                phase()
                dve.memset(craw[:, :, 0:1], 0.0)
                dve.memset(craw[:, :, L + 1:L + 2], 0.0)
                dve.memset(vC[:, :, :, 128:129], 1.0)
                gate_logs()
                conv(0)
                gate_logs2()
                for ch in range(1, 4):
                    conv(ch)
                gate_scans()
                for ch in range(4, 8):
                    conv(ch)
                gate_cols()
                phase()
                mlstm()
                phase()
                c_norm()
                c_out()
                dve.memset(merged[:, :, :], 0.0).then_inc(gate_free, 2)
                phase()
                with dve.Fori(0, 3) as t:
                    for u in range(8):
                        dve.wait_ge(gate_sig, t * 8 + (u + 1))
                        dve.tensor_tensor(two(tg[:, u % 2, :]), two(sg[:, u % 2, :]), halves(4 * (u % 2) + 2), ALU.mult).then_inc(gate_tmp, 1)
                        dve.wait_ge(gate_tmp, t * 8 + (u + 1))
                        dve.tensor_tensor(merged[:, u, :], merged[:, u, :], tg[:, u % 2, :], ALU.add).then_inc(gate_free, 1)
                phase()
                for i, (_, n) in enumerate(TOK):
                    for hf in range(2):
                        dve.wait_ge(y_mm, 2 * i + hf + 1)
                        o = h_tok[0:n, i, 512 * hf:512 * hf + 512]
                        dve.scalar_tensor_tensor(o, o, ALPHA, ps[0:n, (2 * i + hf) % 4, :], ALU.mult, ALU.add).then_inc(y_ev, 1)
                    dve.wait_ge(y_ev, 2 * i + 2)
                    norm_stats(i, n)
                norm_apply(1)
                router()
                phase()
                start_free(dve, "dve")
                nb = dve.value_load(tab[0:1, MAXB:MAXB + 1], min_val=9, max_val=MAXB)
                with dve.Fori(0, nb) as j:
                    dve.wait_ge(e_sil, j + 2)
                    dve.wait_ge(e_u, j + 2)
                    dve.tensor_tensor(hid, sil, ps[:, 1, :], ALU.mult).then_inc(e_hid, 1)
                    dve.wait_ge(e_ht, j + 1)
                    dve.tensor_copy(hidT[:, :, :].rearrange("p k n -> p (k n)"), ps[:, 4, :]).then_inc(e_htev, 1)
                    dve.wait_ge(ys_out, j * 16 + 16)
                    dve.wait_ge(e_dn, j + 2)
                    dve.tensor_copy(ye[:, 0:512], ps[:, 5, :]).then_inc(e_ye, 1)
                phase()
                for i, (_, n) in enumerate(TOK):
                    dve.wait_ge(gathered[i], l * 32 + 32)
                    o = h_tok[0:n, i, :]
                    y1, y2 = gath[0:n, i, 0, :], gath[0:n, i, 1, :]
                    link(dve.tensor_scalar(y1, y1, r5[0:n, 7, i:i + 1], None, ALU.mult))
                    link(dve.scalar_tensor_tensor(o, o, ALPHA, y1, ALU.mult, ALU.add))
                    link(dve.scalar_tensor_tensor(o, y2, r5[0:n, 8, i:i + 1], o, ALU.mult, ALU.add))
                    norm_stats(i, n)
                dve.wait_ge(ln2_in, 32)
                norm_apply(2)
                end_layer(dve, "dve")


def constants():
    c = np.zeros((P, NCONST), np.float32)

    def put(name, value):
        at, w = CONST[name]
        c[:, at:at + w] = value

    inv = (1.0 / (np.float32(10000.0) ** (np.arange(0, 64, 2, dtype=np.float32) / np.float32(64)))).astype(np.float32)
    ang = np.arange(L, dtype=np.float32)[None, :] * inv[np.arange(P) % 32][:, None]
    put("cos", np.cos(ang))
    put("sin", np.sin(ang))
    put("ident", np.eye(P))
    rot = np.zeros((P, P), np.float32)
    for m in range(P):
        if m % 64 < 32:
            rot[m + 32, m] = -1.0
        else:
            rot[m - 32, m] = 1.0
    put("rot", rot)
    q, k = np.arange(P)[:, None], np.arange(P)[None, :]
    prev, nxt = np.where(k >= q, 0.0, NEG), np.where(k <= q, 0.0, NEG)
    m0 = np.zeros((P, 144))
    m0[:, 16:] = np.where(k <= q + P - META, 0.0, NEG)
    put("mask0", m0)
    z16, z128 = np.zeros((P, 16)), np.zeros((P, P))
    put("mask1", np.concatenate([z16, z128, nxt], 1))
    put("mask2", np.concatenate([z16, prev, z128, nxt], 1))
    put("ltri", q < k)
    put("ones", 1.0)
    valid = np.ones((P, NT))
    valid[META:, 0] = 0.0
    put("valid", valid)
    put("wg4", 4.0 - np.arange(4))
    put("we32", float(NE) - np.arange(NE))
    put("thr", float(P) * np.arange(NT))
    put("jj", np.arange(MAXB))
    return c


def kernel(**inputs):
    import numpy as _np
    import concourse.bacc as _bacc
    from concourse import mybir as _mybir
    from concourse.bass_utils import run_bass_kernel_spmd as _run

    i = {k: _np.asarray(v) for k, v in inputs.items()}
    arrays = {n: _np.ascontiguousarray(i[n]) for n in
              ("x", "meta", "ln_in_g", "ln_in_b", "w_in", "w_branch", "w_out", "ln1_g", "ln1_b", "ln2_g", "ln2_b",
               "w_gate", "w_up", "w_down")}
    f = _np.float32
    lam_init = _np.array([0.8 - 0.6 * _np.exp(-0.3 * l) for l in range(DEPTH)], f)[:, None]
    arrays["consts"] = constants()
    arrays["rowp"] = _np.concatenate([i["gate_b"], i["b_rg"], i["b_re"], i["sink"], i["lam_q1"], i["lam_k1"],
                                      i["lam_q2"], i["lam_k2"], -lam_init, f(1) - lam_init], axis=1)
    cw = i["conv_w"].reshape(DEPTH, 3, 8, P).transpose(0, 3, 2, 1).reshape(DEPTH, P, 24)
    arrays["colp"] = _np.concatenate([cw, i["conv_b"].reshape(DEPTH, 8, P).transpose(0, 2, 1),
                                      i["mlstm_g"].reshape(DEPTH, 4, P).transpose(0, 2, 1),
                                      i["diff_g"][:, :, None]], axis=2)
    arrays["w_r"] = _np.concatenate([i["w_rg"], i["w_re"]], axis=2)
    arrays = {f"in_{n}": _np.ascontiguousarray(v) for n, v in arrays.items()}
    nc = _bacc.Bacc("TRN2", target_bir_lowering=False, num_devices=1)
    aps = {n[3:]: nc.dram_tensor(n, v.shape, _mybir.dt.from_np(v.dtype), kind="ExternalInput").ap() for n, v in arrays.items()}
    aps["out"] = nc.dram_tensor("out_h", (1, SEQ, DM), F32, kind="ExternalOutput").ap()
    program(nc, aps)
    r = _run(nc, [arrays], core_ids=[0])
    return r.results[0]["out_h"]
```

```python
from contextlib import ExitStack

import numpy as np

import concourse.bass as bass
from concourse import mybir

F32 = mybir.dt.float32
F32R = mybir.dt.float32r
I32 = mybir.dt.int32
U32 = mybir.dt.uint32
ALU = mybir.AluOpType
ACT = mybir.ActivationFunctionType
AX = mybir.AxisListType

P = 128
DM = 1024
KD = DM // P
META = 16
SEQ = 512
L = META + SEQ
HALF = L // 2
NT = 5
TOK = [(0, META)] + [(META + P * i, P) for i in range(4)]
DEPTH = 2
ALPHA = (2.0 * DEPTH) ** 0.25
EPS = 1e-5
NEG = -1e30
LOW = -3e38

DIN = 7440
COL = {"aq": 0, "ak": 512, "av": 1024, "bq": 1536, "bkv": 2048, "cq": 2304, "ck": 2816, "cv": 3328,
       "co": 3840, "cg": 4352, "gz": 4368}
QSCALE = 64 ** -0.5
MSCALE = 128 ** -0.5
NE = 32
MAXB = 40
DE = 512

CONST = {}
_at = 0
for _n, _w in (("cos", L), ("sin", L), ("ident", P), ("rot", P), ("mask0", 144), ("mask1", 272),
               ("mask2", 400), ("ltri", P), ("ones", P), ("valid", NT), ("wg4", 4), ("we32", NE),
               ("thr", NT), ("jj", MAXB), ("zero", NE)):
    CONST[_n] = (_at, _w)
    _at += _w
NCONST = _at

ROW = {"gate_b": (0, 16), "b_r": (16, 36), "sink": (52, 8), "lam": (60, 256), "neg_lam_init": (316, 1),
       "one_minus": (317, 1)}
NROW = 318
NCOLP = 24 + 8 + 4 + 1

RING = 0
SLOT = 4096
X = 3 * SLOT
Y = X + 6912
Z = Y + 3 * 4 * L
W = Z + 5392
ARENA = W + 5952
HTOK = 6 * SLOT + 6656


def program(nc, a):
    ctx = ExitStack()
    with ctx:
        def sb(name, shape, dt=F32):
            return ctx.enter_context(nc.sbuf_tensor(name, shape, dt))

        def sem(name):
            return ctx.enter_context(nc.semaphore(name))

        layer_sems = []

        def lsem(name):
            s = sem(name)
            layer_sems.append(s)
            return s

        xs = nc.dram_tensor("moe_rows", [(MAXB + 1) * P, DM], F32, kind="Internal").ap()
        h_rows = nc.dram_tensor("h_rows", [P, NT, DM], F32, kind="Internal").ap()
        mrow = nc.dram_tensor("mlstm_max_rows", [2, 8, L], F32, kind="Internal").ap()

        arena = sb("arena", [P, ARENA])
        arena_at = int(nc.sbuf_base) - 4 * ARENA
        hT_hi = sb("hT_hi", [P, KD, L], F32R)
        hT_lo = sb("hT_lo", [P, KD, L], F32R)
        hT = nc.alloc_sbuf_tensor_at("hT", [P, KD, L], F32, offset=int(nc.sbuf_base) - 8 * KD * L)
        w_hi = nc.alloc_sbuf_tensor_at("w_hi", [P, 2, KD, P], F32R, offset=arena_at + 4 * 2 * SLOT)
        w_lo = nc.alloc_sbuf_tensor_at("w_lo", [P, 2, KD, P], F32R, offset=arena_at + 4 * (2 * SLOT + 2 * KD * P))
        cst = sb("cst", [P, NCONST])
        lngb = sb("lngb", [P, 2, DM])
        rowp = sb("rowp", [P, NROW])
        colp = sb("colp", [P, NCOLP])
        w_r = sb("w_r", [P, KD, 36])
        bn = sb("bn", [P, NT, 48])
        mv = sb("mv", [P, NT, 2])
        rstd = sb("rstd", [P, NT])
        st = sb("st", [P, 64])
        rs = sb("rs", [P, 2, NT, 8])
        ss = sb("ss", [P, NT, 4, 2])
        ssr = sb("ssr", [P, NT, 4])
        cg = sb("cg", [P, 2, NT, 16])
        gcol = sb("gcol", [P, NT, 32])
        r4 = cg[:, :, :, :].rearrange("p a b c -> p (a b c)")[:, 0:3 * NT * 4].rearrange("p (a b c) -> p a b c", b=NT, c=4)
        lg = sb("lg", [P, NT, 36])
        r5 = sb("r5", [P, 12, NT])
        e32 = sb("e32", [P, 4, NT, NE])
        zeros = e32[:, :, :, :].rearrange("p a b c -> p (a b c)")[:, 0:512]
        n32 = sb("n32", [P, 4, NE])
        dst = sb("dst", [P, NT, 2], U32)
        tab = sb("tab", [1, 3 * MAXB + 2], I32)

        ps = ctx.enter_context(nc.psum_tensor("ps", [P, 8, 512], F32))

        def C(name, rows=P, w=None):
            at, width = CONST[name]
            return cst[0:rows, at:at + (width if w is None else w)]

        def R(name):
            at, width = ROW[name]
            return rowp[:, at:at + width]

        def v(at, *dims):
            n = int(np.prod(dims))
            f = arena[:, at:at + n]
            if len(dims) == 2:
                return f.rearrange("p (a b) -> p a b", b=dims[1])
            if len(dims) == 3:
                return f.rearrange("p (a b c) -> p a b c", b=dims[1], c=dims[2])
            return f

        ident = C("ident")
        slot = [v(RING + SLOT * i, KD, 512) for i in range(2)]
        h_tok = v(HTOK, NT, DM)
        qA, kA, vA = v(X, 4, L), [v(X + 4 * L, 4, L), v(Y + 8 * L, 4, L)], v(X + 8 * L, NT, 512)
        qC, kC, vC = qA, kA[0], v(X + 8 * L, NT, 4, 129)
        merged = v(X, KD, L)
        outT = v(Y, 3, 4, L)
        mb = v(Y + 8 * L, 2, 2, L)
        qB, kB, vB = v(Z, 4, L), [v(Z + 4 * L, 1, L), v(Z + 3280, 1, L)], v(Z + 5 * L, NT, 128)
        sco = v(Z + 3280, 4, L)
        raw = v(W + 4 * L + 4, 2, L)
        t_sin = v(W + 2 * L, 2, L)
        pA = v(W, 2, 2, L)
        ptA = v(W + 4 * L, 2, 4, P)
        ptm = v(W + 4 * L + 1024, 2, P)
        oA = v(W + 4 * L + 1024 + 256, NT, 512)
        sB = v(W, 3, 400)
        oB = v(X, NT, 512)
        sq = v(W, 2, 512)
        craw = v(W, 2, L + 2)
        ctmp = v(W + 2 * (L + 2), 2, L)
        SAT = [[0], [0]]
        for j in range(NT):
            SAT[0].append(SAT[0][-1] + L - TOK[j][0])
        SAT[1][0] = SAT[0][-1]
        for j in range(NT):
            SAT[1].append(SAT[1][-1] + sum(TOK[j]))
        NS = SAT[1][-1]
        sC = [v(W, NS), v(Z, NS)]
        hsum = v(W + NS, NT, 512)
        ROWS = [v(Z + L * i, L) for i in range(6)] + [v(W + 3172 + L * i, L) for i in range(5)]
        LF, LI, ZR, BF, BB, UF, UB, MF, MB, EF, EB = [r[0:8, :] for r in ROWS]
        wbw = [v(X + KD * L, 4, 512), v(Z + 4 * L, 4, 512)]
        sg = v(Z, 2, L)
        tg = v(Z + 2 * L, 2, L)
        yraw = v(Z + 4 * L + 2048, 2, L)
        WSET = 3 * SLOT
        mo = 2 * WSET
        assert mo + 6656 <= HTOK and HTOK + NT * DM <= ARENA and NS <= 3280
        xe = v(mo, DM)
        xeT = v(mo + 1024, KD, P)
        sil = v(mo + 2048, DE)
        hid = v(mo + 2560, DE)
        hidT = v(mo + 3072, 4, P)
        ye = v(mo + 3584, DM)
        gath = v(2 * SLOT + 4096, NT, 2, DM)
        tabf = arena[:, mo + MAXB * NE:mo + MAXB * NE + 128]

        const_in = sem("const_in")
        x_in = sem("x_in")
        xs_zeroed = sem("xs_zeroed")
        ln0_in = sem("ln0_in")
        out_done = sem("out_done")
        scattered = sem("scattered")
        gathered = [sem(f"gathered{i}") for i in range(NT)]
        arrived = sem("arrived")
        go = {e: sem(f"go_{e}") for e in ("pe", "act", "dve", "pool")}

        zero_ready = lsem("zero_ready")
        phase_done = lsem("phase_done")
        dve_step = lsem("dve_step")
        act_step = lsem("act_step")
        first_in = [sem(f"first_in{i}") for i in range(2)]
        h_saved = sem("h_saved")
        h_back = lsem("h_back")
        k_zeroed = lsem("k_zeroed")
        slot_in = [lsem(f"slot_in{i}") for i in range(2)]
        w_split_hi, w_split_lo = lsem("w_split_hi"), lsem("w_split_lo")
        m_split_hi, m_split_lo = lsem("m_split_hi"), lsem("m_split_lo")
        par_in = lsem("par_in")
        ln2_in = lsem("ln2_in")
        unit_mm = lsem("unit_mm")
        unit_ev = lsem("unit_ev")
        rot_mm = lsem("rot_mm")
        rot_ev = lsem("rot_ev")
        conv_done = lsem("conv_done")
        silu_done = lsem("silu_done")
        a_s, a_m, a_exp, a_comb, a_t, a_tev, a_tmev, a_o, a_oev = [lsem(f"a_{n}") for n in
            ("s", "m", "exp", "comb", "t", "tev", "tmev", "o", "oev")]
        b_s, b_m, b_exp, b_t, b_tev, b_tmev, b_o, b_snk, b_oev = [lsem(f"b_{n}") for n in
            ("s", "m", "exp", "t", "tev", "tmev", "o", "snk", "oev")]
        g_lf, g_exp, g_ln, g_t, g_rows, g_e, g_t2, g_col = [lsem(f"g_{n}") for n in
            ("lf", "exp", "ln", "t", "rows", "e", "t2", "col")]
        m_out = lsem("m_out")
        m_in = [lsem(f"m_in{i}") for i in range(2)]
        c_qk, c_w, c_mul, c_sel, c_pv, c_post, c_mbused = [lsem(f"c_{n}") for n in
            ("qk", "w", "mul", "sel", "pv", "post", "mbused")]
        n_ready, n_sqrt, n_norm, n_t, n_ev = [lsem(f"n_{n}") for n in ("ready", "sqrt", "norm", "t", "ev")]
        wb_in = [lsem(f"wb_in{i}") for i in range(2)]
        wb_used, gate_mm, gate_sig, gate_tmp, gate_free = [lsem(f"gate_{n}") for n in
            ("wb_used", "mm", "sig", "tmp", "free")]
        y_mm, y_ev, y_t, y_add = [lsem(f"y_{n}") for n in ("mm", "ev", "t", "add")]
        r_mm, r_dst, r_exp, r_exp2, r_cnt, r_rank, r_tab, r_a, r_b = [lsem(f"r_{n}") for n in
            ("mm", "dst", "exp", "exp2", "cnt", "rank", "tab", "a", "b")]
        rows_back = lsem("rows_back")
        wg_in, wu_in, wd_in, xe_in, ys_out = [lsem(f"moe_{n}") for n in ("wg_in", "wu_in", "wd_in", "xe_in", "ys_out")]
        e_xt, e_xtev, e_g, e_u, e_sil, e_hid, e_ht, e_htev, e_dn, e_ye = [lsem(f"e_{n}") for n in
            ("xt", "xtev", "g", "u", "sil", "hid", "ht", "htev", "dn", "ye")]
        FREE = {"pe": [(e_g, 1), (e_u, 1), (e_dn, 1)], "act": [(e_sil, 1)], "dve": [(e_hid, 1), (e_ye, 2)],
                "sp": [(ys_out, 16)]}

        def start_free(eng, who):
            for s, n in FREE[who]:
                eng.sem_inc(s, n)

        l_var, l_sqrt, l_mul, l_add, l_t, l_ev, l_lo = [lsem(f"l_{n}") for n in ("var", "sqrt", "mul", "add", "t", "ev", "lo")]

        UNITS = [(kind, c) for kind, n in (("aq", 4), ("ak", 4), ("av", 4), ("bq", 4), ("bk", 1), ("bv", 1)) for c in range(n)]
        NAB = len(UNITS)
        UNITS += [(kind, c) for kind, n in (("cg", 1), ("cq", 4), ("ck", 4), ("cv", 4), ("co", 4)) for c in range(n)]
        NU = len(UNITS)
        NG = 3 * KD
        WBLOCK = {"aq": 0, "ak": 1, "av": 2, "bq": 3, "bk": 4, "bv": 4, "cg": 4, "cq": 5, "ck": 6, "cv": 7, "co": 8}
        WAT = {"bk": 0, "bv": 1, "cg": 2}
        FIRST = [min(u for u, (k, _) in enumerate(UNITS) if WBLOCK[k] == b) for b in range(9)] + [NU, NU + 4]
        ROPE = {"aq": qA, "ak": kA, "bq": qB, "bk": kB}
        TURN = ("av", "bv", "cv", "cg")
        POST = {}
        for _u, (_k, _) in enumerate(UNITS):
            if _k in ROPE or _k in TURN:
                POST[_u] = len(POST)
        IN = {}
        _n = [0, 0]
        for _b in range(2, 9):
            _n[_b % 2] += 32 if _b == 4 else 16
            IN[_b] = _n[_b % 2]
        IN_GZ = [_n[1], _n[0]]

        def chunk_source(q):
            if q < NU:
                kind, c = UNITS[q]
                w = slot[WBLOCK[kind] % 2]
                if kind == "bq":
                    return w.rearrange("p k (g c d) -> p k g c d", g=2, d=64)[:, :, :, c, :]
                c = WAT.get(kind, c)
            else:
                w, c = slot[(1 + (q - NU) // 4) % 2], (q - NU) % 4
            return w[:, :, P * c:P * c + P].rearrange("p k (g d) -> p k g d", d=64)

        def chunk_split(t, q):
            return t[:, q % 2, :, :].rearrange("p k (g d) -> p k g d", d=64)

        def as_f32(t):
            return t.bitcast(F32)

        def halves(bank, rows=P):
            return ps[0:rows, bank:bank + 2, 0:HALF]

        def two(apx):
            return apx.rearrange("p (a b) -> p a b", b=HALF)

        class Phase:

            def __init__(self, eng):
                self.eng, self.n = eng, 0

            def __call__(self):
                self.n += 1
                self.eng.drain().then_inc(phase_done, 1)
                self.eng.wait_ge(phase_done, 3 * self.n)

        def end_layer(eng, who):
            eng.drain().then_inc(arrived, 1)
            eng.wait_ge(go[who], 1)
            eng.sem_clear(go[who])

        def next_layer(sp):
            sp.wait_ge(arrived, 4)
            for s in layer_sems:
                sp.sem_clear(s)
            sp.sem_clear(arrived)
            for g in go.values():
                sp.sem_inc(g, 1)

        BKEYS = [[(0, 16), (16, 128)], [(0, 272)], [(0, 400)], [(0, 16), (144, 384)], [(0, 16), (272, 256)]]
        BTILES = [[1], [1, 2], [1, 2, 3], [2, 3, 4], [3, 4]]
        BHEAD = [0, 4, 1, 5, 2, 6, 3, 7]
        BMASK = ["mask0", "mask1", "mask2", "mask2", "mask2"]
        bwidth = [sum(n for _, n in k) for k in BKEYS]

        block = ctx.enter_context(nc.Block())

        @block.sync
        def _(sp):
            sp.dma_start(cst[:, :], a["consts"]).then_inc(const_in, 16)
            sp.dma_start(h_tok[0:META, 0, :], a["meta"]).then_inc(x_in, 16)
            sp.dma_start(h_tok[:, 1:NT, :], a["x"][0].rearrange("(i p) n -> p i n", p=P)).then_inc(x_in, 16)
            sp.dma_start(lngb[:, 0, :], a["ln_in_g"].partition_broadcast(P)).then_inc(ln0_in, 16)
            sp.dma_start(lngb[:, 1, :], a["ln_in_b"].partition_broadcast(P)).then_inc(ln0_in, 16)

            def first_blocks(l):
                for i, kind in enumerate(("aq", "ak")):
                    sp.dma_start(slot[i][:, :, :], a["w_in"][bass.ds(l, 1)].rearrange("o (k p) n -> (o p) k n", p=P)
                                 [:, :, COL[kind]:COL[kind] + 512]).then_inc(first_in[i], 16)

            def save_rows(norms):
                sp.wait_ge(l_add, norms * NT)
                sp.dma_start(h_rows[0:META, 0, :], h_tok[0:META, 0, :]).then_inc(h_saved, 16)
                sp.dma_start(h_rows[:, 1:NT, :], h_tok[:, 1:NT, :]).then_inc(h_saved, 16)

            first_blocks(0)
            save_rows(1)
            next_layer(sp)
            with sp.Fori(0, DEPTH) as l:
                def lay(t, pat, **kw):
                    return t[bass.ds(l, 1)].rearrange("o " + pat, **kw)

                sp.dma_start(rowp[:, :], a["rowp"][bass.ds(l, 1), :].broadcast_to([P, NROW])).then_inc(par_in, 16)
                sp.dma_start(colp[:, :], lay(a["colp"], "p n -> (o p) n")).then_inc(par_in, 16)
                sp.dma_start(w_r[:, :, :], lay(a["w_r"], "(k p) n -> (o p) k n", p=P)).then_inc(par_in, 16)
                for i, n in enumerate(("ln1_g", "ln1_b")):
                    sp.dma_start(lngb[:, i, :], a[n][bass.ds(l, 1), :].broadcast_to([P, DM])).then_inc(par_in, 16)

                def w_cols(at, n):
                    return lay(a["w_in"], "(k p) n -> (o p) k n", p=P)[:, :, at:at + n]

                for n, kind in enumerate(("aq", "ak", "av", "bq", "bkv", "cq", "ck", "cv", "co")):
                    if n < 2:
                        continue
                    sp.wait_ge(w_split_lo, FIRST[n - 1])
                    if kind == "bkv":
                        sp.dma_start(slot[n % 2][:, :, 0:256], w_cols(COL["bkv"], 256)).then_inc(slot_in[n % 2], 16)
                        sp.dma_start(slot[n % 2][:, :, 256:384], w_cols(COL["cg"], P)).then_inc(slot_in[n % 2], 16)
                    else:
                        sp.dma_start(slot[n % 2][:, :, :], w_cols(COL[kind], 512)).then_inc(slot_in[n % 2], 16)
                    if n != 5:
                        continue
                    with sp.If(l < 1):
                        sp.wait_ge(zero_ready, 1)
                        for hf in range(2):
                            sp.dma_start(xs.rearrange("(b p) n -> p b n", p=P)[:, :, 512 * hf:512 * hf + 512],
                                         zeros.unsqueeze(1).broadcast_to([P, MAXB + 1, 512])).then_inc(xs_zeroed, 16)

                def load_gz(t, hf):
                    sp.wait_ge(w_split_lo, t * 8 + (FIRST[8] + 4 * hf))
                    sp.dma_start(slot[1 - hf][:, :, :],
                                 lay(a["w_in"], "(k p) n -> (o p) k n", p=P)[:, :, bass.ds(t * 1024 + (COL["gz"] + 512 * hf), 512)]
                                 ).then_inc(slot_in[1 - hf], 16)

                def load_wb(t, hf):
                    wb = a["w_branch"].rearrange("l b (k p) n -> (l b) p k n", p=P)
                    sp.dma_start(wbw[hf][:, :, :],
                                 wb[bass.ds(l * 3 + t, 1), :, :, 512 * hf:512 * hf + 512].rearrange("o p k n -> (o p) k n")
                                 ).then_inc(wb_in[hf], 16)

                def load_max(h):
                    for d in range(2):
                        sp.dma_start(mb[:, h % 2, d, :],
                                     mrow[d, 4 * d + h:4 * d + h + 1, :].broadcast_to([P, L])).then_inc(m_in[h % 2], 16)

                load_gz(0, 0)
                sp.wait_ge(g_rows, 1)
                sp.dma_start(mrow[0], MF).then_inc(m_out, 16)
                sp.dma_start(mrow[1], MB).then_inc(m_out, 16)
                sp.wait_ge(m_out, 32)
                load_max(0)
                load_max(1)
                load_gz(0, 1)
                for h in (2, 3):
                    sp.wait_ge(c_mbused, h - 1)
                    load_max(h)
                sp.wait_ge(c_pv, 4 * NT)
                load_wb(0, 0)
                sp.wait_ge(n_ev, 3 * NT)
                load_wb(0, 1)
                sp.dma_start(h_tok[0:META, 0, :], h_rows[0:META, 0, :]).then_inc(h_back, 16)
                sp.dma_start(h_tok[:, 1:NT, :], h_rows[:, 1:NT, :]).then_inc(h_back, 16)
                with sp.Fori(1, 3) as t:
                    for hf in range(2):
                        load_gz(t, hf)
                        sp.wait_ge(wb_used, t * 2 + (hf - 1))
                        load_wb(t, hf)
                wo = lay(a["w_out"], "(k p) n -> (o p) k n", p=P)
                for hf in range(2):
                    sp.wait_ge(w_split_lo, NU + NG - 4 + 4 * hf)
                    sp.dma_start(slot[1 - hf][:, :, :], wo[:, :, 512 * hf:512 * hf + 512]).then_inc(slot_in[1 - hf], 16)

                sp.wait_ge(l_add, NT)
                sp.wait_ge(l_mul, NT)
                for i, n in enumerate(("ln2_g", "ln2_b")):
                    sp.dma_start(lngb[:, i, :], a[n][bass.ds(l, 1), :].broadcast_to([P, DM])).then_inc(ln2_in, 16)

                start_free(sp, "sp")
                sp.wait_ge(r_tab, 1)
                nb = sp.value_load(tab[0:1, MAXB:MAXB + 1], min_val=9, max_val=MAXB)
                wg3 = a["w_gate"].rearrange("l e (k p) n -> (l e) p k n", p=P)
                wu3 = a["w_up"].rearrange("l e (k p) n -> (l e) p k n", p=P)
                wd3 = a["w_down"].rearrange("l e (k p) n -> (l e) p k n", p=P)

                def load_rows(j):
                    sp.dma_start(xe, xs[bass.ds(j * P, P), :]).then_inc(xe_in, 16)

                def load_w(o, part, e, source, done):
                    sp.dma_start(arena[:, bass.ds((o % 2) * WSET + part * SLOT, SLOT)].rearrange("p (k n) -> p k n", n=(DE, DE, DM)[part]),
                                 source[bass.ds(e, 1)].rearrange("o p k n -> (o p) k n")).then_inc(done, 16)

                def store_rows(j):
                    sp.dma_start(xs[bass.ds(j * P, P), :], ye).then_inc(ys_out, 16)

                e0 = l * NE + sp.value_load(tab[0:1, 0:1], min_val=0, max_val=NE - 1)
                for part, (source, done) in enumerate(((wg3, wg_in), (wu3, wu_in), (wd3, wd_in))):
                    sp.dma_start(arena[:, part * SLOT:(part + 1) * SLOT].rearrange("p (k n) -> p k n", n=(DE, DE, DM)[part]),
                                 source[bass.ds(e0, 1)].rearrange("o p k n -> (o p) k n")).then_inc(done, 16)
                sp.wait_ge(scattered, l * 160 + 160)
                sp.dma_start(xe, xs[0:P, :]).then_inc(xe_in, 16)

                def load_block(i):
                    sp.wait_ge(e_xt, i + 1)
                    load_rows(i + 1)
                    first = sp.value_load(tab[0:1, bass.ds(i + (2 * MAXB + 2), 1)], min_val=0, max_val=1)
                    with sp.If(first > 0):
                        e = l * NE + sp.value_load(tab[0:1, bass.ds(i + 1, 1)], min_val=0, max_val=NE - 1)
                        o = sp.value_load(tab[0:1, bass.ds(i + (MAXB + 2), 1)], min_val=1, max_val=NE - 1)
                        sp.wait_ge(wg_in, o * 16)
                        sp.wait_ge(e_g, i + 1)
                        load_w(o, 0, e, wg3, wg_in)
                        sp.wait_ge(wu_in, o * 16)
                        sp.wait_ge(e_u, i + 1)
                        load_w(o, 1, e, wu3, wu_in)
                        sp.wait_ge(wd_in, o * 16)
                        sp.wait_ge(e_dn, i + 1)
                        load_w(o, 2, e, wd3, wd_in)

                load_block(0)
                with sp.Fori(1, nb - 1) as i:
                    load_block(i)
                    sp.wait_ge(e_ye, i * 2 + 2)
                    store_rows(i - 1)
                sp.wait_ge(e_xt, nb)
                load_rows(nb)
                sp.wait_ge(e_ye, nb * 2)
                store_rows(nb - 2)
                sp.wait_ge(e_ye, nb * 2 + 2)
                store_rows(nb - 1)
                sp.wait_ge(ys_out, nb * 16 + 16)
                sp.sem_inc(rows_back, 1)
                with sp.If(l < DEPTH - 1):
                    sp.wait_ge(gathered[NT - 1], l * 32 + 32)
                    first_blocks(nc.s_assert_within(l + 1, min_val=1, max_val=DEPTH - 1,
                        skip_runtime_bounds_check_because="this branch runs only where l < DEPTH - 1"))
                save_rows(2)
                next_layer(sp)
            sp.dma_start(a["out"][0].rearrange("(i p) n -> p i n", p=P), h_tok[:, 1:NT, :]).then_inc(out_done, 16)
            sp.wait_ge(h_saved, 32 * (DEPTH + 1))
            sp.wait_ge(out_done, 16)

        @block.gpsimd
        def _(pool):
            def norm_bias():
                for i, (_, n) in enumerate(TOK):
                    pool.wait_ge(l_mul, i + 1)
                    pool.tensor_tensor(h_tok[0:n, i, :], h_tok[0:n, i, :], lngb[0:n, 1, :], ALU.add).then_inc(l_add, 1)

            pool.wait_ge(ln0_in, 32)
            norm_bias()
            end_layer(pool, "pool")
            with pool.Fori(0, DEPTH) as l:
                for keys in (kA, kB):
                    for g in range(2):
                        half = slice(64 - 64 * g, 128 - 64 * g)
                        pool.memset(keys[g][half, :, :], 0.0)
                pool.drain().then_inc(k_zeroed, 1)
                pool.wait_ge(par_in, 80)
                for h in range(4):
                    for j, (t0, n) in enumerate(TOK):
                        for d in range(2):
                            pool.wait_ge(c_mul, 2 * (NT * h + j) + d + 1)
                            at = SAT[d][j] + (0 if d == 0 else t0)
                            blk = sC[h % 2][0:n, at:at + n]
                            sgn = 1 if d == 0 else -1
                            pool.affine_select(out=blk, in_=blk, compare_op=ALU.is_ge, fill=0.0, base=0,
                                               pattern=[[sgn, n]], channel_multiplier=-sgn).then_inc(c_sel, 1)
                pool.wait_ge(par_in, 80)
                for i, (_, n) in enumerate(TOK):
                    pool.wait_ge(l_mul, i + 1)
                    pool.tensor_tensor(h_tok[0:n, i, :], h_tok[0:n, i, :], lngb[0:n, 1, :], ALU.add).then_inc(l_add, 1)
                pool.wait_ge(xs_zeroed, 32)
                pool.wait_ge(l_add, NT)
                pool.wait_ge(r_dst, 1)
                for i, (_, n) in enumerate(TOK):
                    for k in range(2):
                        pool.indirect_dma_start(
                            out=xs, out_offset=bass.IndirectOffsetOnAxis(ap=dst[0:n, i, k:k + 1], axis=0),
                            in_=h_tok[0:n, i, :], in_offset=None).then_inc(scattered, 16)
                pool.wait_ge(rows_back, 1)
                pool.wait_ge(phase_done, 3 * 10)
                for i, (_, n) in enumerate(TOK):
                    for k in range(2):
                        pool.indirect_dma_start(
                            out=gath[0:n, i, k, :], out_offset=None, in_=xs,
                            in_offset=bass.IndirectOffsetOnAxis(ap=dst[0:n, i, k:k + 1], axis=0)).then_inc(gathered[i], 16)
                pool.wait_ge(ln2_in, 32)
                for i, (_, n) in enumerate(TOK):
                    pool.wait_ge(l_mul, NT + i + 1)
                    pool.tensor_tensor(h_tok[0:n, i, :], h_tok[0:n, i, :], lngb[0:n, 1, :], ALU.add).then_inc(l_add, 1)
                end_layer(pool, "pool")

        @block.tensor
        def _(pe):
            def norm_transposes(first, split):
                for i, (t0, n) in enumerate(TOK):
                    pe.wait_ge(l_add, first + i + 1)
                    if i >= 2:
                        pe.wait_ge(l_lo if split else l_ev, i - 1)
                    for k in range(KD):
                        mm = pe.transpose(ps[:, 4 + 2 * (i % 2) + k // 4, P * (k % 4):P * (k % 4) + n],
                                          h_tok[0:n, i, P * k:P * k + P], ident[0:n, 0:n])
                    mm.then_inc(l_t, 1)

            def product(bank, q, before=None):
                for k in range(KD):
                    if before:
                        before(k)
                    for x, (w, h) in enumerate(((w_hi, hT_hi), (w_hi, hT_lo), (w_lo, hT_hi))):
                        for b in range(2):
                            mm = pe.matmul(ps[:, bank + b, 0:HALF], w[:, q % 2, k, :], h[:, k, HALF * b:HALF * b + HALF],
                                           start=(k == 0 and x == 0), stop=(k == KD - 1 and x == 2))
                mm.then_inc(unit_mm, 1)

            def unit(u):
                if u >= 2:
                    pe.wait_ge(unit_ev, u - 1)
                pe.wait_ge(w_split_lo, u + 1)
                product(2 * (u % 2), u)

            def turn_rows(bank, src, rows=P):
                for j in range(1, NT):
                    t0 = TOK[j][0]
                    pe.transpose(ps[:, bank, P * (j - 1):P * (j - 1) + rows], src[0:rows, t0:t0 + P], ident[0:rows, 0:rows])
                return pe.transpose(ps[0:META, bank + 1, 0:rows], src[0:rows, 0:META], ident[0:rows, 0:rows])

            def post(u):
                r = POST[u]
                bank = 4 + 2 * (r % 2)
                pe.wait_ge(unit_ev, u + 1)
                if r >= 2:
                    pe.wait_ge(rot_ev, r - 1)
                if UNITS[u][0] in ROPE:
                    for b in range(2):
                        mm = pe.matmul(ps[:, bank + b, 0:HALF], C("rot"), raw[:, r % 2, HALF * b:HALF * b + HALF],
                                       start=True, stop=True)
                else:
                    mm = turn_rows(bank, raw[:, r % 2, :], META if UNITS[u][0] == "cg" else P)
                mm.then_inc(rot_mm, 1)

            def units(lo, hi, extra):
                for u in range(lo, hi):
                    unit(u)
                    if u - 1 in POST and u - 1 >= lo:
                        post(u - 1)
                    if u in extra:
                        extra[u]()
                if hi - 1 in POST:
                    post(hi - 1)

            def attention_a():
                def scores(n):
                    i, h = n // 4, n % 4
                    t0, m = TOK[i]
                    if n >= 1:
                        pe.wait_ge(a_exp, 2 * n)
                    for hf in range(2):
                        for c in range(2):
                            mm = pe.matmul(ps[0:m, 3 + 2 * c + hf, 0:HALF], qA[:, h, t0:t0 + m],
                                           kA[c][:, h, HALF * hf:HALF * hf + HALF], start=True, stop=True)
                            if hf == 1:
                                mm.then_inc(a_s, 1)

                def turn(n):
                    m = TOK[n // 4][1]
                    pe.wait_ge(a_comb, n + 1)
                    if n >= 2:
                        pe.wait_ge(a_tev, n - 1)
                    if n >= 1:
                        pe.wait_ge(a_tmev, n)
                    prob = pA[0:m, n % 2, 0, :]
                    for j in range(1, NT):
                        pe.transpose(ps[:, (7, 1)[n % 2], P * (j - 1):P * (j - 1) + m],
                                     prob[:, TOK[j][0]:TOK[j][0] + P], ident[0:m, 0:m])
                    pe.transpose(ps[0:META, 0, 0:m], prob[:, 0:META], ident[0:m, 0:m]).then_inc(a_t, 1)

                def values(n):
                    i, h = n // 4, n % 4
                    m = TOK[i][1]
                    pe.wait_ge(a_tev, n + 1)
                    pe.wait_ge(a_tmev, n + 1)
                    if h == 0 and i >= 1:
                        pe.wait_ge(a_oev, i)
                    o = ps[0:m, 2, P * h:P * h + P]
                    for j in range(1, NT):
                        pe.matmul(o, ptA[:, n % 2, j - 1, 0:m], vA[:, j, P * h:P * h + P], start=(j == 1), stop=False)
                    pe.matmul(o, ptm[0:META, n % 2, 0:m], vA[0:META, 0, P * h:P * h + P],
                              start=False, stop=True).then_inc(a_o, 1)

                scores(0)
                for n in range(4 * NT):
                    if n + 1 < 4 * NT:
                        scores(n + 1)
                    turn(n)
                    if n >= 1:
                        values(n - 1)
                values(4 * NT - 1)

            def attention_b():
                def scores(n):
                    i = n // 8
                    t0, m = TOK[i]
                    c = BHEAD[n % 8]
                    if n >= 4:
                        pe.wait_ge(b_m, n - 2)
                    at = 0
                    for k0, w in BKEYS[i]:
                        for g in range(2):
                            mm = pe.matmul(ps[0:m, 3 + (n + g) % 4, at:at + w], qB[:, c, t0:t0 + m],
                                           kB[g][:, 0, k0:k0 + w], start=True, stop=True)
                            if (k0, w) == BKEYS[i][-1]:
                                mm.then_inc(b_s, 1)
                        at += w

                def turn(n):
                    i = n // 8
                    m = TOK[i][1]
                    pe.wait_ge(b_exp, n + 1)
                    if n >= 2:
                        pe.wait_ge(b_tev, n - 1)
                    if n >= 1:
                        pe.wait_ge(b_tmev, n)
                    for x, j in enumerate(BTILES[i]):
                        pe.transpose(ps[:, (7, 1)[n % 2], P * x:P * x + m],
                                     sB[0:m, n % 3, META + P * x:META + P * x + P], ident[0:m, 0:m])
                    pe.transpose(ps[0:META, 0, 0:m], sB[0:m, n % 3, 0:META], ident[0:m, 0:m]).then_inc(b_t, 1)

                def values(n):
                    i, h = n // 8, BHEAD[n % 8]
                    m, g = TOK[i][1], h // 4
                    pe.wait_ge(b_tev, n + 1)
                    pe.wait_ge(b_tmev, n + 1)
                    if n % 8 == 0 and i >= 1:
                        pe.wait_ge(b_oev, i)
                    o = ps[0:m, 2, 64 * h:64 * h + 64]
                    for x, j in enumerate(BTILES[i]):
                        pe.matmul(o, ptA[:, n % 2, x, 0:m], vB[:, j, 64 * g:64 * g + 64], start=(x == 0), stop=False)
                    pe.matmul(o, ptm[0:META, n % 2, 0:m], vB[0:META, 0, 64 * g:64 * g + 64],
                              start=False, stop=True).then_inc(b_o, 1)

                N = 8 * NT
                scores(0)
                for n in range(N):
                    if n % 2 == 0 and n + 2 < N:
                        scores(n + 2)
                    turn(n)
                    if n >= 1:
                        values(n - 1)
                values(N - 1)

            def branch_transposes(src, first, want):
                for i, (_, n) in enumerate(TOK):
                    want(i)
                    q = first + i
                    if q >= 4:
                        pe.wait_ge(n_ev, q - 3)
                    for c in range(4):
                        mm = pe.transpose(ps[:, 4 + q % 4, P * c:P * c + n], src[0:n, i, P * c:P * c + P], ident[0:n, 0:n])
                    mm.then_inc(n_t, 1)

            def gate_rows():
                pe.wait_ge(g_lf, 1)
                for i, (t0, n) in enumerate(TOK):
                    for kind in range(2):
                        bank, at = (4 + 2 * kind, t0) if i < 4 else (5 + 2 * kind, 0)
                        mm = pe.transpose(ps[0:8, bank, at:at + n], cg[0:n, 1, i, 8 * kind:8 * kind + 8], ident[0:n, 0:n])
                mm.then_inc(g_t, 1)

            def gate_columns():
                pe.wait_ge(g_e, 1)
                pe.wait_ge(g_rows, 1)
                for i, (t0, n) in enumerate(TOK):
                    for x, row in enumerate((UF, UB, EF, EB)):
                        mm = pe.transpose(ps[0:n, 4, 32 * i + 8 * x:32 * i + 8 * x + 8], row[:, t0:t0 + n], ident[0:8, 0:8])
                mm.then_inc(g_t2, 1)

            QKB = (0, 3)

            def mlstm():
                def qk(h, j):
                    q = NT * h + j
                    t0, n = TOK[j]
                    if q >= 2:
                        pe.wait_ge(c_mul, 2 * (q - 1))
                    b = QKB[q % 2]
                    pe.matmul(ps[0:n, b, 0:272], kC[:, h, t0:t0 + n], qC[:, h, 0:272], start=True, stop=True)
                    pe.matmul(ps[0:n, b + 1, 0:256], kC[:, h, t0:t0 + n], qC[:, h, 272:L],
                              start=True, stop=True).then_inc(c_qk, 1)

                def values(h, i):
                    q = NT * h + i
                    t0, m = TOK[i]
                    if i == 0:
                        pe.wait_ge(c_sel, 2 * NT * (h + 1))
                    if q >= 2:
                        pe.wait_ge(c_post, q - 1)
                    bank = 5 + q % 2
                    for d, js in enumerate((range(i + 1), range(i, NT))):
                        for x, j in enumerate(js):
                            n = TOK[j][1]
                            at = SAT[d][j] + t0 - (TOK[j][0] if d == 0 else 0)
                            mm = pe.matmul(ps[0:m, bank, 256 * d:256 * d + 129], sC[h % 2][0:n, at:at + m],
                                           vC[0:n, j, h, :], start=(x == 0), stop=(x == len(js) - 1))
                    mm.then_inc(c_pv, 1)

                for h in range(5):
                    for j in range(NT):
                        if h < 4:
                            qk(h, j)
                        if h >= 1:
                            values(h - 1, j)

            def gates():
                with pe.Fori(0, 3) as t:
                    for hf in range(2):
                        for c in range(4):
                            u = 4 * hf + c
                            s = 4 * (u % 2)
                            pe.wait_ge(gate_free, t * 8 + (u + 1))
                            pe.wait_ge(w_split_lo, t * 8 + (NU + u + 1))
                            product(s, NU + u)
                            if c == 0:
                                pe.wait_ge(wb_in[hf], t * 16 + 16)
                            for b in range(2):
                                for k in range(4):
                                    mm = pe.matmul(ps[:, s + 2 + b, 0:HALF], wbw[hf][:, k, P * c:P * c + P],
                                                   arena[:, bass.ds(t * (4 * L) + (Y + k * L + HALF * b), HALF)],
                                                   start=(k == 0), stop=(k == 3))
                            mm.then_inc(gate_mm, 1)
                        pe.drain().then_inc(wb_used, 1)

            def project_out():
                def turn(m):
                    pe.wait_ge(y_ev, m + 1)
                    if m >= 2:
                        pe.wait_ge(y_add, m - 1)
                    turn_rows(4 + 2 * (m % 2), yraw[:, m % 2, :]).then_inc(y_t, 1)

                for m in range(KD):
                    if m >= 2:
                        pe.wait_ge(y_ev, m - 1)
                    pe.wait_ge(w_split_lo, NU + NG + m + 1)
                    product(2 * (m % 2), NU + NG + m, (lambda k: pe.wait_ge(m_split_lo, k + 1)) if m == 0 else None)
                    if m >= 1:
                        turn(m - 1)
                turn(KD - 1)

            def router():
                pe.wait_ge(l_ev, NT)
                for i, (t0, n) in enumerate(TOK):
                    for k in range(KD):
                        mm = pe.matmul(ps[0:n, 0, 36 * i:36 * i + 36], hT[:, k, t0:t0 + n], w_r[:, k, :],
                                       start=(k == 0), stop=(k == KD - 1))
                mm.then_inc(r_mm, 1)
                pe.wait_ge(r_cnt, 1)
                for i in range(NT + 1):
                    for j in range(min(i + 1, NT)):
                        whole = j < i
                        mm = pe.matmul(ps[:, 1, NE * i:NE * i + NE], C("ones") if whole else C("ltri"), e32[:, 2, j, :],
                                       start=(j == 0), stop=(j == min(i, NT - 1)))
                mm.then_inc(r_rank, 1)

            def experts():
                start_free(pe, "pe")
                pe.wait_ge(r_tab, 1)
                nb = pe.value_load(tab[0:1, MAXB:MAXB + 1], min_val=9, max_val=MAXB)

                def rows_turn():
                    for k in range(KD):
                        mm = pe.transpose(ps[:, 2 + k // 4, P * (k % 4):P * (k % 4) + P], xe[:, P * k:P * k + P], ident)
                    mm.then_inc(e_xt, 1)

                def weights(o, part, at, n):
                    if isinstance(o, int):
                        return arena[:, (o % 2) * WSET + part * SLOT + at:(o % 2) * WSET + part * SLOT + at + n]
                    return arena[:, bass.ds((o % 2) * WSET + (part * SLOT + at), n)]

                def gate(o):
                    for k in range(KD):
                        mm = pe.matmul(ps[:, 0, :], xeT[:, k, :], weights(o, 0, DE * k, DE), start=(k == 0), stop=(k == KD - 1))
                    mm.then_inc(e_g, 1)

                def up(o):
                    for k in range(KD):
                        mm = pe.matmul(ps[:, 1, :], xeT[:, k, :], weights(o, 1, DE * k, DE), start=(k == 0), stop=(k == KD - 1))
                    mm.then_inc(e_u, 1)

                def hid_turn():
                    for c in range(4):
                        mm = pe.transpose(ps[:, 4, P * c:P * c + P], hid[:, P * c:P * c + P], ident)
                    mm.then_inc(e_ht, 1)

                def down(o):
                    for hf in range(2):
                        for k in range(4):
                            mm = pe.matmul(ps[:, 5 + hf, :], hidT[:, k, :], weights(o, 2, DM * k + 512 * hf, 512),
                                           start=(k == 0), stop=(k == 3))
                    mm.then_inc(e_dn, 1)

                pe.wait_ge(xe_in, 16)
                rows_turn()
                pe.wait_ge(e_xtev, 1)
                pe.wait_ge(wg_in, 16)
                gate(0)
                pe.wait_ge(wu_in, 16)
                up(0)
                pe.wait_ge(xe_in, 32)
                rows_turn()
                with pe.Fori(1, nb) as j:
                    o = pe.value_load(tab[0:1, bass.ds(j + (MAXB + 1), 1)], min_val=0, max_val=NE - 1)
                    pe.wait_ge(e_xtev, j + 1)
                    pe.wait_ge(e_sil, j + 1)
                    pe.wait_ge(wg_in, o * 16 + 16)
                    gate(o)
                    pe.wait_ge(e_hid, j + 1)
                    hid_turn()
                    pe.wait_ge(wu_in, o * 16 + 16)
                    up(o)
                    pe.wait_ge(xe_in, j * 16 + 32)
                    rows_turn()
                    o1 = pe.value_load(tab[0:1, bass.ds(j + MAXB, 1)], min_val=0, max_val=NE - 1)
                    pe.wait_ge(e_htev, j)
                    pe.wait_ge(wd_in, o1 * 16 + 16)
                    pe.wait_ge(e_ye, j * 2)
                    down(o1)
                last = pe.value_load(tab[0:1, bass.ds(nb + MAXB, 1)], min_val=0, max_val=NE - 1)
                pe.wait_ge(e_hid, nb + 1)
                hid_turn()
                pe.wait_ge(e_htev, nb)
                pe.wait_ge(wd_in, last * 16 + 16)
                pe.wait_ge(e_ye, nb * 2)
                down(last)

            pe.wait_ge(const_in, 16)
            norm_transposes(0, True)
            end_layer(pe, "pe")
            with pe.Fori(0, DEPTH) as l:
                phase = Phase(pe)
                units(0, NAB, {})
                phase()
                pe.wait_ge(k_zeroed, 1)
                attention_a()
                phase()
                attention_b()
                phase()
                branch_transposes(oA, 0, lambda i: pe.wait_ge(n_norm, i + 1))
                branch_transposes(oB, NT, lambda i: pe.wait_ge(b_oev, NT))
                phase()

                def rows_then_v():
                    pe.wait_ge(g_rows, 1)

                def columns():
                    pe.wait_ge(rot_ev, len(POST))
                    gate_columns()

                units(NAB, NU, {NAB + 2: gate_rows, UNITS.index(("cv", 0)): rows_then_v, UNITS.index(("co", 1)): columns})
                phase()
                mlstm()
                phase()
                branch_transposes(hsum, 2 * NT, lambda i: pe.wait_ge(n_norm, NT + i + 1))
                phase()
                gates()
                phase()
                project_out()
                norm_transposes(0, False)
                router()
                phase()
                experts()
                phase()
                norm_transposes(NT, True)
                end_layer(pe, "pe")

        @block.scalar
        def _(act):
            steps = [0]

            def link(ins):
                steps[0] += 1
                ins.then_inc(act_step, 1)
                act.wait_ge(act_step, steps[0])

            def norm_root(n):
                act.wait_ge(l_var, n)
                act.activation(rstd[:, :], rstd[:, :], ACT.Sqrt).then_inc(l_sqrt, 1)

            def norm_evacuate(first, to):
                for i, (t0, n) in enumerate(TOK):
                    act.wait_ge(l_t, first + i + 1)
                    b = 4 + 2 * (i % 2)
                    act.activation(to[:, 0:4, t0:t0 + n], ps[:, b, :].rearrange("p (k n) -> p k n", n=P)[:, :, 0:n], ACT.Copy)
                    act.activation(to[:, 4:8, t0:t0 + n], ps[:, b + 1, :].rearrange("p (k n) -> p k n", n=P)[:, :, 0:n],
                                   ACT.Copy).then_inc(l_ev, 1)

            def split(q):
                if q < NU:
                    b = WBLOCK[UNITS[q][0]]
                    if b >= 2 and q == FIRST[b]:
                        act.wait_ge(slot_in[b % 2], IN[b])
                elif q == NU:
                    act.wait_ge(slot_in[1], IN_GZ[0] + 16)
                act.activation(chunk_split(w_hi, q), chunk_source(q), ACT.Copy).then_inc(w_split_hi, 1)

            def evacuate(u):
                kind, c = UNITS[u]
                bank = halves(2 * (u % 2))
                act.wait_ge(unit_mm, u + 1)
                if u in POST:
                    r = POST[u]
                    if r >= 2:
                        act.wait_ge(rot_ev, r - 1)
                    scale = QSCALE if kind in ("aq", "bq") else 1.0
                    act.activation(two(raw[:, r % 2, :]), bank, ACT.Copy, scale=scale).then_inc(unit_ev, 1)
                elif kind in ("cq", "ck"):
                    ch = c + 4 * (kind == "ck")
                    if ch >= 2:
                        act.wait_ge(conv_done, ch - 1)
                    act.activation(two(craw[:, ch % 2, 1:1 + L]), bank, ACT.Copy).then_inc(unit_ev, 1)
                else:
                    act.activation(two(sco[:, c, :]), bank, ACT.Sigmoid).then_inc(unit_ev, 1)

            def attention_a():
                def exp(n, c):
                    m = TOK[n // 4][1]
                    act.wait_ge(a_m, 2 * n + c + 1)
                    if n >= 2 and c == 0:
                        act.wait_ge(a_t, n - 1)
                    act.activation(two(pA[0:m, n % 2, c, :]), halves(3 + 2 * c, m), ACT.Exp,
                                   bias=st[0:m, 2 * (n % 2) + c:2 * (n % 2) + c + 1],
                                   accum_out=st[0:m, 4 + 2 * (n % 2) + c:5 + 2 * (n % 2) + c]).then_inc(a_exp, 1)

                def evac(n):
                    m = TOK[n // 4][1]
                    act.wait_ge(a_t, n + 1)
                    if n >= 2:
                        act.wait_ge(a_o, n - 1)
                    act.activation(ptA[:, n % 2, :, 0:m],
                                   ps[:, (7, 1)[n % 2], :].rearrange("p (j q) -> p j q", q=P)[:, :, 0:m],
                                   ACT.Copy).then_inc(a_tev, 1)

                for n in range(4 * NT):
                    exp(n, 0)
                    if n >= 1:
                        evac(n - 1)
                    exp(n, 1)
                evac(4 * NT - 1)

            def attention_b():
                def exp(n):
                    i, h = n // 8, BHEAD[n % 8]
                    m = TOK[i][1]
                    act.wait_ge(b_m, n + 1)
                    act.activation(sB[0:m, n % 3, 0:bwidth[i]], sB[0:m, n % 3, 0:bwidth[i]], ACT.Exp,
                                   bias=st[0:m, 16 + h:17 + h],
                                   accum_out=st[0:m, 24 + h:25 + h]).then_inc(b_exp, 1)

                def evac(n):
                    i = n // 8
                    m, nbk = TOK[i][1], len(BTILES[i])
                    act.wait_ge(b_t, n + 1)
                    if n >= 2:
                        act.wait_ge(b_o, n - 1)
                    act.activation(ptA[:, n % 2, 0:nbk, 0:m],
                                   ps[:, (7, 1)[n % 2], 0:P * nbk].rearrange("p (j q) -> p j q", q=P)[:, :, 0:m],
                                   ACT.Copy).then_inc(b_tev, 1)

                for n in range(8 * NT):
                    exp(n)
                    if n >= 1:
                        evac(n - 1)
                    if n % 8 == 7:
                        m = TOK[n // 8][1]
                        act.wait_ge(b_snk, 2 * (n // 8) + 1)
                        act.activation(st[0:m, 40:48], st[0:m, 32:40], ACT.Exp).then_inc(b_snk, 1)
                evac(8 * NT - 1)

            def mlstm():
                for h in range(4):
                    act.wait_ge(m_in[h % 2], 32 * (h // 2 + 1))
                    for j, (t0, n) in enumerate(TOK):
                        for d in range(2):
                            lo, hi = (t0, L) if d == 0 else (0, t0 + n)
                            if h >= 2 and j == 0 and d == 0:
                                act.wait_ge(c_pv, NT * (h - 1))
                            col = 8 * d + 4 * d + h
                            act.activation(sC[h % 2][0:n, SAT[d][j]:SAT[d][j] + hi - lo], mb[0:n, h % 2, d, lo:hi], ACT.Exp,
                                           scale=-1.0, bias=gcol[0:n, j, col:col + 1]).then_inc(c_w, 1)
                    act.drain().then_inc(c_mbused, 1)

            norm_root(1)
            norm_evacuate(0, hT_hi)
            end_layer(act, "act")
            with act.Fori(0, DEPTH) as l:
                phase = Phase(act)
                steps[0] = 0
                act.wait_ge(first_in[0], l * 16 + 16)
                act.wait_ge(first_in[1], l * 16 + 16)
                split(0)
                split(1)
                act.wait_ge(h_saved, l * 32 + 32)
                for u in range(NAB):
                    act.wait_ge(unit_mm, u + 1)
                    split(u + 2)
                    evacuate(u)
                act.wait_ge(n_ready, 1)
                act.activation(st[:, 10:12], st[:, 8:10], ACT.Exp).then_inc(n_sqrt, 1)
                phase()
                attention_a()
                phase()
                act.wait_ge(n_ready, 2)
                act.activation(ssr[:, :, :], ssr[:, :, :], ACT.Sqrt).then_inc(n_sqrt, 1)
                attention_b()
                phase()
                for q in range(2 * NT):
                    t0, n = TOK[q % NT]
                    act.wait_ge(n_t, q + 1)
                    src = ps[:, 4 + q % 4, :].rearrange("p (c t) -> p c t", t=P)[:, :, 0:n]
                    act.activation(outT[:, q // NT, :, t0:t0 + n], src, ACT.Copy,
                                   scale=(colp[:, 36:37] if q < NT else 1.0)).then_inc(n_ev, 1)
                phase()
                chunk = 0

                def silu(ch):
                    c = ch % 4
                    act.wait_ge(conv_done, ch + 1)
                    d_ = (qC if ch < 4 else kC)[:, c, :]
                    act.activation(d_, ctmp[:, ch % 2, :], ACT.Silu, bias=colp[:, 24 + ch:25 + ch]).then_inc(silu_done, 1)

                for u in range(NAB, NU):
                    kind, c = UNITS[u]
                    act.wait_ge(unit_mm, u + 1)
                    split(u + 2)
                    if kind in ("cq", "ck"):
                        ch = c + 4 * (kind == "ck")
                        if ch >= 2:
                            silu(ch - 2)
                    evacuate(u)
                    if kind == "cq" and c == 0:
                        act.wait_ge(g_exp, 1)
                        act.activation(cg[:, 1, :, :], cg[:, 1, :, :], ACT.Exp, scale=-1.0).then_inc(g_exp, 1)
                        act.wait_ge(g_exp, 2)
                        act.activation(cg[:, 1, :, :], cg[:, 1, :, :], ACT.Ln, bias=1.0).then_inc(g_ln, 1)
                    if kind == "cv" and c == 0:
                        silu(6)
                        silu(7)
                        act.wait_ge(g_rows, 1)
                        act.activation(EF, EF, ACT.Exp, scale=-1.0)
                        act.activation(EB, EB, ACT.Exp, scale=-1.0).then_inc(g_e, 1)
                phase()
                mlstm()
                phase()
                act.wait_ge(n_ready, 3)
                act.activation(ssr[:, :, :], ssr[:, :, :], ACT.Sqrt).then_inc(n_sqrt, 1)
                phase()
                with act.Fori(0, 3) as t:
                    for u in range(8):
                        act.wait_ge(unit_mm, t * 8 + (NU + u + 1))
                        if u == 2:
                            act.wait_ge(slot_in[0], t * 16 + (IN_GZ[1] + 16))
                        if u == 6:
                            act.wait_ge(slot_in[1], t * 16 + (IN_GZ[0] + 32))
                        act.activation(chunk_split(w_hi, NU + u + 2), chunk_source(NU + u + 2), ACT.Copy).then_inc(w_split_hi, 1)
                        act.activation(two(sg[:, u % 2, :]), halves(4 * (u % 2)), ACT.Sigmoid).then_inc(gate_sig, 1)
                phase()
                for k in range(KD):
                    act.activation(hT_hi[:, k, :], merged[:, k, :], ACT.Copy).then_inc(m_split_hi, 1)
                for m in range(KD):
                    act.wait_ge(unit_mm, NU + NG + m + 1)
                    if m == 2:
                        act.wait_ge(slot_in[0], IN_GZ[1] + 64)
                    if m < KD - 2:
                        q = NU + NG + m + 2
                        act.activation(chunk_split(w_hi, q), chunk_source(q), ACT.Copy).then_inc(w_split_hi, 1)
                    if m >= 2:
                        act.wait_ge(y_t, m - 1)
                    act.activation(two(yraw[:, m % 2, :]), halves(2 * (m % 2)), ACT.Copy).then_inc(y_ev, 1)
                norm_root(1)
                norm_evacuate(0, hT)
                act.wait_ge(r_a, 1)
                act.activation(r4[:, 0, :, :], r4[:, 0, :, :], ACT.Exp).then_inc(r_exp, 1)
                act.wait_ge(r_b, 1)
                act.activation(r5[:, 4, :], r5[:, 3, :], ACT.Exp).then_inc(r_exp2, 1)
                phase()
                start_free(act, "act")
                nb = act.value_load(tab[0:1, MAXB:MAXB + 1], min_val=9, max_val=MAXB)

                def rows_evacuate(done):
                    act.wait_ge(e_xt, done)
                    act.activation(xeT[:, :, :].rearrange("p (b k) n -> p b (k n)", b=2), ps[:, 2:4, :], ACT.Copy).then_inc(e_xtev, 1)

                def result(done):
                    act.wait_ge(ys_out, done * 16)
                    act.wait_ge(e_dn, done + 1)
                    act.activation(ye[:, 512:1024], ps[:, 6, :], ACT.Copy).then_inc(e_ye, 1)

                rows_evacuate(1)
                act.wait_ge(e_g, 2)
                act.activation(sil, ps[:, 0, :], ACT.Silu).then_inc(e_sil, 1)
                act.wait_ge(e_u, 2)
                rows_evacuate(2)
                with act.Fori(1, nb) as j:
                    act.wait_ge(e_g, j + 2)
                    act.wait_ge(e_hid, j + 1)
                    act.activation(sil, ps[:, 0, :], ACT.Silu).then_inc(e_sil, 1)
                    act.wait_ge(e_u, j + 2)
                    rows_evacuate(j + 2)
                    result(j)
                result(nb)
                phase()
                norm_root(2)
                norm_evacuate(NT, hT_hi)
                end_layer(act, "act")

        @block.vector
        def _(dve):
            steps = [0]

            def link(ins):
                steps[0] += 1
                ins.then_inc(dve_step, 1)
                dve.wait_ge(dve_step, steps[0])

            def norm_stats(i, n):
                dve.bn_stats(bn[0:n, i, 0:6], h_tok[0:n, i, 0:512])
                link(dve.bn_stats(bn[0:n, i, 6:12], h_tok[0:n, i, 512:1024]))
                link(dve.bn_aggr(mv[0:n, i, :], bn[0:n, i, 0:12]))

            def norm_apply(n_sq, split):
                dve.tensor_scalar(rstd[:, :], mv[:, :, 1], EPS, None, ALU.add).then_inc(l_var, 1)
                dve.wait_ge(l_sqrt, n_sq)
                link(dve.reciprocal(rstd[:, :], rstd[:, :]))

                def low(i):
                    t0, n = TOK[i]
                    dve.wait_ge(l_ev, NT * (n_sq - 1) + i + 1)
                    for x in range(2):
                        ins = dve.tensor_tensor(hT_lo[:, 4 * x:4 * x + 4, t0:t0 + n],
                                                ps[:, 4 + 2 * (i % 2) + x, :].rearrange("p (k n) -> p k n", n=P)[:, :, 0:n],
                                                as_f32(hT_hi)[:, 4 * x:4 * x + 4, t0:t0 + n], ALU.subtract)
                    ins.then_inc(l_lo, 1)

                for i, (_, n) in enumerate(TOK):
                    link(dve.tensor_scalar(h_tok[0:n, i, :], h_tok[0:n, i, :], mv[0:n, i, 0:1], rstd[0:n, i:i + 1],
                                           ALU.subtract, ALU.mult))
                    dve.tensor_tensor(h_tok[0:n, i, :], h_tok[0:n, i, :], lngb[0:n, 0, :], ALU.mult).then_inc(l_mul, 1)
                    if split and i >= 2:
                        low(i - 2)
                if split:
                    low(NT - 2)
                    low(NT - 1)

            def split_low(q, done):
                dve.wait_ge(w_split_hi, done)
                dve.tensor_tensor(chunk_split(w_lo, q), chunk_source(q), chunk_split(as_f32(w_hi), q),
                                  ALU.subtract).then_inc(w_split_lo, 1)

            def post(u):
                kind, c = UNITS[u]
                r = POST[u]
                bank = 4 + 2 * (r % 2)
                dve.wait_ge(rot_mm, r + 1)
                if kind in ROPE:
                    dve.tensor_tensor(two(t_sin[:, r % 2, :]), halves(bank), two(C("sin")), ALU.mult)
                    link(dve.tensor_tensor(raw[:, r % 2, :], raw[:, r % 2, :], C("cos"), ALU.mult))
                    if kind in ("aq", "bq"):
                        dve.tensor_tensor(ROPE[kind][:, c, :], raw[:, r % 2, :], t_sin[:, r % 2, :], ALU.add).then_inc(rot_ev, 1)
                        return
                    for g in range(2):
                        half = slice(64 * g, 64 * g + 64)
                        ins = dve.tensor_tensor(ROPE[kind][g][half, c, :], raw[half, r % 2, :], t_sin[half, r % 2, :], ALU.add)
                    ins.then_inc(rot_ev, 1)
                    return
                cols = slice(0, META if kind == "cg" else P)
                to = {"av": lambda: vA[:, :, P * c:P * c + P], "bv": lambda: vB, "cv": lambda: vC[:, :, c, 0:P],
                      "cg": lambda: cg[:, 0, :, :]}[kind]()
                dve.tensor_copy(to[:, 1:NT, :], ps[:, bank, :].rearrange("p (j d) -> p j d", d=P)[:, :, cols])
                dve.tensor_copy(to[0:META, 0, :], ps[0:META, bank + 1, cols]).then_inc(rot_ev, 1)

            def attention_a():
                nlam = st[:, 12:13]

                def rowmax(n, c):
                    m = TOK[n // 4][1]
                    dve.wait_ge(a_s, 2 * n + c + 1)
                    dve.tensor_reduce(st[0:m, 2 * (n % 2) + c:2 * (n % 2) + c + 1], halves(3 + 2 * c, m), AX.XY, ALU.max,
                                      negate=True).then_inc(a_m, 1)

                def combine(n):
                    i, h = n // 4, n % 4
                    m = TOK[i][1]
                    s = 4 + 2 * (n % 2)
                    dve.wait_ge(a_exp, 2 * n + 2)
                    dve.reciprocal(rs[0:m, 0, i, h:h + 1], st[0:m, s:s + 1])
                    link(dve.reciprocal(st[0:m, 14:15], st[0:m, s + 1:s + 2]))
                    link(dve.scalar_tensor_tensor(st[0:m, 13:14], st[0:m, s:s + 1], nlam[0:m, :], st[0:m, 14:15], ALU.mult, ALU.mult))
                    dve.scalar_tensor_tensor(pA[0:m, n % 2, 0, :], pA[0:m, n % 2, 1, :], st[0:m, 13:14], pA[0:m, n % 2, 0, :],
                                             ALU.mult, ALU.add).then_inc(a_comb, 1)

                def meta_evac(n):
                    m = TOK[n // 4][1]
                    dve.wait_ge(a_t, n + 1)
                    if n >= 2:
                        dve.wait_ge(a_o, n - 1)
                    dve.tensor_copy(ptm[0:META, n % 2, 0:m], ps[0:META, 0, 0:m]).then_inc(a_tmev, 1)

                def out(i):
                    m = TOK[i][1]
                    dve.wait_ge(a_o, 4 * (i + 1))
                    dve.tensor_tensor(oA[0:m, i, :].rearrange("p (h d) -> p h d", d=P),
                                      ps[0:m, 2, :].rearrange("p (h d) -> p h d", d=P),
                                      rs[0:m, 0, i, 0:4].unsqueeze(2).broadcast_to([m, 4, P]), ALU.mult).then_inc(a_oev, 1)

                rowmax(0, 0)
                rowmax(0, 1)
                for n in range(4 * NT):
                    if n >= 1:
                        meta_evac(n - 1)
                    combine(n)
                    if n + 1 < 4 * NT:
                        rowmax(n + 1, 0)
                    if n >= 4 and n % 4 == 0:
                        out(n // 4 - 1)
                    if n + 1 < 4 * NT:
                        rowmax(n + 1, 1)
                meta_evac(4 * NT - 1)
                out(NT - 1)

            def attention_b():
                def rowmax(n):
                    i, h = n // 8, BHEAD[n % 8]
                    m, w = TOK[i][1], bwidth[i]
                    dve.wait_ge(b_s, n + 1)
                    if n >= 2:
                        dve.wait_ge(b_m, n - 1)
                    if n >= 3:
                        dve.wait_ge(b_t, n - 2)
                    link(dve.tensor_tensor_reduce(sB[0:m, n % 3, 0:w], ps[0:m, 3 + n % 4, 0:w], C(BMASK[i], m, w), 1.0, LOW,
                                                  ALU.add, ALU.max, st[0:m, 60 + n % 2:61 + n % 2]))
                    dve.tensor_scalar(st[0:m, 16 + h:17 + h], st[0:m, 60 + n % 2:61 + n % 2], R("sink")[0:m, h:h + 1], -1.0, ALU.max, ALU.mult
                                      ).then_inc(b_m, 1)

                def meta_evac(n):
                    m = TOK[n // 8][1]
                    dve.wait_ge(b_t, n + 1)
                    if n >= 2:
                        dve.wait_ge(b_o, n - 1)
                    dve.tensor_copy(ptm[0:META, n % 2, 0:m], ps[0:META, 0, 0:m]).then_inc(b_tmev, 1)

                def sink(i):
                    m = TOK[i][1]
                    dve.wait_ge(b_m, 8 * (i + 1))
                    dve.tensor_tensor(st[0:m, 32:40], R("sink")[0:m, :], st[0:m, 16:24], ALU.add).then_inc(b_snk, 1)
                    dve.wait_ge(b_exp, 8 * (i + 1))
                    dve.wait_ge(b_snk, 2 * (i + 1))
                    link(dve.tensor_tensor(st[0:m, 48:56], st[0:m, 24:32], st[0:m, 40:48], ALU.add))
                    link(dve.reciprocal(rs[0:m, 1, i, :], st[0:m, 48:56]))

                def out(i):
                    m = TOK[i][1]
                    dve.wait_ge(b_o, 8 * (i + 1))
                    dve.tensor_tensor(oB[0:m, i, :].rearrange("p (h d) -> p h d", d=64),
                                      ps[0:m, 2, :].rearrange("p (h d) -> p h d", d=64),
                                      rs[0:m, 1, i, :].unsqueeze(2).broadcast_to([m, 8, 64]), ALU.mult).then_inc(b_oev, 1)

                N = 8 * NT
                rowmax(0)
                for n in range(N):
                    if n >= 1:
                        meta_evac(n - 1)
                    if n >= 8 and n % 8 == 0:
                        out(n // 8 - 1)
                    if n % 8 == 7:
                        sink(n // 8)
                    if n + 1 < N:
                        rowmax(n + 1)
                meta_evac(N - 1)
                out(NT - 1)

            def lambdas():
                dve.wait_ge(par_in, 80)
                lam = R("lam").rearrange("p (a b) -> p a b", b=64)
                for x in range(2):
                    ins = dve.tensor_tensor_reduce(t_sin[:, 0, 64 * x:64 * x + 64], lam[:, 2 * x, :], lam[:, 2 * x + 1, :], 1.0, 0.0,
                                                   ALU.mult, ALU.add, st[:, 8 + x:9 + x])
                ins.then_inc(n_ready, 1)
                dve.wait_ge(n_ready, 1)

            def lambda_end():
                dve.wait_ge(n_sqrt, 1)
                link(dve.tensor_tensor(st[:, 13:14], st[:, 11:12], st[:, 10:11], ALU.subtract))
                link(dve.tensor_tensor(st[:, 12:13], st[:, 13:14], R("neg_lam_init"), ALU.add))
                link(dve.tensor_tensor(colp[:, 36:37], colp[:, 36:37], R("one_minus"), ALU.mult))

            def rms_stats():
                for i, (_, n) in enumerate(TOK):
                    o = oA[0:n, i, :]
                    link(dve.tensor_tensor(sq[0:n, i % 2, :], o, o, ALU.mult))
                    link(dve.tensor_reduce(ssr[0:n, i, :], sq[0:n, i % 2, :].rearrange("p (h d) -> p h d", d=P), AX.X, ALU.add))
                dve.tensor_scalar(ssr[:, :, :], ssr[:, :, :], 1.0 / P, EPS, ALU.mult, ALU.add).then_inc(n_ready, 1)

            def rms_apply():
                dve.wait_ge(n_sqrt, 2)
                link(dve.reciprocal(ssr[:, :, :], ssr[:, :, :]))
                for i, (_, n) in enumerate(TOK):
                    o = oA[0:n, i, :].rearrange("p (h d) -> p h d", d=P)
                    dve.tensor_tensor(o, o, ssr[0:n, i, :].unsqueeze(2).broadcast_to([n, 4, P]), ALU.mult).then_inc(n_norm, 1)

            def gate_logs():
                dve.wait_ge(rot_ev, POST[NAB] + 1)
                link(dve.tensor_tensor(cg[:, 0, :, :], cg[:, 0, :, :], R("gate_b").unsqueeze(1).broadcast_to([P, NT, 16]), ALU.add))
                dve.scalar_tensor_tensor(cg[:, 1, :, :], cg[:, 0, :, :], -1.0, cg[:, 0, :, :], ALU.mult, ALU.max).then_inc(g_exp, 1)

            def gate_logs2():
                dve.wait_ge(g_ln, 1)
                z = cg[:, 0, :, :].rearrange("p t (d k h) -> p t d k h", d=2, k=2)
                for d in range(2):
                    zl = z[:, :, d, 1, :]
                    ll = cg[:, 1, :, 8 * d + 4:8 * d + 8]
                    link(dve.scalar_tensor_tensor(zl, zl, 0.0, ll, ALU.min, ALU.subtract))
                for d in range(2):
                    dve.tensor_copy(cg[:, 1, :, 4 * d:4 * d + 4], z[:, :, d, 1, :])
                    ins = dve.tensor_copy(cg[:, 1, :, 8 + 4 * d:12 + 4 * d], z[:, :, d, 0, :])
                ins.then_inc(g_lf, 1)

            def gate_scans():
                dve.wait_ge(g_t, 1)
                dve.memset(ZR, 0.0)
                for bank, row in ((4, LF), (6, LI)):
                    dve.tensor_copy(row[:, 0:400], ps[0:8, bank, 0:400])
                    link(dve.tensor_copy(row[:, 400:L], ps[0:8, bank + 1, 0:P]))
                dve.tensor_tensor_scan(BF, ZR, LF, 0.0, ALU.add, ALU.add)
                link(dve.tensor_tensor_scan(BB[:, ::-1], ZR, LF[:, ::-1], 0.0, ALU.add, ALU.add))
                dve.tensor_tensor(UF, LI, BF, ALU.subtract)
                link(dve.tensor_tensor(UB, LI, BB, ALU.subtract))
                dve.tensor_tensor_scan(MF, ZR, UF, 0.0, ALU.add, ALU.max)
                link(dve.tensor_tensor_scan(MB[:, ::-1], ZR, UB[:, ::-1], 0.0, ALU.add, ALU.max))
                dve.tensor_tensor(EF, MF, BF, ALU.add)
                dve.tensor_tensor(EB, MB, BB, ALU.add).then_inc(g_rows, 1)

            def gate_cols():
                dve.wait_ge(g_t2, 1)
                dve.tensor_copy(gcol[0:META, 0, :], ps[0:META, 4, 0:32])
                dve.tensor_copy(gcol[:, 1:NT, :], ps[:, 4, 32:32 * NT].rearrange("p (t x) -> p t x", x=32)).then_inc(g_col, 1)

            def conv(ch):
                dve.wait_ge(unit_ev, NAB + 1 + ch + 1)
                if ch >= 2:
                    dve.wait_ge(silu_done, ch - 1)
                src, o = craw[:, ch % 2, :], ctmp[:, ch % 2, :]
                tap = [colp[:, 3 * ch + k:3 * ch + k + 1] for k in range(3)]
                link(dve.tensor_scalar(o, src[:, 0:L], tap[0], None, ALU.mult))
                link(dve.scalar_tensor_tensor(o, src[:, 1:L + 1], tap[1], o, ALU.mult, ALU.add))
                dve.scalar_tensor_tensor(o, src[:, 2:L + 2], tap[2], o, ALU.mult, ALU.add).then_inc(conv_done, 1)

            def mlstm():
                def weigh(h, j):
                    q = NT * h + j
                    t0, n = TOK[j]
                    b = (0, 3)[q % 2]
                    dve.wait_ge(c_qk, q + 1)
                    for d in range(2):
                        lo, hi = (t0, L) if d == 0 else (0, t0 + n)
                        dve.wait_ge(c_w, 2 * q + d + 1)
                        for bank, x0, x1 in ((b, lo, min(hi, 272)), (b + 1, max(lo, 272), hi)):
                            if x1 > x0:
                                s = sC[h % 2][0:n, SAT[d][j] + x0 - lo:SAT[d][j] + x1 - lo]
                                base = 0 if bank == b else 272
                                ins = dve.scalar_tensor_tensor(s, ps[0:n, bank, x0 - base:x1 - base], MSCALE, s, ALU.mult, ALU.mult)
                        ins.then_inc(c_mul, 1)

                def post(h, i):
                    q = NT * h + i
                    m = TOK[i][1]
                    dve.wait_ge(c_pv, q + 1)
                    bank = ps[0:m, 5 + q % 2, :]
                    den = bank.rearrange("p (d x) -> p d x", x=256)[:, :, 128]
                    em = gcol[0:m, i, 16:32].rearrange("p (d x) -> p d x", x=8)
                    for d in range(2):
                        ins = dve.tensor_scalar(st[0:m, 56 + d:57 + d], den[:, d:d + 1], -1.0, em[:, d, 4 * d + h:4 * d + h + 1],
                                                ALU.mult, ALU.max)
                    link(ins)
                    link(dve.tensor_tensor(st[0:m, 56:58], st[0:m, 56:58], den, ALU.max))
                    link(dve.reciprocal(st[0:m, 58:60], st[0:m, 56:58]))
                    o = hsum[0:m, i, P * h:P * h + P]
                    link(dve.tensor_scalar(o, bank[:, 0:P], st[0:m, 58:59], None, ALU.mult))
                    link(dve.scalar_tensor_tensor(o, bank[:, 256:256 + P], st[0:m, 59:60], o, ALU.mult, ALU.add))
                    dve.bn_stats(bn[0:m, i, 0:6], o).then_inc(c_post, 1)
                    dve.wait_ge(c_post, q + 1)
                    dve.bn_aggr(ss[0:m, i, h, :], bn[0:m, i, 0:6])

                for h in range(5):
                    for j in range(NT):
                        if h < 4:
                            weigh(h, j)
                        if h >= 1:
                            post(h - 1, j)

            def c_norm():
                link(dve.tensor_scalar(ssr[:, :, :], ss[:, :, :, 1], EPS, None, ALU.add))
                dve.drain().then_inc(n_ready, 1)
                dve.wait_ge(n_sqrt, 3)
                link(dve.reciprocal(ssr[:, :, :], ssr[:, :, :]))
                for i, (_, n) in enumerate(TOK):
                    for h in range(4):
                        o = hsum[0:n, i, P * h:P * h + P]
                        ins = dve.tensor_scalar(o, o, ss[0:n, i, h, 0:1], ssr[0:n, i, h:h + 1], ALU.subtract, ALU.mult)
                    ins.then_inc(n_norm, 1)

            def c_out():
                for i, (t0, n) in enumerate(TOK):
                    q = 2 * NT + i
                    dve.wait_ge(n_t, q + 1)
                    for c in range(4):
                        ins = dve.scalar_tensor_tensor(outT[:, 2, c, t0:t0 + n], ps[:, 4 + q % 4, P * c:P * c + n],
                                                       colp[:, 32 + c:33 + c], sco[:, c, t0:t0 + n], ALU.mult, ALU.mult)
                    ins.then_inc(n_ev, 1)

            def router():
                dve.wait_ge(r_mm, 1)
                for i, (_, n) in enumerate(TOK):
                    ins = dve.tensor_tensor(lg[0:n, i, :], ps[0:n, 0, 36 * i:36 * i + 36], R("b_r")[0:n, :], ALU.add)
                link(ins)
                g4, x32 = lg[:, :, 0:4], lg[:, :, 4:36]
                b5 = lambda k, w: r5[:, k, :].unsqueeze(2).broadcast_to([P, NT, w])
                link(dve.tensor_reduce(r5[:, 0, :], g4, AX.X, ALU.max))
                dve.tensor_tensor(r4[:, 0, :, :], g4, b5(0, 4), ALU.subtract).then_inc(r_a, 1)
                link(dve.tensor_tensor(r4[:, 1, :, :], g4, b5(0, 4), ALU.is_equal))
                link(dve.tensor_tensor(r4[:, 1, :, :], r4[:, 1, :, :], C("wg4").unsqueeze(1).broadcast_to([P, NT, 4]), ALU.mult))
                link(dve.tensor_reduce(r5[:, 1, :], r4[:, 1, :, :], AX.X, ALU.max))
                link(dve.tensor_tensor(r4[:, 2, :, :], r4[:, 1, :, :], b5(1, 4), ALU.is_equal))
                link(dve.tensor_scalar(r4[:, 2, :, :], r4[:, 2, :, :], -1.0, -NEG, ALU.add, ALU.mult))
                dve.wait_ge(xs_zeroed, 32)
                em = e32[:, 3, :, :]
                link(dve.tensor_tensor(em.rearrange("p t (g e) -> p t g e", e=8), x32.rearrange("p t (g e) -> p t g e", e=8),
                                       r4[:, 2, :, :].unsqueeze(3).broadcast_to([P, NT, 4, 8]), ALU.add))
                we = C("we32").unsqueeze(1).broadcast_to([P, NT, NE])
                for k in range(2):
                    oh = e32[:, k, :, :]
                    link(dve.tensor_reduce(r5[:, 5 + k, :], em, AX.X, ALU.max))
                    link(dve.tensor_tensor(oh, em, b5(5 + k, NE), ALU.is_equal))
                    link(dve.tensor_tensor(oh, oh, we, ALU.mult))
                    link(dve.tensor_reduce(r5[:, 1, :], oh, AX.X, ALU.max))
                    link(dve.tensor_tensor(oh, oh, b5(1, NE), ALU.is_equal))
                    if k == 0:
                        link(dve.scalar_tensor_tensor(em, oh, 2 * NEG, em, ALU.mult, ALU.add))
                dve.tensor_tensor(r5[:, 3, :], r5[:, 6, :], r5[:, 5, :], ALU.subtract).then_inc(r_b, 1)
                link(dve.tensor_tensor(e32[:, 2, :, :], e32[:, 0, :, :], e32[:, 1, :, :], ALU.add))
                dve.tensor_tensor(e32[:, 2, :, :], e32[:, 2, :, :], C("valid").unsqueeze(2).broadcast_to([P, NT, NE]),
                                  ALU.mult).then_inc(r_cnt, 1)
                dve.wait_ge(r_exp, 1)
                link(dve.tensor_reduce(r5[:, 2, :], r4[:, 0, :, :], AX.X, ALU.add))
                dve.wait_ge(r_exp2, 1)
                link(dve.scalar_tensor_tensor(r5[:, 9, :], r5[:, 4, :], 1.0, r5[:, 2, :], ALU.add, ALU.mult))
                link(dve.reciprocal(r5[:, 7, :], r5[:, 9, :]))
                link(dve.tensor_tensor(r5[:, 8, :], r5[:, 7, :], r5[:, 4, :], ALU.mult))
                dve.wait_ge(r_rank, 1)
                link(dve.tensor_copy(n32[:, 0, :], ps[:, 1, NE * NT:NE * NT + NE]))
                cmp = e32[:, 3, :, :].rearrange("p t e -> p (t e)").rearrange("p (e t) -> p e t", t=NT)
                link(dve.tensor_tensor(cmp, n32[:, 0, :].unsqueeze(2).broadcast_to([P, NE, NT]),
                                       C("thr").unsqueeze(1).broadcast_to([P, NE, NT]), ALU.is_gt))
                link(dve.tensor_reduce(n32[:, 1, :], cmp, AX.X, ALU.add))
                link(dve.tensor_tensor_scan(n32[:, 2, :], C("zero"), n32[:, 1, :], 0.0, ALU.add, ALU.add))
                link(dve.tensor_tensor(n32[:, 3, :], n32[:, 2, :], n32[:, 1, :], ALU.subtract))
                link(dve.tensor_scalar(n32[:, 3, :], n32[:, 3, :], float(P), None, ALU.mult))
                link(dve.tensor_tensor(e32[:, 3, :, :], ps[:, 1, 0:NE * NT].rearrange("p (t e) -> p t e", e=NE),
                                       n32[:, 3, :].unsqueeze(1).broadcast_to([P, NT, NE]), ALU.add))
                for k in range(2):
                    link(dve.tensor_tensor(e32[:, k, :, :], e32[:, k, :, :], e32[:, 3, :, :], ALU.mult))
                    link(dve.tensor_reduce(r5[:, 10 + k, :], e32[:, k, :, :], AX.X, ALU.add))
                    ins = dve.tensor_copy(dst[:, :, k], r5[:, 10 + k, :])
                ins.then_inc(r_dst, 1)
                big = arena[0:1, mo:mo + MAXB * NE].rearrange("p (j e) -> p j e", e=NE)
                link(dve.tensor_tensor(big, n32[0:1, 2, :].unsqueeze(1).broadcast_to([1, MAXB, NE]),
                                       C("jj", 1).unsqueeze(2).broadcast_to([1, MAXB, NE]), ALU.is_le))
                link(dve.tensor_reduce(tabf[0:1, 0:MAXB], big, AX.X, ALU.add))
                link(dve.tensor_scalar(tabf[0:1, 0:MAXB], tabf[0:1, 0:MAXB], float(NE - 1), None, ALU.min))
                dve.memset(tabf[0:1, 2 * MAXB + 1:2 * MAXB + 2], 1.0)
                dve.tensor_copy(tabf[0:1, MAXB:MAXB + 1], n32[0:1, 2, NE - 1:NE])
                link(dve.tensor_scalar(n32[0:1, 0, :], n32[0:1, 1, :], 1.0, None, ALU.min))
                link(dve.tensor_tensor(big, big, n32[0:1, 0, :].unsqueeze(1).broadcast_to([1, MAXB, NE]), ALU.mult))
                link(dve.tensor_reduce(tabf[0:1, MAXB + 1:2 * MAXB + 1], big, AX.X, ALU.add))
                link(dve.tensor_tensor(tabf[0:1, 2 * MAXB + 2:3 * MAXB + 1], tabf[0:1, MAXB + 2:2 * MAXB + 1],
                                       tabf[0:1, MAXB + 1:2 * MAXB], ALU.subtract))
                dve.tensor_copy(tab[0:1, 0:3 * MAXB + 1], tabf[0:1, 0:3 * MAXB + 1]).then_inc(r_tab, 1)

            for t in (mv, ssr, ss, cg, lg, rs, gcol):
                dve.memset(t[:], 1.0)
            dve.wait_ge(const_in, 16)
            dve.wait_ge(x_in, 32)
            dve.wait_ge(ln0_in, 32)
            for i, (_, n) in enumerate(TOK):
                norm_stats(i, n)
            norm_apply(1, True)
            end_layer(dve, "dve")
            with dve.Fori(0, DEPTH) as l:
                phase = Phase(dve)
                steps[0] = 0
                dve.memset(zeros, 0.0).then_inc(zero_ready, 1)
                split_low(0, 1)
                split_low(1, 2)
                dve.wait_ge(h_saved, l * 32 + 32)
                lambdas()
                for u in range(NAB):
                    split_low(u + 2, u + 3)
                    post(u)
                lambda_end()
                phase()
                attention_a()
                phase()
                rms_stats()
                rms_apply()
                attention_b()
                phase()
                dve.memset(craw[:, :, 0:1], 0.0)
                dve.memset(craw[:, :, L + 1:L + 2], 0.0)
                dve.memset(vC[:, :, :, 128:129], 1.0)
                phase()
                for u in range(NAB, NU):
                    kind, c = UNITS[u]
                    split_low(u + 2, u + 3)
                    if u in POST:
                        post(u)
                    if kind == "cg":
                        gate_logs()
                    if kind in ("cq", "ck"):
                        conv(c + 4 * (kind == "ck"))
                    if kind == "cq" and c == 0:
                        gate_logs2()
                    if kind == "cq" and c == 3:
                        gate_scans()
                    if kind == "co" and c == 2:
                        gate_cols()
                phase()
                mlstm()
                phase()
                c_norm()
                c_out()
                dve.memset(merged[:, :, :], 0.0).then_inc(gate_free, 2)
                phase()
                with dve.Fori(0, 3) as t:
                    for u in range(8):
                        split_low(NU + u + 2, t * 8 + (NU + u + 3))
                        dve.wait_ge(gate_sig, t * 8 + (u + 1))
                        dve.wait_ge(gate_mm, t * 8 + (u + 1))
                        dve.tensor_tensor(two(tg[:, u % 2, :]), two(sg[:, u % 2, :]), halves(4 * (u % 2) + 2), ALU.mult).then_inc(gate_tmp, 1)
                        dve.wait_ge(gate_tmp, t * 8 + (u + 1))
                        dve.tensor_tensor(merged[:, u, :], merged[:, u, :], tg[:, u % 2, :], ALU.add).then_inc(gate_free, 1)
                phase()
                for k in range(KD):
                    dve.wait_ge(m_split_hi, k + 1)
                    dve.tensor_tensor(hT_lo[:, k, :], merged[:, k, :], as_f32(hT_hi)[:, k, :], ALU.subtract).then_inc(m_split_lo, 1)
                dve.wait_ge(h_back, 32)
                for m in range(KD):
                    if m < KD - 2:
                        split_low(NU + NG + m + 2, NU + NG + m + 3)
                    dve.wait_ge(y_t, m + 1)
                    bank, cols = 4 + 2 * (m % 2), slice(P * m, P * m + P)
                    o = h_tok[:, 1:NT, cols]
                    dve.scalar_tensor_tensor(o, o, ALPHA, ps[:, bank, :].rearrange("p (j d) -> p j d", d=P), ALU.mult, ALU.add)
                    o = h_tok[0:META, 0, cols]
                    dve.scalar_tensor_tensor(o, o, ALPHA, ps[0:META, bank + 1, 0:P], ALU.mult, ALU.add).then_inc(y_add, 1)
                    dve.wait_ge(y_add, m + 1)
                    for i, (_, n) in enumerate(TOK):
                        ins = dve.bn_stats(bn[0:n, i, 6 * m:6 * m + 6], h_tok[0:n, i, cols])
                link(ins)
                for i, (_, n) in enumerate(TOK):
                    ins = dve.bn_aggr(mv[0:n, i, :], bn[0:n, i, :])
                link(ins)
                norm_apply(1, False)
                router()
                phase()
                start_free(dve, "dve")
                nb = dve.value_load(tab[0:1, MAXB:MAXB + 1], min_val=9, max_val=MAXB)

                def hidden(j):
                    dve.wait_ge(e_sil, j + 2)
                    dve.wait_ge(e_u, j + 2)
                    dve.tensor_tensor(hid, sil, ps[:, 1, :], ALU.mult).then_inc(e_hid, 1)

                def hidden_turned(j):
                    dve.wait_ge(e_ht, j)
                    dve.tensor_copy(hidT[:, :, :].rearrange("p k n -> p (k n)"), ps[:, 4, :]).then_inc(e_htev, 1)

                def result(done):
                    dve.wait_ge(ys_out, done * 16)
                    dve.wait_ge(e_dn, done + 1)
                    dve.tensor_copy(ye[:, 0:512], ps[:, 5, :]).then_inc(e_ye, 1)

                hidden(0)
                with dve.Fori(1, nb) as j:
                    hidden_turned(j)
                    hidden(j)
                    result(j)
                hidden_turned(nb)
                result(nb)
                phase()
                for i, (_, n) in enumerate(TOK):
                    dve.wait_ge(gathered[i], l * 32 + 32)
                    o = h_tok[0:n, i, :]
                    y1, y2 = gath[0:n, i, 0, :], gath[0:n, i, 1, :]
                    link(dve.tensor_scalar(y1, y1, r5[0:n, 7, i:i + 1], None, ALU.mult))
                    link(dve.scalar_tensor_tensor(o, o, ALPHA, y1, ALU.mult, ALU.add))
                    link(dve.scalar_tensor_tensor(o, y2, r5[0:n, 8, i:i + 1], o, ALU.mult, ALU.add))
                    norm_stats(i, n)
                dve.wait_ge(ln2_in, 32)
                norm_apply(2, True)
                end_layer(dve, "dve")


def constants():
    c = np.zeros((P, NCONST), np.float32)

    def put(name, value):
        at, w = CONST[name]
        c[:, at:at + w] = value

    inv = (1.0 / (np.float32(10000.0) ** (np.arange(0, 64, 2, dtype=np.float32) / np.float32(64)))).astype(np.float32)
    ang = np.arange(L, dtype=np.float32)[None, :] * inv[np.arange(P) % 32][:, None]
    put("cos", np.cos(ang))
    put("sin", np.sin(ang))
    put("ident", np.eye(P))
    rot = np.zeros((P, P), np.float32)
    for m in range(P):
        if m % 64 < 32:
            rot[m + 32, m] = -1.0
        else:
            rot[m - 32, m] = 1.0
    put("rot", rot)
    q, k = np.arange(P)[:, None], np.arange(P)[None, :]
    prev, nxt = np.where(k >= q, 0.0, NEG), np.where(k <= q, 0.0, NEG)
    m0 = np.zeros((P, 144))
    m0[:, 16:] = np.where(k <= q + P - META, 0.0, NEG)
    put("mask0", m0)
    z16, z128 = np.zeros((P, 16)), np.zeros((P, P))
    put("mask1", np.concatenate([z16, z128, nxt], 1))
    put("mask2", np.concatenate([z16, prev, z128, nxt], 1))
    put("ltri", q < k)
    put("ones", 1.0)
    valid = np.ones((P, NT))
    valid[META:, 0] = 0.0
    put("valid", valid)
    put("wg4", 4.0 - np.arange(4))
    put("we32", float(NE) - np.arange(NE))
    put("thr", float(P) * np.arange(NT))
    put("jj", np.arange(MAXB))
    return c


def kernel(**inputs):
    import numpy as _np
    import concourse.bacc as _bacc
    from concourse import mybir as _mybir
    from concourse.bass_utils import run_bass_kernel_spmd as _run

    i = {k: _np.asarray(v) for k, v in inputs.items()}
    arrays = {n: _np.ascontiguousarray(i[n]) for n in
              ("x", "meta", "ln_in_g", "ln_in_b", "w_in", "w_branch", "w_out", "ln1_g", "ln1_b", "ln2_g", "ln2_b",
               "w_gate", "w_up", "w_down")}
    f = _np.float32
    lam_init = _np.array([0.8 - 0.6 * _np.exp(-0.3 * l) for l in range(DEPTH)], f)[:, None]
    arrays["consts"] = constants()
    arrays["rowp"] = _np.concatenate([i["gate_b"], i["b_rg"], i["b_re"], i["sink"], i["lam_q1"], i["lam_k1"],
                                      i["lam_q2"], i["lam_k2"], -lam_init, f(1) - lam_init], axis=1)
    cw = i["conv_w"].reshape(DEPTH, 3, 8, P).transpose(0, 3, 2, 1).reshape(DEPTH, P, 24)
    arrays["colp"] = _np.concatenate([cw, i["conv_b"].reshape(DEPTH, 8, P).transpose(0, 2, 1),
                                      i["mlstm_g"].reshape(DEPTH, 4, P).transpose(0, 2, 1),
                                      i["diff_g"][:, :, None]], axis=2)
    arrays["w_r"] = _np.concatenate([i["w_rg"], i["w_re"]], axis=2)
    arrays = {f"in_{n}": _np.ascontiguousarray(v) for n, v in arrays.items()}
    nc = _bacc.Bacc("TRN2", target_bir_lowering=False, num_devices=1)
    aps = {n[3:]: nc.dram_tensor(n, v.shape, _mybir.dt.from_np(v.dtype), kind="ExternalInput").ap() for n, v in arrays.items()}
    aps["out"] = nc.dram_tensor("out_h", (1, SEQ, DM), F32, kind="ExternalOutput").ap()
    program(nc, aps)
    r = _run(nc, [arrays], core_ids=[0])
    return r.results[0]["out_h"]
```

```python
from contextlib import ExitStack

import numpy as np

import concourse.bass as bass
from concourse import mybir

F32 = mybir.dt.float32
F32R = mybir.dt.float32r
I32 = mybir.dt.int32
U32 = mybir.dt.uint32
ALU = mybir.AluOpType
ACT = mybir.ActivationFunctionType
AX = mybir.AxisListType

P = 128
DM = 1024
KD = DM // P
META = 16
SEQ = 512
L = META + SEQ
HALF = L // 2
NT = 5
TOK = [(0, META)] + [(META + P * i, P) for i in range(4)]
DEPTH = 2
ALPHA = (2.0 * DEPTH) ** 0.25
EPS = 1e-5
NEG = -1e30
LOW = -3e38

DIN = 7440
COL = {"aq": 0, "ak": 512, "av": 1024, "bq": 1536, "bkv": 2048, "cq": 2304, "ck": 2816, "cv": 3328,
       "co": 3840, "cg": 4352, "gz": 4368}
QSCALE = 64 ** -0.5
MSCALE = 128 ** -0.5
NE = 32
MAXB = 40
DE = 512

CONST = {}
_at = 0
for _n, _w in (("cos", L), ("sin", L), ("ident", P), ("rot", P), ("mask0", 144), ("mask1", 272),
               ("mask2", 400), ("ltri", P), ("ones", P), ("valid", NT), ("wg4", 4), ("we32", NE),
               ("thr", NT), ("jj", MAXB), ("zero", NE)):
    CONST[_n] = (_at, _w)
    _at += _w
NCONST = _at

ROW = {"gate_b": (0, 16), "b_r": (16, 36), "sink": (52, 8), "lam": (60, 256), "neg_lam_init": (316, 1),
       "one_minus": (317, 1)}
NROW = 318
NCOLP = 24 + 8 + 4 + 1

RING = 0
SLOT = 4096
X = 3 * SLOT
Y = X + 6912
Z = Y + 3 * 4 * L
W = Z + 5392
ARENA = W + 5952
BC = (640, 512)
SAVED = 16 * NT
HTOK = 6 * SLOT + 6656


def program(nc, a):
    ctx = ExitStack()
    with ctx:
        def sb(name, shape, dt=F32):
            return ctx.enter_context(nc.sbuf_tensor(name, shape, dt))

        def sem(name):
            return ctx.enter_context(nc.semaphore(name))

        layer_sems = []

        def lsem(name):
            s = sem(name)
            layer_sems.append(s)
            return s

        xs = nc.dram_tensor("moe_rows", [(MAXB + 1) * P, DM], F32, kind="Internal").ap()
        h_rows = nc.dram_tensor("h_rows", [P, NT, DM], F32, kind="Internal").ap()
        mrow = nc.dram_tensor("mlstm_max_rows", [2, 8, L], F32, kind="Internal").ap()

        arena = sb("arena", [P, ARENA])
        arena_at = int(nc.sbuf_base) - 4 * ARENA
        hT_hi = sb("hT_hi", [P, KD, L], F32R)
        hT_lo = sb("hT_lo", [P, KD, L], F32R)
        hT = nc.alloc_sbuf_tensor_at("hT", [P, KD, L], F32, offset=int(nc.sbuf_base) - 8 * KD * L)
        w_hi = nc.alloc_sbuf_tensor_at("w_hi", [P, 2, KD, P], F32R, offset=arena_at + 4 * 2 * SLOT)
        raw_hi = nc.alloc_sbuf_tensor_at("raw_hi", [P, 2, L], F32R, offset=arena_at + 4 * (W + 6 * L + 8))
        raw_lo = nc.alloc_sbuf_tensor_at("raw_lo", [P, 2, L], F32R, offset=arena_at + 4 * (W + 8 * L + 8))
        w_lo = nc.alloc_sbuf_tensor_at("w_lo", [P, 2, KD, P], F32R, offset=arena_at + 4 * (2 * SLOT + 2 * KD * P))
        cst = sb("cst", [P, NCONST])
        lngb = sb("lngb", [P, 2, DM])
        rowp = sb("rowp", [P, NROW])
        colp = sb("colp", [P, NCOLP])
        w_r = sb("w_r", [P, KD, 36])
        rot_r = sb("rot_r", [P, P], F32R)
        bn = sb("bn", [P, NT, 48])
        mv = sb("mv", [P, NT, 2])
        rstd = sb("rstd", [P, NT])
        nbias = bn[:, :, 0]
        st = sb("st", [P, 64])
        rs = sb("rs", [P, 2, NT, 8])
        ss = sb("ss", [P, NT, 4, 2])
        ssr = sb("ssr", [P, NT, 4])
        cg = sb("cg", [P, 2, NT, 16])
        gcol = sb("gcol", [P, NT, 32])
        r4 = cg[:, :, :, :].rearrange("p a b c -> p (a b c)")[:, 0:3 * NT * 4].rearrange("p (a b c) -> p a b c", b=NT, c=4)
        lg = sb("lg", [P, NT, 36])
        r5 = sb("r5", [P, 12, NT])
        e32 = sb("e32", [P, 4, NT, NE])
        zeros = e32[:, :, :, :].rearrange("p a b c -> p (a b c)")[:, 0:512]
        n32 = sb("n32", [P, 4, NE])
        dst = sb("dst", [P, NT, 2], U32)
        tab = sb("tab", [1, 3 * MAXB + 2], I32)

        ps = ctx.enter_context(nc.psum_tensor("ps", [P, 8, 512], F32))

        def C(name, rows=P, w=None):
            at, width = CONST[name]
            return cst[0:rows, at:at + (width if w is None else w)]

        def R(name):
            at, width = ROW[name]
            return rowp[:, at:at + width]

        def v(at, *dims):
            n = int(np.prod(dims))
            f = arena[:, at:at + n]
            if len(dims) == 2:
                return f.rearrange("p (a b) -> p a b", b=dims[1])
            if len(dims) == 3:
                return f.rearrange("p (a b c) -> p a b c", b=dims[1], c=dims[2])
            return f

        ident = C("ident")
        slot = [v(RING + SLOT * i, KD, 512) for i in range(2)]
        h_tok = v(HTOK, NT, DM)
        qA, kA, vA = v(X, 4, L), [v(X + 4 * L, 4, L), v(Y + 8 * L, 4, L)], v(X + 8 * L, NT, 512)
        qC, kC, vC = qA, kA[0], v(X + 8 * L, NT, 4, 129)
        merged = v(X, KD, L)
        outT = v(Y, 3, 4, L)
        mb = v(Y + 8 * L, 2, 2, L)
        qB, kB, vB = v(Z, 4, L), [v(Z + 4 * L, 1, L), v(Z + 3280, 1, L)], v(Z + 5 * L, NT, 128)
        sco = v(Z + 3280, 4, L)
        raw = v(W + 4 * L + 4, 2, L)
        t_sin = v(W + 2 * L, 2, L)
        pA = v(W, 2, 2, L)
        ptA = v(W + 4 * L, 2, 4, P)
        ptm = v(W + 4 * L + 1024, 2, P)
        oA = v(W + 4 * L + 1024 + 256, NT, 512)
        sB = v(W, 4, 400)
        ptmB = v(W + 1600, 3, P)
        ptB = v(W + 4 * L, 3, 3, P)
        stB = bn[:, :, :].rearrange("p a b -> p (a b)")[:, 0:80].rearrange("p (t k h) -> p t k h", t=2, h=8)
        oB = v(X, NT, 512)
        sq = v(W, 2, 512)
        craw = v(W, 2, L + 2)
        ctmp = v(W + 2 * (L + 2), 2, L)
        SAT = [[0], [0]]
        for j in range(NT):
            SAT[0].append(SAT[0][-1] + L - TOK[j][0])
        SAT[1][0] = SAT[0][-1]
        for j in range(NT):
            SAT[1].append(SAT[1][-1] + sum(TOK[j]))
        NS = SAT[1][-1]
        sC = [v(W, NS), v(Z, NS)]
        hsum = v(W + NS, NT, 512)
        ROWS = [v(Z + L * i, L) for i in range(6)] + [v(W + 3172 + L * i, L) for i in range(5)]
        LF, LI, ZR, BF, BB, UF, UB, MF, MB, EF, EB = [r[0:8, :] for r in ROWS]
        wbw = [v(X + KD * L, 4, 512), v(Z + 4 * L, 4, 512)]
        sg = v(Z, 2, L)
        tg = v(Z + 2 * L, 2, L)
        yraw = v(Z + 4 * L + 2048, 2, L)
        WSET = 3 * SLOT
        mo = 2 * WSET
        assert mo + 6656 <= HTOK and HTOK + NT * DM <= ARENA and NS <= 3280
        xe = v(mo, DM)
        xeT = v(mo + 1024, KD, P)
        sil = v(mo + 2048, DE)
        hid = v(mo + 2560, DE)
        hidT = v(mo + 3072, 4, P)
        ye = v(mo + 3584, DM)
        gath = v(2 * SLOT + 4096, NT, 2, DM)
        tabf = arena[:, mo + MAXB * NE:mo + MAXB * NE + 128]

        const_in = sem("const_in")
        x_in = [sem(f"x_in{i}") for i in range(NT)]
        xs_zeroed = sem("xs_zeroed")
        ln0_in = sem("ln0_in")
        out_done = sem("out_done")
        scattered = sem("scattered")
        gathered = [sem(f"gathered{i}") for i in range(NT)]
        arrived = sem("arrived")
        go = {e: sem(f"go_{e}") for e in ("pe", "act", "dve", "pool")}

        zero_ready = lsem("zero_ready")
        phase_done = lsem("phase_done")
        pool_last = lsem("pool_last")
        dve_step = lsem("dve_step")
        act_step = lsem("act_step")
        first_in = [sem(f"first_in{i}") for i in range(2)]
        h_saved = sem("h_saved")
        h_back = lsem("h_back")
        k_zeroed = lsem("k_zeroed")
        slot_in = [lsem(f"slot_in{i}") for i in range(2)]
        w_split_hi, w_split_lo = lsem("w_split_hi"), lsem("w_split_lo")
        m_split_hi, m_split_lo = lsem("m_split_hi"), lsem("m_split_lo")
        par_in = lsem("par_in")
        ln2_in = lsem("ln2_in")
        unit_mm = lsem("unit_mm")
        unit_ev = lsem("unit_ev")
        rot_mm = lsem("rot_mm")
        rot_lo = lsem("rot_lo")
        rot_ev = lsem("rot_ev")
        conv_done = lsem("conv_done")
        silu_done = lsem("silu_done")
        a_s, a_m, a_exp, a_comb, a_t, a_tev, a_tmev, a_o, a_oev = [lsem(f"a_{n}") for n in
            ("s", "m", "exp", "comb", "t", "tev", "tmev", "o", "oev")]
        b_s, b_m, b_exp, b_t, b_tev, b_o, b_snk, b_oev = [lsem(f"b_{n}") for n in
            ("s", "m", "exp", "t", "tev", "o", "snk", "oev")]
        g_lf, g_exp, g_ln, g_t, g_rows, g_e, g_t2, g_col = [lsem(f"g_{n}") for n in
            ("lf", "exp", "ln", "t", "rows", "e", "t2", "col")]
        m_out = lsem("m_out")
        m_in = [lsem(f"m_in{i}") for i in range(2)]
        c_qk, c_w, c_mul, c_sel, c_pv, c_post, c_mbused = [lsem(f"c_{n}") for n in
            ("qk", "w", "mul", "sel", "pv", "post", "mbused")]
        n_ready, n_sqrt, n_norm, n_t, n_ev = [lsem(f"n_{n}") for n in ("ready", "sqrt", "norm", "t", "ev")]
        wb_in = [lsem(f"wb_in{i}") for i in range(2)]
        wb_used, gate_mm, gate_sig, gate_tmp, gate_free = [lsem(f"gate_{n}") for n in
            ("wb_used", "mm", "sig", "tmp", "free")]
        y_ev, y_t, y_add = [lsem(f"y_{n}") for n in ("ev", "t", "add")]
        r_mm, r_dst, r_exp, r_exp2, r_cnt, r_rank, r_tab, r_a, r_b = [lsem(f"r_{n}") for n in
            ("mm", "dst", "exp", "exp2", "cnt", "rank", "tab", "a", "b")]
        rows_back = lsem("rows_back")
        wg_in, wu_in, wd_in, xe_in, ys_out = [lsem(f"moe_{n}") for n in ("wg_in", "wu_in", "wd_in", "xe_in", "ys_out")]
        e_xt, e_xtev, e_g, e_u, e_sil, e_hid, e_ht, e_htev, e_dn, e_ye = [lsem(f"e_{n}") for n in
            ("xt", "xtev", "g", "u", "sil", "hid", "ht", "htev", "dn", "ye")]
        FREE = {"pe": [(e_g, 1), (e_u, 1), (e_dn, 1)], "act": [(e_sil, 1)], "dve": [(e_hid, 1), (e_ye, 2)],
                "sp": [(ys_out, 16)]}

        def start_free(eng, who):
            for s, n in FREE[who]:
                eng.sem_inc(s, n)

        l_var, l_sqrt, l_scale, l_x, l_mul, l_add, l_addv, l_t, l_ev, l_lo = [lsem(f"l_{n}") for n in
            ("var", "sqrt", "scale", "x", "mul", "add", "addv", "t", "ev", "lo")]

        LATE = [phase_done, pool_last, dve_step, act_step, ln2_in, rows_back, l_var, l_sqrt, l_scale, l_x, l_mul, l_add, l_addv,
                l_t, l_ev, l_lo]

        UNITS = [(kind, c) for kind, n in (("aq", 4), ("ak", 4), ("av", 4), ("bq", 4), ("bk", 1), ("bv", 1)) for c in range(n)]
        NAB = len(UNITS)
        UNITS += [(kind, c) for kind, n in (("cg", 1), ("cq", 4), ("ck", 4), ("cv", 4), ("co", 4)) for c in range(n)]
        NU = len(UNITS)
        NG = 3 * KD
        WBLOCK = {"aq": 0, "ak": 1, "av": 2, "bq": 3, "bk": 4, "bv": 4, "cg": 4, "cq": 5, "ck": 6, "cv": 7, "co": 8}
        WAT = {"bk": 0, "bv": 1, "cg": 2}
        FIRST = [min(u for u, (k, _) in enumerate(UNITS) if WBLOCK[k] == b) for b in range(9)] + [NU, NU + 4]
        ROPE = {"aq": qA, "ak": kA, "bq": qB, "bk": kB}
        TURN = ("av", "bv", "cv", "cg")
        NROPE = {}
        POST = {}
        for _u, (_k, _) in enumerate(UNITS):
            if _k in ROPE or _k in TURN:
                POST[_u] = len(POST)
            if _k in ROPE:
                NROPE[_u] = len(NROPE)
        IN = {}
        _n = [0, 0]
        for _b in range(2, 9):
            _n[_b % 2] += 32 if _b == 4 else 16
            IN[_b] = _n[_b % 2]
        IN_GZ = [_n[1], _n[0]]

        def chunk_source(q):
            if q < NU:
                kind, c = UNITS[q]
                w = slot[WBLOCK[kind] % 2]
                if kind == "bq":
                    return w.rearrange("p k (g c d) -> p k g c d", g=2, d=64)[:, :, :, c, :]
                c = WAT.get(kind, c)
            else:
                w, c = slot[(1 + (q - NU) // 4) % 2], (q - NU) % 4
            return w[:, :, P * c:P * c + P].rearrange("p k (g d) -> p k g d", d=64)

        def chunk_split(t, q):
            return t[:, q % 2, :, :].rearrange("p k (g d) -> p k g d", d=64)

        def as_f32(t):
            return t.bitcast(F32)

        def halves(bank, rows=P):
            return ps[0:rows, bank:bank + 2, 0:HALF]

        def two(apx):
            return apx.rearrange("p (a b) -> p a b", b=HALF)

        class Phase:

            def __init__(self, eng):
                self.eng, self.n = eng, 0

            def __call__(self):
                self.n += 1
                self.eng.drain().then_inc(phase_done, 1)
                self.eng.wait_ge(phase_done, 3 * self.n)

        def end_layer(eng, who):
            eng.drain().then_inc(arrived, 1)
            eng.wait_ge(go[who], 1)
            eng.sem_clear(go[who])

        def next_layer(sp):
            sp.wait_ge(arrived, 4)
            for s in LATE:
                sp.sem_clear(s)
            sp.sem_clear(arrived)
            for g in go.values():
                sp.sem_inc(g, 1)

        BKEYS = [[(0, 16), (16, 128)], [(0, 272)], [(0, 400)], [(0, 16), (144, 384)], [(0, 16), (272, 256)]]
        BTILES = [[1], [1, 2], [1, 2, 3], [2, 3, 4], [3, 4]]
        BHEAD = [0, 4, 1, 5, 2, 6, 3, 7]
        QKB = (0, 3)
        ASTEPS = [(0, None)] + [(i, h) for i in range(1, NT) for h in range(4)]
        TB = (7, 1, 0)
        BMASK = ["mask0", "mask1", "mask2", "mask2", "mask2"]
        bwidth = [sum(n for _, n in k) for k in BKEYS]

        block = ctx.enter_context(nc.Block())

        @block.sync
        def _(sp):
            sp.dma_start(h_tok[0:META, 0, :], a["meta"]).then_inc(x_in[0], 16)
            for i in range(1, NT):
                sp.dma_start(h_tok[:, i, :], a["x"][0, P * (i - 1):P * i, :]).then_inc(x_in[i], 16)
            sp.dma_start(lngb[:, 0, :], a["ln_in_g"].partition_broadcast(P)).then_inc(ln0_in, 16)
            sp.dma_start(lngb[:, 1, :], a["ln_in_b"].partition_broadcast(P)).then_inc(ln0_in, 16)
            sp.dma_start(cst[:, :], a["consts"]).then_inc(const_in, 16)

            def first_blocks(l):
                for i, kind in enumerate(("aq", "ak")):
                    sp.dma_start(slot[i][:, :, :], a["w_in"][bass.ds(l, 1)].rearrange("o (k p) n -> (o p) k n", p=P)
                                 [:, :, COL[kind]:COL[kind] + 512]).then_inc(first_in[i], 16)

            def each_row_tile(norm):
                for i in range(NT):
                    sp.wait_ge(l_add, norm * NT + i + 1)
                    sp.wait_ge(l_addv, norm * NT + i + 1)
                    yield i, TOK[i][1]

            def save_rows(norm):
                for i, n in each_row_tile(norm):
                    sp.dma_start(h_rows[0:n, i, :], h_tok[0:n, i, :]).then_inc(h_saved, 16)

            first_blocks(0)
            save_rows(0)
            next_layer(sp)
            with sp.Fori(0, DEPTH) as l:
                def lay(t, pat, **kw):
                    return t[bass.ds(l, 1)].rearrange("o " + pat, **kw)

                sp.dma_start(rowp[:, :], a["rowp"][bass.ds(l, 1), :].broadcast_to([P, NROW])).then_inc(par_in, 16)
                sp.dma_start(colp[:, :], lay(a["colp"], "p n -> (o p) n")).then_inc(par_in, 16)
                sp.dma_start(w_r[:, :, :], lay(a["w_r"], "(k p) n -> (o p) k n", p=P)).then_inc(par_in, 16)
                for i, n in enumerate(("ln1_g", "ln1_b")):
                    sp.dma_start(lngb[:, i, :], a[n][bass.ds(l, 1), :].broadcast_to([P, DM])).then_inc(par_in, 16)

                def w_cols(at, n):
                    return lay(a["w_in"], "(k p) n -> (o p) k n", p=P)[:, :, at:at + n]

                for n, kind in enumerate(("aq", "ak", "av", "bq", "bkv", "cq", "ck", "cv", "co")):
                    if n < 2:
                        continue
                    sp.wait_ge(w_split_lo, FIRST[n - 1])
                    if kind == "bkv":
                        sp.dma_start(slot[n % 2][:, :, 0:256], w_cols(COL["bkv"], 256)).then_inc(slot_in[n % 2], 16)
                        sp.dma_start(slot[n % 2][:, :, 256:384], w_cols(COL["cg"], P)).then_inc(slot_in[n % 2], 16)
                    else:
                        sp.dma_start(slot[n % 2][:, :, :], w_cols(COL[kind], 512)).then_inc(slot_in[n % 2], 16)
                    if n != 5:
                        continue
                    with sp.If(l < 1):
                        sp.wait_ge(zero_ready, 1)
                        for hf in range(2):
                            sp.dma_start(xs.rearrange("(b p) n -> p b n", p=P)[:, :, 512 * hf:512 * hf + 512],
                                         zeros.unsqueeze(1).broadcast_to([P, MAXB + 1, 512])).then_inc(xs_zeroed, 16)

                def load_gz(t, hf):
                    sp.wait_ge(w_split_lo, t * 8 + (FIRST[8] + 4 * hf))
                    sp.dma_start(slot[1 - hf][:, :, :],
                                 lay(a["w_in"], "(k p) n -> (o p) k n", p=P)[:, :, bass.ds(t * 1024 + (COL["gz"] + 512 * hf), 512)]
                                 ).then_inc(slot_in[1 - hf], 16)

                def load_wb(t, hf):
                    wb = a["w_branch"].rearrange("l b (k p) n -> (l b) p k n", p=P)
                    sp.dma_start(wbw[hf][:, :, :],
                                 wb[bass.ds(l * 3 + t, 1), :, :, 512 * hf:512 * hf + 512].rearrange("o p k n -> (o p) k n")
                                 ).then_inc(wb_in[hf], 16)

                def load_max(h):
                    for d in range(2):
                        sp.dma_start(mb[:, h % 2, d, :],
                                     mrow[d, 4 * d + h:4 * d + h + 1, :].broadcast_to([P, L])).then_inc(m_in[h % 2], 16)

                load_gz(0, 0)
                sp.wait_ge(g_rows, 1)
                sp.dma_start(mrow[0], MF).then_inc(m_out, 16)
                sp.dma_start(mrow[1], MB).then_inc(m_out, 16)
                sp.wait_ge(m_out, 32)
                load_max(0)
                load_max(1)
                load_gz(0, 1)
                for h in (2, 3):
                    sp.wait_ge(c_mbused, h - 1)
                    load_max(h)
                sp.wait_ge(c_pv, 4 * NT)
                load_wb(0, 0)
                sp.wait_ge(n_ev, 3 * NT)
                load_wb(0, 1)
                sp.dma_start(h_tok[0:META, 0, :], h_rows[0:META, 0, :]).then_inc(h_back, 16)
                sp.dma_start(h_tok[:, 1:NT, :], h_rows[:, 1:NT, :]).then_inc(h_back, 16)
                with sp.Fori(1, 3) as t:
                    for hf in range(2):
                        load_gz(t, hf)
                        sp.wait_ge(wb_used, t * 2 + (hf - 1))
                        load_wb(t, hf)
                wo = lay(a["w_out"], "(k p) n -> (o p) k n", p=P)
                for hf in range(2):
                    sp.wait_ge(w_split_lo, NU + NG - 4 + 4 * hf)
                    sp.dma_start(slot[1 - hf][:, :, :], wo[:, :, 512 * hf:512 * hf + 512]).then_inc(slot_in[1 - hf], 16)

                sp.wait_ge(l_add, NT)
                sp.wait_ge(l_addv, NT)
                sp.wait_ge(l_mul, NT)
                for i, n in enumerate(("ln2_g", "ln2_b")):
                    sp.dma_start(lngb[:, i, :], a[n][bass.ds(l, 1), :].broadcast_to([P, DM])).then_inc(ln2_in, 16)

                start_free(sp, "sp")
                sp.wait_ge(r_tab, 1)
                nb = sp.value_load(tab[0:1, MAXB:MAXB + 1], min_val=9, max_val=MAXB)
                wg3 = a["w_gate"].rearrange("l e (k p) n -> (l e) p k n", p=P)
                wu3 = a["w_up"].rearrange("l e (k p) n -> (l e) p k n", p=P)
                wd3 = a["w_down"].rearrange("l e (k p) n -> (l e) p k n", p=P)

                def load_rows(j):
                    sp.dma_start(xe, xs[bass.ds(j * P, P), :]).then_inc(xe_in, 16)

                def load_w(o, part, e, source, done):
                    sp.dma_start(arena[:, bass.ds((o % 2) * WSET + part * SLOT, SLOT)].rearrange("p (k n) -> p k n", n=(DE, DE, DM)[part]),
                                 source[bass.ds(e, 1)].rearrange("o p k n -> (o p) k n")).then_inc(done, 16)

                def store_rows(j):
                    sp.dma_start(xs[bass.ds(j * P, P), :], ye).then_inc(ys_out, 16)

                e0 = l * NE + sp.value_load(tab[0:1, 0:1], min_val=0, max_val=NE - 1)
                for part, (source, done) in enumerate(((wg3, wg_in), (wu3, wu_in), (wd3, wd_in))):
                    sp.dma_start(arena[:, part * SLOT:(part + 1) * SLOT].rearrange("p (k n) -> p k n", n=(DE, DE, DM)[part]),
                                 source[bass.ds(e0, 1)].rearrange("o p k n -> (o p) k n")).then_inc(done, 16)
                    if part == 0:
                        sp.wait_ge(scattered, l * 160 + 160)
                        sp.dma_start(xe, xs[0:P, :]).then_inc(xe_in, 16)

                def load_block(i):
                    sp.wait_ge(e_xt, i + 1)
                    load_rows(i + 1)
                    first = sp.value_load(tab[0:1, bass.ds(i + (2 * MAXB + 2), 1)], min_val=0, max_val=1)
                    with sp.If(first > 0):
                        e = l * NE + sp.value_load(tab[0:1, bass.ds(i + 1, 1)], min_val=0, max_val=NE - 1)
                        o = sp.value_load(tab[0:1, bass.ds(i + (MAXB + 2), 1)], min_val=1, max_val=NE - 1)
                        sp.wait_ge(wg_in, o * 16)
                        sp.wait_ge(e_g, i + 1)
                        load_w(o, 0, e, wg3, wg_in)
                        sp.wait_ge(wu_in, o * 16)
                        sp.wait_ge(e_u, i + 1)
                        load_w(o, 1, e, wu3, wu_in)
                        sp.wait_ge(wd_in, o * 16)
                        sp.wait_ge(e_dn, i + 1)
                        load_w(o, 2, e, wd3, wd_in)

                load_block(0)
                with sp.Fori(1, nb - 1) as i:
                    load_block(i)
                    sp.wait_ge(e_ye, i * 2 + 2)
                    store_rows(i - 1)
                sp.wait_ge(e_xt, nb)
                load_rows(nb)
                sp.wait_ge(e_ye, nb * 2)
                store_rows(nb - 2)
                sp.wait_ge(e_ye, nb * 2 + 2)
                store_rows(nb - 1)
                sp.wait_ge(ys_out, nb * 16 + 16)
                sp.sem_inc(rows_back, 1)
                sp.wait_ge(phase_done, 3 * 10)
                sp.wait_ge(pool_last, 1)
                for s in layer_sems:
                    if s not in LATE:
                        sp.sem_clear(s)
                with sp.If(l < DEPTH - 1):
                    sp.wait_ge(gathered[NT - 1], l * 32 + 32)
                    first_blocks(nc.s_assert_within(l + 1, min_val=1, max_val=DEPTH - 1,
                        skip_runtime_bounds_check_because="this branch runs only where l < DEPTH - 1"))
                    save_rows(1)
                with sp.If(l > DEPTH - 2):
                    for i, n in each_row_tile(1):
                        if i > 0:
                            sp.dma_start(a["out"][0, P * (i - 1):P * i, :], h_tok[:, i, :]).then_inc(out_done, 16)
                next_layer(sp)
            sp.wait_ge(out_done, 16 * (NT - 1))
            sp.wait_ge(h_saved, SAVED * DEPTH)

        @block.gpsimd
        def _(pool):
            def add_bias(i, n, cols):
                return pool.tensor_tensor(h_tok[0:n, i, 0:cols], h_tok[0:n, i, 0:cols], lngb[0:n, 1, 0:cols], ALU.add)

            def norm_bias():
                for i, (_, n) in enumerate(TOK):
                    pool.wait_ge(l_mul, i + 1)
                    add_bias(i, n, BC[0]).then_inc(l_add, 1)

            pool.wait_ge(ln0_in, 32)
            norm_bias()
            end_layer(pool, "pool")
            with pool.Fori(0, DEPTH) as l:
                for keys in (kA, kB):
                    for g in range(2):
                        half = slice(64 - 64 * g, 128 - 64 * g)
                        pool.memset(keys[g][half, :, :], 0.0)
                pool.drain().then_inc(k_zeroed, 1)
                pool.wait_ge(par_in, 80)
                for h in range(4):
                    for j, (t0, n) in enumerate(TOK):
                        for d in range(2):
                            pool.wait_ge(c_mul, 2 * (NT * h + j) + d + 1)
                            at = SAT[d][j] + (0 if d == 0 else t0)
                            blk = sC[h % 2][0:n, at:at + n]
                            sgn = 1 if d == 0 else -1
                            pool.affine_select(out=blk, in_=blk, compare_op=ALU.is_ge, fill=0.0, base=0,
                                               pattern=[[sgn, n]], channel_multiplier=-sgn).then_inc(c_sel, 1)
                pool.wait_ge(par_in, 80)
                for i, (_, n) in enumerate(TOK):
                    pool.wait_ge(l_mul, i + 1)
                    add_bias(i, n, BC[1]).then_inc(l_add, 1)
                pool.wait_ge(xs_zeroed, 32)
                pool.wait_ge(l_add, NT)
                pool.wait_ge(l_addv, NT)
                pool.wait_ge(r_dst, 1)
                for i, (_, n) in enumerate(TOK):
                    for k in range(2):
                        pool.indirect_dma_start(
                            out=xs, out_offset=bass.IndirectOffsetOnAxis(ap=dst[0:n, i, k:k + 1], axis=0),
                            in_=h_tok[0:n, i, :], in_offset=None).then_inc(scattered, 16)
                pool.wait_ge(rows_back, 1)
                pool.wait_ge(phase_done, 3 * 10)
                pool.sem_inc(pool_last, 1)
                for i, (_, n) in enumerate(TOK):
                    for k in range(2):
                        pool.indirect_dma_start(
                            out=gath[0:n, i, k, :], out_offset=None, in_=xs,
                            in_offset=bass.IndirectOffsetOnAxis(ap=dst[0:n, i, k:k + 1], axis=0)).then_inc(gathered[i], 16)
                pool.wait_ge(ln2_in, 32)
                for i, (_, n) in enumerate(TOK):
                    pool.wait_ge(l_mul, NT + i + 1)
                    add_bias(i, n, BC[0]).then_inc(l_add, 1)
                end_layer(pool, "pool")

        @block.tensor
        def _(pe):
            def norm_transposes(first, split, then=None):
                for i, (t0, n) in enumerate(TOK):
                    pe.wait_ge(l_add, first + i + 1)
                    pe.wait_ge(l_addv, first + i + 1)
                    if i >= 2:
                        pe.wait_ge(l_lo if split else l_ev, i - 1)
                    for k in range(KD):
                        mm = pe.transpose(ps[:, 4 + 2 * (i % 2) + k // 4, P * (k % 4):P * (k % 4) + n],
                                          h_tok[0:n, i, P * k:P * k + P], ident[0:n, 0:n])
                    mm.then_inc(l_t, 1)
                    if then and i >= 1:
                        then(i - 1)
                if then:
                    then(NT - 1)

            def product(bank, q, before=None):
                for k in range(KD):
                    if before:
                        before(k)
                    for x, (w, h) in enumerate(((w_hi, hT_hi), (w_hi, hT_lo), (w_lo, hT_hi))):
                        for b in range(2):
                            mm = pe.matmul(ps[:, bank + b, 0:HALF], w[:, q % 2, k, :], h[:, k, HALF * b:HALF * b + HALF],
                                           start=(k == 0 and x == 0), stop=(k == KD - 1 and x == 2))
                mm.then_inc(unit_mm, 1)

            def unit(u):
                if u >= 2:
                    pe.wait_ge(unit_ev, u - 1)
                pe.wait_ge(w_split_lo, u + 1)
                product(2 * (u % 2), u)

            def turn_rows(bank, src, rows=P):
                for j in range(1, NT):
                    t0 = TOK[j][0]
                    pe.transpose(ps[:, bank, P * (j - 1):P * (j - 1) + rows], src[0:rows, t0:t0 + P], ident[0:rows, 0:rows])
                return pe.transpose(ps[0:META, bank + 1, 0:rows], src[0:rows, 0:META], ident[0:rows, 0:rows])

            def post(u):
                r = POST[u]
                bank = 4 + 2 * (r % 2)
                pe.wait_ge(unit_ev, u + 1)
                if r >= 2:
                    pe.wait_ge(rot_ev, r - 1)
                if UNITS[u][0] in ROPE:
                    pe.wait_ge(rot_lo, NROPE[u] + 1)
                    for b in range(2):
                        for x, part in enumerate((raw_hi, raw_lo)):
                            mm = pe.matmul(ps[:, bank + b, 0:HALF], rot_r[:, :], part[:, r % 2, HALF * b:HALF * b + HALF],
                                           start=(x == 0), stop=(x == 1))
                else:
                    mm = turn_rows(bank, raw[:, r % 2, :], META if UNITS[u][0] == "cg" else P)
                mm.then_inc(rot_mm, 1)

            def units(lo, hi, extra):
                for u in range(lo, hi):
                    if u != NAB:
                        unit(u)
                    if u - 1 in POST and u - 1 >= lo:
                        post(u - 1)
                    if u in extra:
                        extra[u]()
                if hi - 1 in POST:
                    post(hi - 1)

            def attention_a():
                def scores(n, c):
                    i, h = ASTEPS[n]
                    if h is None:
                        for h in range(4):
                            for hf in range(2):
                                mm = pe.matmul(ps[32 * h:32 * h + 32, 3 + 2 * c + hf, 0:HALF], qA[:, h, 0:32],
                                               kA[c][:, h, HALF * hf:HALF * hf + HALF], start=True, stop=True)
                        mm.then_inc(a_s, 1)
                        return
                    t0, m = TOK[i]
                    pe.wait_ge(a_exp, 2 * n + c - 1)
                    for hf in range(2):
                        mm = pe.matmul(ps[0:m, 3 + 2 * c + hf, 0:HALF], qA[:, h, t0:t0 + m],
                                       kA[c][:, h, HALF * hf:HALF * hf + HALF], start=True, stop=True)
                    mm.then_inc(a_s, 1)

                def turn(n):
                    m = P
                    pe.wait_ge(a_comb, n + 1)
                    if n >= 2:
                        pe.wait_ge(a_tev, n - 1)
                        pe.wait_ge(a_tmev, n - 1)
                    prob = pA[0:m, n % 2, 0, :]
                    for j in range(1, NT):
                        pe.transpose(ps[:, (7, 1)[n % 2], P * (j - 1):P * (j - 1) + m],
                                     prob[:, TOK[j][0]:TOK[j][0] + P], ident[0:m, 0:m])
                    pe.transpose(ps[0:META, 0, P * (n % 2):P * (n % 2) + m], prob[:, 0:META], ident[0:m, 0:m]).then_inc(a_t, 1)

                def values(n):
                    i, h = ASTEPS[n]
                    m = TOK[i][1]
                    pe.wait_ge(a_tev, n + 1)
                    pe.wait_ge(a_tmev, n + 1)
                    if h is None:
                        for h in range(4):
                            o, rows = ps[0:m, 2, P * h:P * h + P], slice(32 * h, 32 * h + m)
                            for j in range(1, NT):
                                pe.matmul(o, ptA[:, 0, j - 1, rows], vA[:, j, P * h:P * h + P], start=(j == 1), stop=False)
                            mm = pe.matmul(o, ptm[0:META, 0, rows], vA[0:META, 0, P * h:P * h + P], start=False, stop=True)
                        mm.then_inc(a_o, 1)
                        return
                    if h == 0 and i >= 1:
                        pe.wait_ge(a_oev, i)
                    o = ps[0:m, 2, P * h:P * h + P]
                    for j in range(1, NT):
                        pe.matmul(o, ptA[:, n % 2, j - 1, 0:m], vA[:, j, P * h:P * h + P], start=(j == 1), stop=False)
                    pe.matmul(o, ptm[0:META, n % 2, 0:m], vA[0:META, 0, P * h:P * h + P],
                              start=False, stop=True).then_inc(a_o, 1)

                N = len(ASTEPS)
                scores(0, 0)
                scores(0, 1)
                for n in range(N):
                    if n + 1 < N:
                        scores(n + 1, 0)
                    if n >= 1:
                        values(n - 1)
                    if n + 1 < N:
                        scores(n + 1, 1)
                    turn(n)
                values(N - 1)

            def attention_b():
                def scores(n):
                    i, h = n // 8, BHEAD[n % 8]
                    t0, m = TOK[i]
                    if n >= 4:
                        pe.wait_ge(b_m, n - 3)
                    at = 0
                    for k0, w in BKEYS[i]:
                        mm = pe.matmul(ps[0:m, 3 + n % 4, at:at + w], qB[:, h % 4, t0:t0 + m],
                                       kB[h // 4][:, 0, k0:k0 + w], start=True, stop=True)
                        at += w
                    mm.then_inc(b_s, 1)

                def turn(n):
                    i = n // 8
                    m = TOK[i][1]
                    pe.wait_ge(b_exp, n + 1)
                    if n >= 3:
                        pe.wait_ge(b_tev, n - 2)
                    bank = TB[n % 3]
                    for x, j in enumerate(BTILES[i]):
                        pe.transpose(ps[:, bank, P * x:P * x + m],
                                     sB[0:m, n % 4, META + P * x:META + P * x + P], ident[0:m, 0:m])
                    pe.transpose(ps[0:META, bank, 3 * P:3 * P + m], sB[0:m, n % 4, 0:META], ident[0:m, 0:m]).then_inc(b_t, 1)

                def values(n):
                    i, h = n // 8, BHEAD[n % 8]
                    m, g = TOK[i][1], h // 4
                    pe.wait_ge(b_tev, n + 1)
                    if n % 8 == 0 and i >= 1:
                        pe.wait_ge(b_oev, i)
                    o = ps[0:m, 2, 64 * h:64 * h + 64]
                    for x, j in enumerate(BTILES[i]):
                        pe.matmul(o, ptB[:, n % 3, x, 0:m], vB[:, j, 64 * g:64 * g + 64], start=(x == 0), stop=False)
                    pe.matmul(o, ptmB[0:META, n % 3, 0:m], vB[0:META, 0, 64 * g:64 * g + 64],
                              start=False, stop=True).then_inc(b_o, 1)

                N = 8 * NT
                for n in range(4):
                    scores(n)
                for n in range(N):
                    if n + 4 < N:
                        scores(n + 4)
                    turn(n)
                    if n >= 2:
                        values(n - 2)
                values(N - 2)
                values(N - 1)

            def branch_transposes(src, first, want):
                for i, (_, n) in enumerate(TOK):
                    want(i)
                    q = first + i
                    if q >= 4:
                        pe.wait_ge(n_ev, q - 3)
                    for c in range(4):
                        mm = pe.transpose(ps[:, 4 + q % 4, P * c:P * c + n], src[0:n, i, P * c:P * c + P], ident[0:n, 0:n])
                    mm.then_inc(n_t, 1)

            def gate_rows():
                pe.wait_ge(g_lf, 1)
                for i, (t0, n) in enumerate(TOK):
                    for kind in range(2):
                        bank, at = (4 + 2 * kind, t0) if i < 4 else (5 + 2 * kind, 0)
                        mm = pe.transpose(ps[0:8, bank, at:at + n], cg[0:n, 1, i, 8 * kind:8 * kind + 8], ident[0:n, 0:n])
                mm.then_inc(g_t, 1)

            def gate_columns():
                pe.wait_ge(g_e, 1)
                pe.wait_ge(g_rows, 1)
                for i, (t0, n) in enumerate(TOK):
                    for x, row in enumerate((UF, UB, EF, EB)):
                        mm = pe.transpose(ps[0:n, 4, 32 * i + 8 * x:32 * i + 8 * x + 8], row[:, t0:t0 + n], ident[0:8, 0:8])
                mm.then_inc(g_t2, 1)

            def mlstm():
                def qk(h, j):
                    q = NT * h + j
                    t0, n = TOK[j]
                    if q >= 2:
                        pe.wait_ge(c_mul, 2 * (q - 1))
                    b = QKB[q % 2]
                    pe.matmul(ps[0:n, b, 0:272], kC[:, h, t0:t0 + n], qC[:, h, 0:272], start=True, stop=True)
                    pe.matmul(ps[0:n, b + 1, 0:256], kC[:, h, t0:t0 + n], qC[:, h, 272:L],
                              start=True, stop=True).then_inc(c_qk, 1)

                def values(h, i):
                    q = NT * h + i
                    t0, m = TOK[i]
                    if i == 0:
                        pe.wait_ge(c_sel, 2 * NT * (h + 1))
                    if q >= 2:
                        pe.wait_ge(c_post, q - 1)
                    bank = 5 + q % 2
                    for d, js in enumerate((range(i + 1), range(i, NT))):
                        for x, j in enumerate(js):
                            n = TOK[j][1]
                            at = SAT[d][j] + t0 - (TOK[j][0] if d == 0 else 0)
                            mm = pe.matmul(ps[0:m, bank, 256 * d:256 * d + 129], sC[h % 2][0:n, at:at + m],
                                           vC[0:n, j, h, :], start=(x == 0), stop=(x == len(js) - 1))
                    mm.then_inc(c_pv, 1)

                for h in range(5):
                    for j in range(NT):
                        if h < 4:
                            qk(h, j)
                        if h >= 1:
                            values(h - 1, j)

            def gates():
                with pe.Fori(0, 3) as t:
                    for hf in range(2):
                        for c in range(4):
                            u = 4 * hf + c
                            s = 4 * (u % 2)
                            if u == 0:
                                with pe.If(t > 0):
                                    pe.wait_ge(gate_free, t * 8 + (u + 1))
                                    pe.wait_ge(w_split_lo, t * 8 + (NU + u + 1))
                                    product(s, NU + u)
                            else:
                                pe.wait_ge(gate_free, t * 8 + (u + 1))
                                pe.wait_ge(w_split_lo, t * 8 + (NU + u + 1))
                                product(s, NU + u)
                            if c == 0:
                                pe.wait_ge(wb_in[hf], t * 16 + 16)
                            for b in range(2):
                                for k in range(4):
                                    mm = pe.matmul(ps[:, s + 2 + b, 0:HALF], wbw[hf][:, k, P * c:P * c + P],
                                                   arena[:, bass.ds(t * (4 * L) + (Y + k * L + HALF * b), HALF)],
                                                   start=(k == 0), stop=(k == 3))
                            mm.then_inc(gate_mm, 1)
                        pe.drain().then_inc(wb_used, 1)

            def project_out():
                def turn(m):
                    pe.wait_ge(y_ev, m + 1)
                    if m >= 2:
                        pe.wait_ge(y_add, m - 1)
                    turn_rows(4 + 2 * (m % 2), yraw[:, m % 2, :]).then_inc(y_t, 1)

                for m in range(KD):
                    if m >= 2:
                        pe.wait_ge(y_ev, m - 1)
                    pe.wait_ge(w_split_lo, NU + NG + m + 1)
                    product(2 * (m % 2), NU + NG + m, (lambda k: pe.wait_ge(m_split_lo, k + 1)) if m == 0 else None)
                    if m >= 1:
                        turn(m - 1)
                turn(KD - 1)

            def logits(i):
                t0, n = TOK[i]
                pe.wait_ge(l_ev, i + 1)
                for k in range(KD):
                    mm = pe.matmul(ps[0:n, 0, 36 * i:36 * i + 36], hT[:, k, t0:t0 + n], w_r[:, k, :],
                                   start=(k == 0), stop=(k == KD - 1))
                mm.then_inc(r_mm, 1)

            def router():
                pe.wait_ge(r_cnt, 1)
                rank = ps[:, 1, 0:NE * NT]
                pe.matmul(rank, C("ltri"), e32[:, 2, :, :].rearrange("p t e -> p (t e)"), start=True, stop=False)
                pe.matmul(rank, C("ones"), e32[:, 3, :, :].rearrange("p t e -> p (t e)"), start=False, stop=True)
                mm = pe.matmul(ps[:, 1, NE * NT:NE * NT + NE], C("ones"), n32[:, 3, :], start=True, stop=True)
                mm.then_inc(r_rank, 1)

            def experts():
                start_free(pe, "pe")
                pe.wait_ge(r_tab, 1)
                nb = pe.value_load(tab[0:1, MAXB:MAXB + 1], min_val=9, max_val=MAXB)

                def rows_turn():
                    for k in range(KD):
                        mm = pe.transpose(ps[:, 2 + k // 4, P * (k % 4):P * (k % 4) + P], xe[:, P * k:P * k + P], ident)
                    mm.then_inc(e_xt, 1)

                def weights(o, part, at, n):
                    if isinstance(o, int):
                        return arena[:, (o % 2) * WSET + part * SLOT + at:(o % 2) * WSET + part * SLOT + at + n]
                    return arena[:, bass.ds((o % 2) * WSET + (part * SLOT + at), n)]

                def gate(o):
                    for k in range(KD):
                        mm = pe.matmul(ps[:, 0, :], xeT[:, k, :], weights(o, 0, DE * k, DE), start=(k == 0), stop=(k == KD - 1))
                    mm.then_inc(e_g, 1)

                def up(o):
                    for k in range(KD):
                        mm = pe.matmul(ps[:, 1, :], xeT[:, k, :], weights(o, 1, DE * k, DE), start=(k == 0), stop=(k == KD - 1))
                    mm.then_inc(e_u, 1)

                def hid_turn():
                    for c in range(4):
                        mm = pe.transpose(ps[:, 4, P * c:P * c + P], hid[:, P * c:P * c + P], ident)
                    mm.then_inc(e_ht, 1)

                def down(o):
                    for hf in range(2):
                        for k in range(4):
                            mm = pe.matmul(ps[:, 5 + hf, :], hidT[:, k, :], weights(o, 2, DM * k + 512 * hf, 512),
                                           start=(k == 0), stop=(k == 3))
                    mm.then_inc(e_dn, 1)

                pe.wait_ge(xe_in, 16)
                rows_turn()
                pe.wait_ge(e_xtev, 1)
                pe.wait_ge(wg_in, 16)
                gate(0)
                pe.wait_ge(wu_in, 16)
                up(0)
                pe.wait_ge(xe_in, 32)
                rows_turn()
                with pe.Fori(1, nb) as j:
                    o = pe.value_load(tab[0:1, bass.ds(j + (MAXB + 1), 1)], min_val=0, max_val=NE - 1)
                    pe.wait_ge(e_xtev, j + 1)
                    pe.wait_ge(e_sil, j + 1)
                    pe.wait_ge(wg_in, o * 16 + 16)
                    gate(o)
                    pe.wait_ge(e_hid, j + 1)
                    hid_turn()
                    pe.wait_ge(wu_in, o * 16 + 16)
                    up(o)
                    pe.wait_ge(xe_in, j * 16 + 32)
                    rows_turn()
                    o1 = pe.value_load(tab[0:1, bass.ds(j + MAXB, 1)], min_val=0, max_val=NE - 1)
                    pe.wait_ge(e_htev, j)
                    pe.wait_ge(wd_in, o1 * 16 + 16)
                    pe.wait_ge(e_ye, j * 2)
                    down(o1)
                last = pe.value_load(tab[0:1, bass.ds(nb + MAXB, 1)], min_val=0, max_val=NE - 1)
                pe.wait_ge(e_hid, nb + 1)
                hid_turn()
                pe.wait_ge(e_htev, nb)
                pe.wait_ge(wd_in, last * 16 + 16)
                pe.wait_ge(e_ye, nb * 2)
                down(last)

            pe.wait_ge(const_in, 16)
            norm_transposes(0, True)
            end_layer(pe, "pe")
            with pe.Fori(0, DEPTH) as l:
                phase = Phase(pe)
                units(0, NAB, {})
                phase()
                pe.wait_ge(k_zeroed, 1)
                attention_a()
                phase()
                attention_b()
                pe.wait_ge(b_tev, 8 * NT)
                unit(NAB)
                phase()
                branch_transposes(oA, 0, lambda i: pe.wait_ge(n_norm, i + 1))
                branch_transposes(oB, NT, lambda i: pe.wait_ge(b_oev, NT))
                phase()

                def rows_then_v():
                    pe.wait_ge(g_rows, 1)

                def columns():
                    pe.wait_ge(rot_ev, len(POST))
                    gate_columns()

                units(NAB, NU, {NAB + 2: gate_rows, UNITS.index(("cv", 0)): rows_then_v, UNITS.index(("co", 1)): columns})
                phase()
                mlstm()
                phase()
                pe.wait_ge(w_split_lo, NU + 1)
                product(0, NU)
                branch_transposes(hsum, 2 * NT, lambda i: pe.wait_ge(n_norm, NT + i + 1))
                phase()
                gates()
                phase()
                project_out()
                norm_transposes(0, False, logits)
                router()
                phase()
                experts()
                phase()
                norm_transposes(NT, True)
                end_layer(pe, "pe")

        @block.scalar
        def _(act):
            steps = [0]

            def link(ins):
                steps[0] += 1
                ins.then_inc(act_step, 1)
                act.wait_ge(act_step, steps[0])

            def norm_root(n):
                act.wait_ge(l_var, n)
                act.activation(rstd[:, :], rstd[:, :], ACT.Sqrt).then_inc(l_sqrt, 1)
                act.wait_ge(l_scale, n)
                for i, (_, m) in enumerate(TOK):
                    act.activation(h_tok[0:m, i, :], h_tok[0:m, i, :], ACT.Identity, bias=nbias[0:m, i:i + 1],
                                   scale=rstd[0:m, i:i + 1]).then_inc(l_x, 1)

            def norm_evacuate(first, to):
                for i, (t0, n) in enumerate(TOK):
                    act.wait_ge(l_t, first + i + 1)
                    b = 4 + 2 * (i % 2)
                    act.activation(to[:, 0:4, t0:t0 + n], ps[:, b, :].rearrange("p (k n) -> p k n", n=P)[:, :, 0:n], ACT.Copy)
                    act.activation(to[:, 4:8, t0:t0 + n], ps[:, b + 1, :].rearrange("p (k n) -> p k n", n=P)[:, :, 0:n],
                                   ACT.Copy).then_inc(l_ev, 1)

            def split(q):
                if q < NU:
                    b = WBLOCK[UNITS[q][0]]
                    if b >= 2 and q == FIRST[b]:
                        act.wait_ge(slot_in[b % 2], IN[b])
                elif q == NU:
                    act.wait_ge(slot_in[1], IN_GZ[0] + 16)
                act.activation(chunk_split(w_hi, q), chunk_source(q), ACT.Copy).then_inc(w_split_hi, 1)

            def evacuate(u):
                kind, c = UNITS[u]
                bank = halves(2 * (u % 2))
                act.wait_ge(unit_mm, u + 1)
                if u in POST:
                    r = POST[u]
                    if r >= 2:
                        act.wait_ge(rot_ev, r - 1)
                    scale = QSCALE if kind in ("aq", "bq") else 1.0
                    if u in NROPE:
                        act.activation(two(raw_hi[:, r % 2, :]), bank, ACT.Copy, scale=scale)
                    act.activation(two(raw[:, r % 2, :]), bank, ACT.Copy, scale=scale).then_inc(unit_ev, 1)
                elif kind in ("cq", "ck"):
                    ch = c + 4 * (kind == "ck")
                    if ch >= 2:
                        act.wait_ge(conv_done, ch - 1)
                    act.activation(two(craw[:, ch % 2, 1:1 + L]), bank, ACT.Copy).then_inc(unit_ev, 1)
                else:
                    act.activation(two(sco[:, c, :]), bank, ACT.Sigmoid).then_inc(unit_ev, 1)

            def attention_a():
                def exp(n, c):
                    m = P
                    act.wait_ge(a_m, 2 * n + c + 1)
                    if n >= 2 and c == 0:
                        act.wait_ge(a_t, n - 1)
                    act.activation(two(pA[0:m, n % 2, c, :]), halves(3 + 2 * c, m), ACT.Exp,
                                   bias=st[0:m, 2 * (n % 2) + c:2 * (n % 2) + c + 1],
                                   accum_out=st[0:m, 4 + 2 * (n % 2) + c:5 + 2 * (n % 2) + c]).then_inc(a_exp, 1)

                def evac(n):
                    m = P
                    act.wait_ge(a_t, n + 1)
                    if n >= 2:
                        act.wait_ge(a_o, n - 1)
                    act.activation(ptA[:, n % 2, :, 0:m],
                                   ps[:, (7, 1)[n % 2], :].rearrange("p (j q) -> p j q", q=P)[:, :, 0:m],
                                   ACT.Copy).then_inc(a_tev, 1)

                for n in range(len(ASTEPS)):
                    exp(n, 0)
                    if n >= 1:
                        evac(n - 1)
                    exp(n, 1)
                evac(len(ASTEPS) - 1)

            def attention_b():
                def exp(n):
                    i, h = n // 8, BHEAD[n % 8]
                    m = TOK[i][1]
                    act.wait_ge(b_m, n + 1)
                    act.activation(sB[0:m, n % 4, 0:bwidth[i]], sB[0:m, n % 4, 0:bwidth[i]], ACT.Exp,
                                   bias=stB[0:m, i % 2, 0, h:h + 1],
                                   accum_out=stB[0:m, i % 2, 1, h:h + 1]).then_inc(b_exp, 1)

                def evac(n):
                    i = n // 8
                    m, nbk = TOK[i][1], len(BTILES[i])
                    act.wait_ge(b_t, n + 1)
                    if n >= 3:
                        act.wait_ge(b_o, n - 2)
                    act.activation(ptB[:, n % 3, 0:nbk, 0:m],
                                   ps[:, TB[n % 3], 0:P * nbk].rearrange("p (j q) -> p j q", q=P)[:, :, 0:m], ACT.Copy)
                    act.activation(ptmB[0:META, n % 3, 0:m], ps[0:META, TB[n % 3], 3 * P:3 * P + m],
                                   ACT.Copy).then_inc(b_tev, 1)

                exp(0)
                for n in range(8 * NT):
                    if n + 1 < 8 * NT:
                        exp(n + 1)
                    if n >= 1:
                        evac(n - 1)
                    if n % 8 == 7:
                        i = n // 8
                        m = TOK[i][1]
                        act.wait_ge(b_snk, 2 * i + 1)
                        act.activation(stB[0:m, i % 2, 3, :], stB[0:m, i % 2, 2, :], ACT.Exp).then_inc(b_snk, 1)
                evac(8 * NT - 1)

            def mlstm():
                for h in range(4):
                    act.wait_ge(m_in[h % 2], 32 * (h // 2 + 1))
                    for j, (t0, n) in enumerate(TOK):
                        for d in range(2):
                            lo, hi = (t0, L) if d == 0 else (0, t0 + n)
                            if h >= 2 and j == 0 and d == 0:
                                act.wait_ge(c_pv, NT * (h - 1))
                            col = 8 * d + 4 * d + h
                            act.activation(sC[h % 2][0:n, SAT[d][j]:SAT[d][j] + hi - lo], mb[0:n, h % 2, d, lo:hi], ACT.Exp,
                                           scale=-1.0, bias=gcol[0:n, j, col:col + 1]).then_inc(c_w, 1)
                    act.drain().then_inc(c_mbused, 1)

            norm_root(1)
            norm_evacuate(0, hT_hi)
            end_layer(act, "act")
            with act.Fori(0, DEPTH) as l:
                phase = Phase(act)
                steps[0] = 0
                act.wait_ge(first_in[0], l * 16 + 16)
                act.wait_ge(first_in[1], l * 16 + 16)
                split(0)
                split(1)
                act.wait_ge(h_saved, l * SAVED + SAVED)
                for u in range(NAB):
                    act.wait_ge(unit_mm, u + 1)
                    split(u + 2)
                    evacuate(u)
                act.wait_ge(n_ready, 1)
                act.activation(st[:, 10:12], st[:, 8:10], ACT.Exp).then_inc(n_sqrt, 1)
                phase()
                attention_a()
                phase()
                act.wait_ge(n_ready, 2)
                act.activation(ssr[:, :, :], ssr[:, :, :], ACT.Sqrt).then_inc(n_sqrt, 1)
                attention_b()
                phase()
                for q in range(2 * NT):
                    t0, n = TOK[q % NT]
                    act.wait_ge(n_t, q + 1)
                    src = ps[:, 4 + q % 4, :].rearrange("p (c t) -> p c t", t=P)[:, :, 0:n]
                    act.activation(outT[:, q // NT, :, t0:t0 + n], src, ACT.Copy,
                                   scale=(colp[:, 36:37] if q < NT else 1.0)).then_inc(n_ev, 1)
                phase()
                chunk = 0

                def silu(ch):
                    c = ch % 4
                    act.wait_ge(conv_done, ch + 1)
                    d_ = (qC if ch < 4 else kC)[:, c, :]
                    act.activation(d_, ctmp[:, ch % 2, :], ACT.Silu, bias=colp[:, 24 + ch:25 + ch]).then_inc(silu_done, 1)

                for u in range(NAB, NU):
                    kind, c = UNITS[u]
                    act.wait_ge(unit_mm, u + 1)
                    split(u + 2)
                    if kind in ("cq", "ck"):
                        ch = c + 4 * (kind == "ck")
                        if ch >= 2:
                            silu(ch - 2)
                    evacuate(u)
                    if kind == "cq" and c == 0:
                        act.wait_ge(g_exp, 1)
                        act.activation(cg[:, 1, :, :], cg[:, 1, :, :], ACT.Exp, scale=-1.0).then_inc(g_exp, 1)
                        act.wait_ge(g_exp, 2)
                        act.activation(cg[:, 1, :, :], cg[:, 1, :, :], ACT.Ln, bias=1.0).then_inc(g_ln, 1)
                    if kind == "cv" and c == 0:
                        silu(6)
                        silu(7)
                        act.wait_ge(g_rows, 1)
                        act.activation(EF, EF, ACT.Exp, scale=-1.0)
                        act.activation(EB, EB, ACT.Exp, scale=-1.0).then_inc(g_e, 1)
                phase()
                mlstm()
                phase()
                act.wait_ge(n_ready, 3)
                act.activation(ssr[:, :, :], ssr[:, :, :], ACT.Sqrt).then_inc(n_sqrt, 1)
                phase()
                with act.Fori(0, 3) as t:
                    for u in range(8):
                        act.wait_ge(unit_mm, t * 8 + (NU + u + 1))
                        if u == 2:
                            act.wait_ge(slot_in[0], t * 16 + (IN_GZ[1] + 16))
                        if u == 6:
                            act.wait_ge(slot_in[1], t * 16 + (IN_GZ[0] + 32))
                        act.activation(chunk_split(w_hi, NU + u + 2), chunk_source(NU + u + 2), ACT.Copy).then_inc(w_split_hi, 1)
                        act.activation(two(sg[:, u % 2, :]), halves(4 * (u % 2)), ACT.Sigmoid).then_inc(gate_sig, 1)
                phase()
                for k in range(KD):
                    act.activation(hT_hi[:, k, :], merged[:, k, :], ACT.Copy).then_inc(m_split_hi, 1)
                for m in range(KD):
                    act.wait_ge(unit_mm, NU + NG + m + 1)
                    if m == 2:
                        act.wait_ge(slot_in[0], IN_GZ[1] + 64)
                    if m < KD - 2:
                        q = NU + NG + m + 2
                        act.activation(chunk_split(w_hi, q), chunk_source(q), ACT.Copy).then_inc(w_split_hi, 1)
                    if m >= 2:
                        act.wait_ge(y_t, m - 1)
                    act.activation(two(yraw[:, m % 2, :]), halves(2 * (m % 2)), ACT.Copy).then_inc(y_ev, 1)
                norm_root(1)
                norm_evacuate(0, hT)
                act.wait_ge(r_a, 1)
                act.activation(r4[:, 0, :, :], r4[:, 0, :, :], ACT.Exp).then_inc(r_exp, 1)
                act.wait_ge(r_b, 1)
                act.activation(r5[:, 4, :], r5[:, 3, :], ACT.Exp).then_inc(r_exp2, 1)
                phase()
                start_free(act, "act")
                nb = act.value_load(tab[0:1, MAXB:MAXB + 1], min_val=9, max_val=MAXB)

                def rows_evacuate(done):
                    act.wait_ge(e_xt, done)
                    act.activation(xeT[:, :, :].rearrange("p (b k) n -> p b (k n)", b=2), ps[:, 2:4, :], ACT.Copy).then_inc(e_xtev, 1)

                def result(done):
                    act.wait_ge(ys_out, done * 16)
                    act.wait_ge(e_dn, done + 1)
                    act.activation(ye[:, 512:1024], ps[:, 6, :], ACT.Copy).then_inc(e_ye, 1)

                rows_evacuate(1)
                act.wait_ge(e_g, 2)
                act.activation(sil, ps[:, 0, :], ACT.Silu).then_inc(e_sil, 1)
                act.wait_ge(e_u, 2)
                rows_evacuate(2)
                with act.Fori(1, nb) as j:
                    act.wait_ge(e_g, j + 2)
                    act.wait_ge(e_hid, j + 1)
                    act.activation(sil, ps[:, 0, :], ACT.Silu).then_inc(e_sil, 1)
                    act.wait_ge(e_u, j + 2)
                    rows_evacuate(j + 2)
                    result(j)
                result(nb)
                phase()
                norm_root(2)
                norm_evacuate(NT, hT_hi)
                end_layer(act, "act")

        @block.vector
        def _(dve):
            steps = [0]

            def link(ins):
                steps[0] += 1
                ins.then_inc(dve_step, 1)
                dve.wait_ge(dve_step, steps[0])

            def norm_stats(i, n):
                dve.bn_stats(bn[0:n, i, 0:6], h_tok[0:n, i, 0:512])
                link(dve.bn_stats(bn[0:n, i, 6:12], h_tok[0:n, i, 512:1024]))
                link(dve.bn_aggr(mv[0:n, i, :], bn[0:n, i, 0:12]))

            def norm_apply(n_sq, split):
                dve.tensor_scalar(rstd[:, :], mv[:, :, 1], EPS, None, ALU.add).then_inc(l_var, 1)
                dve.wait_ge(l_sqrt, n_sq)
                link(dve.reciprocal(rstd[:, :], rstd[:, :]))
                dve.scalar_tensor_tensor(nbias, mv[:, :, 0], -1.0, rstd[:, :], ALU.mult, ALU.mult).then_inc(l_scale, 1)

                def low(i):
                    t0, n = TOK[i]
                    dve.wait_ge(l_ev, NT * (n_sq - 1) + i + 1)
                    for x in range(2):
                        ins = dve.tensor_tensor(hT_lo[:, 4 * x:4 * x + 4, t0:t0 + n],
                                                ps[:, 4 + 2 * (i % 2) + x, :].rearrange("p (k n) -> p k n", n=P)[:, :, 0:n],
                                                as_f32(hT_hi)[:, 4 * x:4 * x + 4, t0:t0 + n], ALU.subtract)
                    ins.then_inc(l_lo, 1)

                for i, (_, n) in enumerate(TOK):
                    q = NT * (n_sq - 1) + i + 1
                    dve.wait_ge(l_x, q)
                    dve.tensor_tensor(h_tok[0:n, i, :], h_tok[0:n, i, :], lngb[0:n, 0, :], ALU.mult).then_inc(l_mul, 1)
                    dve.wait_ge(l_mul, q)
                    o = h_tok[0:n, i, BC[0 if split else 1]:DM]
                    dve.tensor_tensor(o, o, lngb[0:n, 1, BC[0 if split else 1]:DM], ALU.add).then_inc(l_addv, 1)
                    if split and i >= 2:
                        low(i - 2)
                if split:
                    low(NT - 2)
                    low(NT - 1)

            def split_low(q, done):
                dve.wait_ge(w_split_hi, done)
                dve.tensor_tensor(chunk_split(w_lo, q), chunk_source(q), chunk_split(as_f32(w_hi), q),
                                  ALU.subtract).then_inc(w_split_lo, 1)

            def post(u):
                kind, c = UNITS[u]
                r = POST[u]
                bank = 4 + 2 * (r % 2)
                dve.wait_ge(rot_mm, r + 1)
                if kind in ROPE:
                    dve.tensor_tensor(two(t_sin[:, r % 2, :]), halves(bank), two(C("sin")), ALU.mult)
                    link(dve.tensor_tensor(raw[:, r % 2, :], raw[:, r % 2, :], C("cos"), ALU.mult))
                    if kind in ("aq", "bq"):
                        dve.tensor_tensor(ROPE[kind][:, c, :], raw[:, r % 2, :], t_sin[:, r % 2, :], ALU.add).then_inc(rot_ev, 1)
                        return
                    for g in range(2):
                        half = slice(64 * g, 64 * g + 64)
                        ins = dve.tensor_tensor(ROPE[kind][g][half, c, :], raw[half, r % 2, :], t_sin[half, r % 2, :], ALU.add)
                    ins.then_inc(rot_ev, 1)
                    return
                cols = slice(0, META if kind == "cg" else P)
                to = {"av": lambda: vA[:, :, P * c:P * c + P], "bv": lambda: vB, "cv": lambda: vC[:, :, c, 0:P],
                      "cg": lambda: cg[:, 0, :, :]}[kind]()
                dve.tensor_copy(to[:, 1:NT, :], ps[:, bank, :].rearrange("p (j d) -> p j d", d=P)[:, :, cols])
                dve.tensor_copy(to[0:META, 0, :], ps[0:META, bank + 1, cols]).then_inc(rot_ev, 1)

            def attention_a():
                nlam = st[:, 12:13]

                def rowmax(n, c):
                    m = P
                    dve.wait_ge(a_s, 2 * n + c + 1)
                    dve.tensor_reduce(st[0:m, 2 * (n % 2) + c:2 * (n % 2) + c + 1], halves(3 + 2 * c, m), AX.XY, ALU.max,
                                      negate=True).then_inc(a_m, 1)

                def combine(n):
                    i, h = ASTEPS[n]
                    m = TOK[i][1]
                    s = 4 + 2 * (n % 2)
                    dve.wait_ge(a_exp, 2 * n + 2)
                    if h is None:
                        link(dve.reciprocal(st[:, 13:15], st[:, s:s + 2]))
                        link(dve.tensor_scalar(pA[:, 0, 1, :], pA[:, 0, 1, :], st[:, 14:15], nlam, ALU.mult, ALU.mult))
                        dve.scalar_tensor_tensor(pA[:, 0, 0, :], pA[:, 0, 0, :], st[:, 13:14], pA[:, 0, 1, :],
                                                 ALU.mult, ALU.add).then_inc(a_comb, 1)
                        return
                    dve.reciprocal(rs[0:m, 0, i, h:h + 1], st[0:m, s:s + 1])
                    link(dve.reciprocal(st[0:m, 14:15], st[0:m, s + 1:s + 2]))
                    link(dve.scalar_tensor_tensor(st[0:m, 13:14], st[0:m, s:s + 1], nlam[0:m, :], st[0:m, 14:15], ALU.mult, ALU.mult))
                    dve.scalar_tensor_tensor(pA[0:m, n % 2, 0, :], pA[0:m, n % 2, 1, :], st[0:m, 13:14], pA[0:m, n % 2, 0, :],
                                             ALU.mult, ALU.add).then_inc(a_comb, 1)

                def meta_evac(n):
                    m = P
                    dve.wait_ge(a_t, n + 1)
                    if n >= 2:
                        dve.wait_ge(a_o, n - 1)
                    dve.tensor_copy(ptm[0:META, n % 2, 0:m], ps[0:META, 0, P * (n % 2):P * (n % 2) + m]).then_inc(a_tmev, 1)

                def out(i):
                    m = TOK[i][1]
                    dve.wait_ge(a_o, 4 * i + 1)
                    dve.tensor_tensor(oA[0:m, i, :].rearrange("p (h d) -> p h d", d=P),
                                      ps[0:m, 2, :].rearrange("p (h d) -> p h d", d=P),
                                      rs[0:m, 0, i, 0:4].unsqueeze(2).broadcast_to([m, 4, P]), ALU.mult).then_inc(a_oev, 1)

                rowmax(0, 0)
                rowmax(0, 1)
                N = len(ASTEPS)
                for n in range(N):
                    if n + 1 < N:
                        rowmax(n + 1, 0)
                    combine(n)
                    if n + 1 < N:
                        rowmax(n + 1, 1)
                    if n % 4 == 1:
                        out((n - 1) // 4)
                    meta_evac(n)
                out(NT - 1)

            def attention_b():
                def rowmax(n):
                    i, h = n // 8, BHEAD[n % 8]
                    m, w = TOK[i][1], bwidth[i]
                    dve.wait_ge(b_s, n + 1)
                    if n >= 2:
                        dve.wait_ge(b_m, n - 1)
                    if n >= 4:
                        dve.wait_ge(b_t, n - 3)
                    link(dve.tensor_tensor_reduce(sB[0:m, n % 4, 0:w], ps[0:m, 3 + n % 4, 0:w], C(BMASK[i], m, w), 1.0, LOW,
                                                  ALU.add, ALU.max, st[0:m, 60 + n % 2:61 + n % 2]))
                    dve.tensor_scalar(stB[0:m, i % 2, 0, h:h + 1], st[0:m, 60 + n % 2:61 + n % 2], R("sink")[0:m, h:h + 1], -1.0,
                                      ALU.max, ALU.mult).then_inc(b_m, 1)

                def sink(i):
                    m = TOK[i][1]
                    s5 = stB[0:m, i % 2, :, :]
                    dve.wait_ge(b_m, 8 * (i + 1))
                    dve.tensor_tensor(s5[:, 2, :], R("sink")[0:m, :], s5[:, 0, :], ALU.add).then_inc(b_snk, 1)
                    dve.wait_ge(b_exp, 8 * (i + 1))
                    dve.wait_ge(b_snk, 2 * (i + 1))
                    link(dve.tensor_tensor(s5[:, 4, :], s5[:, 1, :], s5[:, 3, :], ALU.add))
                    link(dve.reciprocal(rs[0:m, 1, i, :], s5[:, 4, :]))

                def out(i):
                    m = TOK[i][1]
                    dve.wait_ge(b_o, 8 * (i + 1))
                    dve.tensor_tensor(oB[0:m, i, :].rearrange("p (h d) -> p h d", d=64),
                                      ps[0:m, 2, :].rearrange("p (h d) -> p h d", d=64),
                                      rs[0:m, 1, i, :].unsqueeze(2).broadcast_to([m, 8, 64]), ALU.mult).then_inc(b_oev, 1)

                N = 8 * NT
                rowmax(0)
                rowmax(1)
                for n in range(N):
                    if n + 2 < N:
                        rowmax(n + 2)
                    if n >= 8 and n % 8 == 2:
                        out(n // 8 - 1)
                    if n % 8 == 7:
                        sink(n // 8)
                out(NT - 1)

            def lambdas():
                dve.wait_ge(par_in, 80)
                lam = R("lam").rearrange("p (a b) -> p a b", b=64)
                for x in range(2):
                    ins = dve.tensor_tensor_reduce(t_sin[:, 0, 64 * x:64 * x + 64], lam[:, 2 * x, :], lam[:, 2 * x + 1, :], 1.0, 0.0,
                                                   ALU.mult, ALU.add, st[:, 8 + x:9 + x])
                ins.then_inc(n_ready, 1)
                dve.wait_ge(n_ready, 1)

            def lambda_end():
                dve.wait_ge(n_sqrt, 1)
                link(dve.tensor_tensor(st[:, 13:14], st[:, 11:12], st[:, 10:11], ALU.subtract))
                link(dve.tensor_tensor(st[:, 12:13], st[:, 13:14], R("neg_lam_init"), ALU.add))
                link(dve.tensor_tensor(colp[:, 36:37], colp[:, 36:37], R("one_minus"), ALU.mult))

            def rms_stats():
                for i, (_, n) in enumerate(TOK):
                    o = oA[0:n, i, :]
                    link(dve.tensor_tensor(sq[0:n, i % 2, :], o, o, ALU.mult))
                    link(dve.tensor_reduce(ssr[0:n, i, :], sq[0:n, i % 2, :].rearrange("p (h d) -> p h d", d=P), AX.X, ALU.add))
                dve.tensor_scalar(ssr[:, :, :], ssr[:, :, :], 1.0 / P, EPS, ALU.mult, ALU.add).then_inc(n_ready, 1)

            def rms_apply():
                dve.wait_ge(n_sqrt, 2)
                link(dve.reciprocal(ssr[:, :, :], ssr[:, :, :]))
                for i, (_, n) in enumerate(TOK):
                    o = oA[0:n, i, :].rearrange("p (h d) -> p h d", d=P)
                    dve.tensor_tensor(o, o, ssr[0:n, i, :].unsqueeze(2).broadcast_to([n, 4, P]), ALU.mult).then_inc(n_norm, 1)

            def gate_logs():
                dve.wait_ge(rot_ev, POST[NAB] + 1)
                link(dve.tensor_tensor(cg[:, 0, :, :], cg[:, 0, :, :], R("gate_b").unsqueeze(1).broadcast_to([P, NT, 16]), ALU.add))
                dve.scalar_tensor_tensor(cg[:, 1, :, :], cg[:, 0, :, :], -1.0, cg[:, 0, :, :], ALU.mult, ALU.max).then_inc(g_exp, 1)

            def gate_logs2():
                dve.wait_ge(g_ln, 1)
                z = cg[:, 0, :, :].rearrange("p t (d k h) -> p t d k h", d=2, k=2)
                for d in range(2):
                    zl = z[:, :, d, 1, :]
                    ll = cg[:, 1, :, 8 * d + 4:8 * d + 8]
                    link(dve.scalar_tensor_tensor(zl, zl, 0.0, ll, ALU.min, ALU.subtract))
                for d in range(2):
                    dve.tensor_copy(cg[:, 1, :, 4 * d:4 * d + 4], z[:, :, d, 1, :])
                    ins = dve.tensor_copy(cg[:, 1, :, 8 + 4 * d:12 + 4 * d], z[:, :, d, 0, :])
                ins.then_inc(g_lf, 1)

            def gate_scans():
                dve.wait_ge(g_t, 1)
                dve.memset(ZR, 0.0)
                for bank, row in ((4, LF), (6, LI)):
                    dve.tensor_copy(row[:, 0:400], ps[0:8, bank, 0:400])
                    link(dve.tensor_copy(row[:, 400:L], ps[0:8, bank + 1, 0:P]))
                dve.tensor_tensor_scan(BF, ZR, LF, 0.0, ALU.add, ALU.add)
                link(dve.tensor_tensor_scan(BB[:, ::-1], ZR, LF[:, ::-1], 0.0, ALU.add, ALU.add))
                dve.tensor_tensor(UF, LI, BF, ALU.subtract)
                link(dve.tensor_tensor(UB, LI, BB, ALU.subtract))
                dve.tensor_tensor_scan(MF, ZR, UF, 0.0, ALU.add, ALU.max)
                link(dve.tensor_tensor_scan(MB[:, ::-1], ZR, UB[:, ::-1], 0.0, ALU.add, ALU.max))
                dve.tensor_tensor(EF, MF, BF, ALU.add)
                dve.tensor_tensor(EB, MB, BB, ALU.add).then_inc(g_rows, 1)

            def gate_cols():
                dve.wait_ge(g_t2, 1)
                dve.tensor_copy(gcol[0:META, 0, :], ps[0:META, 4, 0:32])
                dve.tensor_copy(gcol[:, 1:NT, :], ps[:, 4, 32:32 * NT].rearrange("p (t x) -> p t x", x=32)).then_inc(g_col, 1)

            def conv(ch):
                dve.wait_ge(unit_ev, NAB + 1 + ch + 1)
                if ch >= 2:
                    dve.wait_ge(silu_done, ch - 1)
                src, o = craw[:, ch % 2, :], ctmp[:, ch % 2, :]
                tap = [colp[:, 3 * ch + k:3 * ch + k + 1] for k in range(3)]
                link(dve.tensor_scalar(o, src[:, 0:L], tap[0], None, ALU.mult))
                link(dve.scalar_tensor_tensor(o, src[:, 1:L + 1], tap[1], o, ALU.mult, ALU.add))
                dve.scalar_tensor_tensor(o, src[:, 2:L + 2], tap[2], o, ALU.mult, ALU.add).then_inc(conv_done, 1)

            def mlstm():
                def weigh(h, j, x):
                    if h > 3:
                        return
                    q, d = NT * h + j, x // 2
                    t0, n = TOK[j]
                    b = QKB[q % 2] + x % 2
                    lo, hi = (t0, L) if d == 0 else (0, t0 + n)
                    x0, x1, base = (lo, min(hi, 272), 0) if x % 2 == 0 else (max(lo, 272), hi, 272)
                    last = x % 2 == 1 or hi <= 272
                    if x1 <= x0:
                        return
                    dve.wait_ge(c_qk, q + 1)
                    dve.wait_ge(c_w, 2 * q + d + 1)
                    w = sC[h % 2][0:n, SAT[d][j] + x0 - lo:SAT[d][j] + x1 - lo]
                    ins = dve.scalar_tensor_tensor(w, ps[0:n, b, x0 - base:x1 - base], MSCALE, w, ALU.mult, ALU.mult)
                    if last:
                        ins.then_inc(c_mul, 1)

                def after():
                    dve.wait_ge(dve_step, steps[0])

                def count(ins):
                    steps[0] += 1
                    ins.then_inc(dve_step, 1)

                def stats(h, i):
                    m = TOK[i][1]
                    dve.wait_ge(c_post, NT * h + i + 1)
                    count(dve.bn_stats(bn[0:m, i, 6 * h:6 * h + 6], hsum[0:m, i, P * h:P * h + P]))

                def step(h, j):
                    if h == 0:
                        for x in range(4):
                            weigh(h, j, x)
                        return
                    g, q = h - 1, NT * (h - 1) + j
                    m = TOK[j][1]
                    dve.wait_ge(c_pv, q + 1)
                    bank = ps[0:m, 5 + q % 2, :]
                    den = bank.rearrange("p (d x) -> p d x", x=256)[:, :, 128]
                    em = gcol[0:m, j, 16:32].rearrange("p (d x) -> p d x", x=8)
                    for d in range(2):
                        ins = dve.tensor_scalar(st[0:m, 56 + d:57 + d], den[:, d:d + 1], -1.0, em[:, d, 4 * d + g:4 * d + g + 1],
                                                ALU.mult, ALU.max)
                    count(ins)
                    weigh(h, j, 0)
                    after()
                    count(dve.tensor_tensor(st[0:m, 56:58], st[0:m, 56:58], den, ALU.max))
                    weigh(h, j, 1)
                    after()
                    count(dve.reciprocal(st[0:m, 58:60], st[0:m, 56:58]))
                    weigh(h, j, 2)
                    after()
                    o = hsum[0:m, j, P * g:P * g + P]
                    count(dve.tensor_scalar(o, bank[:, 0:P], st[0:m, 58:59], None, ALU.mult))
                    weigh(h, j, 3)
                    after()
                    dve.scalar_tensor_tensor(o, bank[:, 256:256 + P], st[0:m, 59:60], o, ALU.mult, ALU.add).then_inc(c_post, 1)
                    if q >= 1:
                        stats((q - 1) // NT, (q - 1) % NT)

                for h in range(5):
                    for j in range(NT):
                        step(h, j)
                stats(3, NT - 1)
                after()
                for i, (_, n) in enumerate(TOK):
                    for h in range(4):
                        ins = dve.bn_aggr(ss[0:n, i, h, :], bn[0:n, i, 6 * h:6 * h + 6])
                link(ins)

            def c_norm():
                link(dve.tensor_scalar(ssr[:, :, :], ss[:, :, :, 1], EPS, None, ALU.add))
                dve.drain().then_inc(n_ready, 1)
                dve.wait_ge(n_sqrt, 3)
                link(dve.reciprocal(ssr[:, :, :], ssr[:, :, :]))
                for i, (_, n) in enumerate(TOK):
                    for h in range(4):
                        o = hsum[0:n, i, P * h:P * h + P]
                        ins = dve.tensor_scalar(o, o, ss[0:n, i, h, 0:1], ssr[0:n, i, h:h + 1], ALU.subtract, ALU.mult)
                    ins.then_inc(n_norm, 1)

            def c_out():
                for i, (t0, n) in enumerate(TOK):
                    q = 2 * NT + i
                    dve.wait_ge(n_t, q + 1)
                    for c in range(4):
                        ins = dve.scalar_tensor_tensor(outT[:, 2, c, t0:t0 + n], ps[:, 4 + q % 4, P * c:P * c + n],
                                                       colp[:, 32 + c:33 + c], sco[:, c, t0:t0 + n], ALU.mult, ALU.mult)
                    ins.then_inc(n_ev, 1)

            def router():
                dve.wait_ge(r_mm, NT)
                for i, (_, n) in enumerate(TOK):
                    ins = dve.tensor_tensor(lg[0:n, i, :], ps[0:n, 0, 36 * i:36 * i + 36], R("b_r")[0:n, :], ALU.add)
                link(ins)
                g4, x32 = lg[:, :, 0:4], lg[:, :, 4:36]
                b5 = lambda k, w: r5[:, k, :].unsqueeze(2).broadcast_to([P, NT, w])
                link(dve.tensor_reduce(r5[:, 0, :], g4, AX.X, ALU.max))
                dve.tensor_tensor(r4[:, 0, :, :], g4, b5(0, 4), ALU.subtract).then_inc(r_a, 1)
                link(dve.tensor_tensor(r4[:, 1, :, :], g4, b5(0, 4), ALU.is_equal))
                link(dve.tensor_tensor(r4[:, 1, :, :], r4[:, 1, :, :], C("wg4").unsqueeze(1).broadcast_to([P, NT, 4]), ALU.mult))
                link(dve.tensor_reduce(r5[:, 1, :], r4[:, 1, :, :], AX.X, ALU.max))
                link(dve.tensor_tensor(r4[:, 2, :, :], r4[:, 1, :, :], b5(1, 4), ALU.is_equal))
                link(dve.tensor_scalar(r4[:, 2, :, :], r4[:, 2, :, :], -1.0, -NEG, ALU.add, ALU.mult))
                dve.wait_ge(xs_zeroed, 32)
                em = e32[:, 3, :, :]
                link(dve.tensor_tensor(em.rearrange("p t (g e) -> p t g e", e=8), x32.rearrange("p t (g e) -> p t g e", e=8),
                                       r4[:, 2, :, :].unsqueeze(3).broadcast_to([P, NT, 4, 8]), ALU.add))
                we = C("we32").unsqueeze(1).broadcast_to([P, NT, NE])
                for k in range(2):
                    oh = e32[:, k, :, :]
                    link(dve.tensor_reduce(r5[:, 5 + k, :], em, AX.X, ALU.max))
                    link(dve.tensor_tensor(oh, em, b5(5 + k, NE), ALU.is_equal))
                    link(dve.tensor_tensor(oh, oh, we, ALU.mult))
                    link(dve.tensor_reduce(r5[:, 1, :], oh, AX.X, ALU.max))
                    link(dve.tensor_tensor(oh, oh, b5(1, NE), ALU.is_equal))
                    if k == 0:
                        link(dve.scalar_tensor_tensor(em, oh, 2 * NEG, em, ALU.mult, ALU.add))
                dve.tensor_tensor(r5[:, 3, :], r5[:, 6, :], r5[:, 5, :], ALU.subtract).then_inc(r_b, 1)
                link(dve.tensor_tensor(e32[:, 2, :, :], e32[:, 0, :, :], e32[:, 1, :, :], ALU.add))
                before = lambda i: e32[:, 3, i, :] if i < NT else n32[:, 3, :]
                dve.memset(before(0), 0.0)
                link(dve.tensor_tensor(e32[:, 2, :, :], e32[:, 2, :, :], C("valid").unsqueeze(2).broadcast_to([P, NT, NE]),
                                       ALU.mult))
                for i in range(NT):
                    ins = dve.tensor_tensor(before(i + 1), before(i), e32[:, 2, i, :], ALU.add)
                    if i < NT - 1:
                        link(ins)
                ins.then_inc(r_cnt, 1)
                dve.wait_ge(r_exp, 1)
                link(dve.tensor_reduce(r5[:, 2, :], r4[:, 0, :, :], AX.X, ALU.add))
                dve.wait_ge(r_exp2, 1)
                link(dve.scalar_tensor_tensor(r5[:, 9, :], r5[:, 4, :], 1.0, r5[:, 2, :], ALU.add, ALU.mult))
                link(dve.reciprocal(r5[:, 7, :], r5[:, 9, :]))
                link(dve.tensor_tensor(r5[:, 8, :], r5[:, 7, :], r5[:, 4, :], ALU.mult))
                dve.wait_ge(r_rank, 1)
                link(dve.tensor_copy(n32[:, 0, :], ps[:, 1, NE * NT:NE * NT + NE]))
                cmp = e32[:, 2, :, :].rearrange("p t e -> p (t e)").rearrange("p (e t) -> p e t", t=NT)
                link(dve.tensor_tensor(cmp, n32[:, 0, :].unsqueeze(2).broadcast_to([P, NE, NT]),
                                       C("thr").unsqueeze(1).broadcast_to([P, NE, NT]), ALU.is_gt))
                link(dve.tensor_reduce(n32[:, 1, :], cmp, AX.X, ALU.add))
                link(dve.tensor_tensor_scan(n32[:, 2, :], C("zero"), n32[:, 1, :], 0.0, ALU.add, ALU.add))
                link(dve.tensor_tensor(n32[:, 3, :], n32[:, 2, :], n32[:, 1, :], ALU.subtract))
                link(dve.tensor_scalar(n32[:, 3, :], n32[:, 3, :], float(P), None, ALU.mult))
                link(dve.tensor_tensor(e32[:, 3, :, :], ps[:, 1, 0:NE * NT].rearrange("p (t e) -> p t e", e=NE),
                                       n32[:, 3, :].unsqueeze(1).broadcast_to([P, NT, NE]), ALU.add))
                for k in range(2):
                    link(dve.tensor_tensor(e32[:, k, :, :], e32[:, k, :, :], e32[:, 3, :, :], ALU.mult))
                    link(dve.tensor_reduce(r5[:, 10 + k, :], e32[:, k, :, :], AX.X, ALU.add))
                    ins = dve.tensor_copy(dst[:, :, k], r5[:, 10 + k, :])
                ins.then_inc(r_dst, 1)
                big = arena[0:1, mo:mo + MAXB * NE].rearrange("p (j e) -> p j e", e=NE)
                link(dve.tensor_tensor(big, n32[0:1, 2, :].unsqueeze(1).broadcast_to([1, MAXB, NE]),
                                       C("jj", 1).unsqueeze(2).broadcast_to([1, MAXB, NE]), ALU.is_le))
                link(dve.tensor_reduce(tabf[0:1, 0:MAXB], big, AX.X, ALU.add))
                link(dve.tensor_scalar(tabf[0:1, 0:MAXB], tabf[0:1, 0:MAXB], float(NE - 1), None, ALU.min))
                dve.memset(tabf[0:1, 2 * MAXB + 1:2 * MAXB + 2], 1.0)
                dve.tensor_copy(tabf[0:1, MAXB:MAXB + 1], n32[0:1, 2, NE - 1:NE])
                link(dve.tensor_scalar(n32[0:1, 0, :], n32[0:1, 1, :], 1.0, None, ALU.min))
                link(dve.tensor_tensor(big, big, n32[0:1, 0, :].unsqueeze(1).broadcast_to([1, MAXB, NE]), ALU.mult))
                link(dve.tensor_reduce(tabf[0:1, MAXB + 1:2 * MAXB + 1], big, AX.X, ALU.add))
                link(dve.tensor_tensor(tabf[0:1, 2 * MAXB + 2:3 * MAXB + 1], tabf[0:1, MAXB + 2:2 * MAXB + 1],
                                       tabf[0:1, MAXB + 1:2 * MAXB], ALU.subtract))
                dve.tensor_copy(tab[0:1, 0:3 * MAXB + 1], tabf[0:1, 0:3 * MAXB + 1]).then_inc(r_tab, 1)

            for t in (mv, ssr, ss, cg, lg, rs, gcol):
                dve.memset(t[:], 1.0)
            for i, (_, n) in enumerate(TOK):
                dve.wait_ge(x_in[i], 16)
                norm_stats(i, n)
            dve.wait_ge(ln0_in, 32)
            norm_apply(1, True)
            dve.wait_ge(const_in, 16)
            dve.tensor_copy(rot_r[:, :], C("rot"))
            end_layer(dve, "dve")
            with dve.Fori(0, DEPTH) as l:
                phase = Phase(dve)
                steps[0] = 0
                dve.memset(zeros, 0.0).then_inc(zero_ready, 1)
                split_low(0, 1)
                split_low(1, 2)
                dve.wait_ge(h_saved, l * SAVED + SAVED)
                lambdas()
                for u in range(NAB):
                    split_low(u + 2, u + 3)
                    if u in NROPE:
                        dve.wait_ge(unit_ev, u + 1)
                        r = POST[u] % 2
                        dve.tensor_tensor(raw_lo[:, r, :], raw[:, r, :], as_f32(raw_hi)[:, r, :], ALU.subtract).then_inc(rot_lo, 1)
                    post(u)
                lambda_end()
                phase()
                attention_a()
                phase()
                rms_stats()
                rms_apply()
                attention_b()
                phase()
                dve.memset(craw[:, :, 0:1], 0.0)
                dve.memset(craw[:, :, L + 1:L + 2], 0.0)
                dve.memset(vC[:, :, :, 128:129], 1.0)
                phase()
                for u in range(NAB, NU):
                    kind, c = UNITS[u]
                    split_low(u + 2, u + 3)
                    if u in POST:
                        post(u)
                    if kind == "cg":
                        gate_logs()
                    if kind in ("cq", "ck"):
                        conv(c + 4 * (kind == "ck"))
                    if kind == "cq" and c == 0:
                        gate_logs2()
                    if kind == "cq" and c == 3:
                        gate_scans()
                    if kind == "co" and c == 2:
                        gate_cols()
                phase()
                mlstm()
                phase()
                c_norm()
                c_out()
                dve.memset(merged[:, :, :], 0.0).then_inc(gate_free, 2)
                phase()
                with dve.Fori(0, 3) as t:
                    for u in range(8):
                        split_low(NU + u + 2, t * 8 + (NU + u + 3))
                        dve.wait_ge(gate_sig, t * 8 + (u + 1))
                        dve.wait_ge(gate_mm, t * 8 + (u + 1))
                        dve.tensor_tensor(two(tg[:, u % 2, :]), two(sg[:, u % 2, :]), halves(4 * (u % 2) + 2), ALU.mult).then_inc(gate_tmp, 1)
                        dve.wait_ge(gate_tmp, t * 8 + (u + 1))
                        dve.tensor_tensor(merged[:, u, :], merged[:, u, :], tg[:, u % 2, :], ALU.add).then_inc(gate_free, 1)
                phase()
                for k in range(KD):
                    dve.wait_ge(m_split_hi, k + 1)
                    dve.tensor_tensor(hT_lo[:, k, :], merged[:, k, :], as_f32(hT_hi)[:, k, :], ALU.subtract).then_inc(m_split_lo, 1)
                dve.wait_ge(h_back, 32)
                for m in range(KD):
                    if m < KD - 2:
                        split_low(NU + NG + m + 2, NU + NG + m + 3)
                    dve.wait_ge(y_t, m + 1)
                    bank, cols = 4 + 2 * (m % 2), slice(P * m, P * m + P)
                    o = h_tok[:, 1:NT, cols]
                    dve.scalar_tensor_tensor(o, o, ALPHA, ps[:, bank, :].rearrange("p (j d) -> p j d", d=P), ALU.mult, ALU.add)
                    o = h_tok[0:META, 0, cols]
                    dve.scalar_tensor_tensor(o, o, ALPHA, ps[0:META, bank + 1, 0:P], ALU.mult, ALU.add).then_inc(y_add, 1)
                    dve.wait_ge(y_add, m + 1)
                    for i, (_, n) in enumerate(TOK):
                        ins = dve.bn_stats(bn[0:n, i, 6 * m:6 * m + 6], h_tok[0:n, i, cols])
                link(ins)
                for i, (_, n) in enumerate(TOK):
                    ins = dve.bn_aggr(mv[0:n, i, :], bn[0:n, i, :])
                link(ins)
                norm_apply(1, False)
                router()
                phase()
                start_free(dve, "dve")
                nb = dve.value_load(tab[0:1, MAXB:MAXB + 1], min_val=9, max_val=MAXB)
                dve.wait_ge(scattered, l * 160 + 160)
                dve.tensor_scalar(h_tok[:, 1:NT, :], h_tok[:, 1:NT, :], ALPHA, None, ALU.mult)
                dve.tensor_scalar(h_tok[0:META, 0, :], h_tok[0:META, 0, :], ALPHA, None, ALU.mult)

                def hidden(j):
                    dve.wait_ge(e_sil, j + 2)
                    dve.wait_ge(e_u, j + 2)
                    dve.tensor_tensor(hid, sil, ps[:, 1, :], ALU.mult).then_inc(e_hid, 1)

                def hidden_turned(j):
                    dve.wait_ge(e_ht, j)
                    dve.tensor_copy(hidT[:, :, :].rearrange("p k n -> p (k n)"), ps[:, 4, :]).then_inc(e_htev, 1)

                def result(done):
                    dve.wait_ge(ys_out, done * 16)
                    dve.wait_ge(e_dn, done + 1)
                    dve.tensor_copy(ye[:, 0:512], ps[:, 5, :]).then_inc(e_ye, 1)

                hidden(0)
                with dve.Fori(1, nb) as j:
                    hidden_turned(j)
                    hidden(j)
                    result(j)
                hidden_turned(nb)
                result(nb)
                phase()
                for i, (_, n) in enumerate(TOK):
                    dve.wait_ge(gathered[i], l * 32 + 32)
                    o = h_tok[0:n, i, :]
                    y1, y2 = gath[0:n, i, 0, :], gath[0:n, i, 1, :]
                    link(dve.scalar_tensor_tensor(o, y1, r5[0:n, 7, i:i + 1], o, ALU.mult, ALU.add))
                    link(dve.scalar_tensor_tensor(o, y2, r5[0:n, 8, i:i + 1], o, ALU.mult, ALU.add))
                    norm_stats(i, n)
                dve.wait_ge(ln2_in, 32)
                norm_apply(2, True)
                end_layer(dve, "dve")


def constants():
    c = np.zeros((P, NCONST), np.float32)

    def put(name, value):
        at, w = CONST[name]
        c[:, at:at + w] = value

    inv = (1.0 / (np.float32(10000.0) ** (np.arange(0, 64, 2, dtype=np.float32) / np.float32(64)))).astype(np.float32)
    ang = np.arange(L, dtype=np.float32)[None, :] * inv[np.arange(P) % 32][:, None]
    put("cos", np.cos(ang))
    put("sin", np.sin(ang))
    put("ident", np.eye(P))
    rot = np.zeros((P, P), np.float32)
    for m in range(P):
        if m % 64 < 32:
            rot[m + 32, m] = -1.0
        else:
            rot[m - 32, m] = 1.0
    put("rot", rot)
    q, k = np.arange(P)[:, None], np.arange(P)[None, :]
    prev, nxt = np.where(k >= q, 0.0, NEG), np.where(k <= q, 0.0, NEG)
    m0 = np.zeros((P, 144))
    m0[:, 16:] = np.where(k <= q + P - META, 0.0, NEG)
    put("mask0", m0)
    z16, z128 = np.zeros((P, 16)), np.zeros((P, P))
    put("mask1", np.concatenate([z16, z128, nxt], 1))
    put("mask2", np.concatenate([z16, prev, z128, nxt], 1))
    put("ltri", q < k)
    put("ones", 1.0)
    valid = np.ones((P, NT))
    valid[META:, 0] = 0.0
    put("valid", valid)
    put("wg4", 4.0 - np.arange(4))
    put("we32", float(NE) - np.arange(NE))
    put("thr", float(P) * np.arange(NT))
    put("jj", np.arange(MAXB))
    return c


def kernel(**inputs):
    import numpy as _np
    import concourse.bacc as _bacc
    from concourse import mybir as _mybir
    from concourse.bass_utils import run_bass_kernel_spmd as _run

    i = {k: _np.asarray(v) for k, v in inputs.items()}
    arrays = {n: _np.ascontiguousarray(i[n]) for n in
              ("x", "meta", "ln_in_g", "ln_in_b", "w_in", "w_branch", "w_out", "ln1_g", "ln1_b", "ln2_g", "ln2_b",
               "w_gate", "w_up", "w_down")}
    f = _np.float32
    lam_init = _np.array([0.8 - 0.6 * _np.exp(-0.3 * l) for l in range(DEPTH)], f)[:, None]
    arrays["consts"] = constants()
    arrays["rowp"] = _np.concatenate([i["gate_b"], i["b_rg"], i["b_re"], i["sink"], i["lam_q1"], i["lam_k1"],
                                      i["lam_q2"], i["lam_k2"], -lam_init, f(1) - lam_init], axis=1)
    cw = i["conv_w"].reshape(DEPTH, 3, 8, P).transpose(0, 3, 2, 1).reshape(DEPTH, P, 24)
    arrays["colp"] = _np.concatenate([cw, i["conv_b"].reshape(DEPTH, 8, P).transpose(0, 2, 1),
                                      i["mlstm_g"].reshape(DEPTH, 4, P).transpose(0, 2, 1),
                                      i["diff_g"][:, :, None]], axis=2)
    arrays["w_r"] = _np.concatenate([i["w_rg"], i["w_re"]], axis=2)
    arrays = {f"in_{n}": _np.ascontiguousarray(v) for n, v in arrays.items()}
    nc = _bacc.Bacc("TRN2", target_bir_lowering=False, num_devices=1)
    aps = {n[3:]: nc.dram_tensor(n, v.shape, _mybir.dt.from_np(v.dtype), kind="ExternalInput").ap() for n, v in arrays.items()}
    aps["out"] = nc.dram_tensor("out_h", (1, SEQ, DM), F32, kind="ExternalOutput").ap()
    program(nc, aps)
    r = _run(nc, [arrays], core_ids=[0])
    return r.results[0]["out_h"]
```
